# Optimizing a Trainium2 kernel written in Bass

```python
import math
import jax, jax.numpy as jnp
from jax import lax
import numpy as np

D_MODEL = 2048
BATCH = 1
SEQ = 512
DEPTH = 1
DEC_BATCH = 8
DEC_SEQ = 8
PAST_LEN = 1024
PAGE_SIZE = 128

MIX_WIDTH = D_MODEL
GLA_WIDTH = MIX_WIDTH // 2
SWA_WIDTH = MIX_WIDTH - GLA_WIDTH
GLA_HEADS = 4
GLA_DK = (GLA_WIDTH // 2) // GLA_HEADS
GLA_DV = GLA_WIDTH // GLA_HEADS
GLA_GATE_RANK = 16
GLA_TAU = 16.0
GLA_CHUNK = 64
SWA_HEAD_DIM = 64
SWA_HEADS = SWA_WIDTH // SWA_HEAD_DIM
SWA_KV_HEADS = 2
SWA_GROUP = SWA_HEADS // SWA_KV_HEADS
WINDOW = 128
SWA_BLOCK = WINDOW
ROPE_THETA = 10000.0
PEER_N_KEYS = 128
PEER_EXPERTS = PEER_N_KEYS * PEER_N_KEYS
PEER_HEADS = 8
PEER_QDIM = 128
PEER_HALF = PEER_QDIM // 2
PEER_TOPK = 16
PEER_TOKEN_BLOCK = 128
EPS = 1e-6
NEG_INF = -1e30
PROJ_SPLITS = (GLA_HEADS * GLA_DK,
               GLA_HEADS * GLA_DK,
               GLA_WIDTH,
               GLA_WIDTH,
               GLA_GATE_RANK,
               SWA_WIDTH,
               SWA_KV_HEADS * SWA_HEAD_DIM,
               SWA_KV_HEADS * SWA_HEAD_DIM)
PROJ_WIDTH = sum(PROJ_SPLITS)

kernel_name = 'hymba_gla_swasink_peer_step'

def rms_norm(x, g):
    xf = x.astype(jnp.float32)
    y = xf * lax.rsqrt(jnp.mean(xf * xf, axis=-1, keepdims=True) + EPS)
    return (y * g.astype(jnp.float32)).astype(x.dtype)

def split_cols(p):
    out = []
    start = 0
    for w in PROJ_SPLITS:
        out.append(p[..., start:start + w])
        start += w
    return out

def rope(x, pos):
    hd = x.shape[-1]
    half = hd // 2
    inv = jnp.exp(-math.log(ROPE_THETA) * jnp.arange(half, dtype=jnp.float32) * (2.0 / hd))
    ang = pos.astype(jnp.float32)[:, None] * inv[None, :]
    cos = jnp.cos(ang)[:, None, :]
    sin = jnp.sin(ang)[:, None, :]
    xf = x.astype(jnp.float32)
    x1, x2 = xf[..., :half], xf[..., half:]
    return jnp.concatenate([x1 * cos - x2 * sin, x2 * cos + x1 * sin], axis=-1).astype(x.dtype)

def sink_softmax(s, mask, sink):
    s = jnp.where(mask, s, NEG_INF)
    m = jnp.maximum(jnp.max(s, axis=-1, keepdims=True), sink)
    p = jnp.exp(s - m)
    return p / (jnp.sum(p, axis=-1, keepdims=True) + jnp.exp(sink - m))

def gla_chunked(q, k, v, log_a):
    B, S, H, dk = q.shape
    dv = v.shape[-1]
    C = GLA_CHUNK
    N = S // C

    def blk(t):
        return t.reshape(B, N, C, H, t.shape[-1]).transpose(0, 3, 1, 2, 4)

    q, k, v, log_a = blk(q), blk(k), blk(v), blk(log_a)
    b = jnp.cumsum(log_a, axis=3)
    b_last = b[:, :, :, -1:, :]
    q_t = q * jnp.exp(b)
    k_t = k * jnp.exp(-b)
    k_e = k * jnp.exp(b_last - b)
    causal = jnp.tril(jnp.ones((C, C), dtype=bool))
    a_intra = jnp.where(causal, jnp.einsum('bhncd,bhnsd->bhncs', q_t, k_t), 0.0)
    o_intra = jnp.einsum('bhncs,bhnsv->bhncv', a_intra, v)
    d_state = jnp.einsum('bhncd,bhncv->bhndv', k_e, v)
    decay = jnp.exp(b_last[:, :, :, 0, :])

    def step(s_c, inp):
        dec, ds = inp
        return dec[..., None] * s_c + ds, s_c

    s0 = jnp.zeros((B, H, dk, dv), jnp.float32)
    s_fin, s_in = lax.scan(step, s0, (jnp.moveaxis(decay, 2, 0), jnp.moveaxis(d_state, 2, 0)))
    s_in = jnp.moveaxis(s_in, 0, 2)
    o_inter = jnp.einsum('bhncd,bhndv->bhncv', q_t, s_in)
    o = (o_intra + o_inter).transpose(0, 2, 3, 1, 4).reshape(B, S, H, dv)
    return o, s_fin

def gla_recurrent(q, k, v, log_a, s0):
    def step(s, inp):
        qt, kt, vt, gt = inp
        s = jnp.exp(gt)[..., None] * s + kt[..., :, None] * vt[..., None, :]
        return s, jnp.einsum('bhd,bhdv->bhv', qt, s)

    xs = tuple(jnp.moveaxis(t, 1, 0) for t in (q, k, v, log_a))
    s_fin, o = lax.scan(step, s0.astype(jnp.float32), xs)
    return jnp.moveaxis(o, 0, 1), s_fin

def gla_output(o, r, g_norm):
    B, S = o.shape[:2]
    o = o * lax.rsqrt(jnp.mean(o * o, axis=-1, keepdims=True) + EPS) * g_norm.astype(jnp.float32)
    o = o.reshape(B, S, GLA_WIDTH) * jax.nn.silu(r.astype(jnp.float32))
    return o.astype(r.dtype)

def swa_prompt(q, k, v, sinks):
    B, S, _, hd = q.shape
    L = SWA_BLOCK
    NB = S // L
    qb = q.reshape(B, NB, L, SWA_KV_HEADS, SWA_GROUP, hd).astype(jnp.float32)
    kb = k.reshape(B, NB, L, SWA_KV_HEADS, hd).astype(jnp.float32)
    vb = v.reshape(B, NB, L, SWA_KV_HEADS, hd).astype(jnp.float32)
    pad = ((0, 0), (1, 0), (0, 0), (0, 0), (0, 0))
    kk = jnp.concatenate([jnp.pad(kb, pad)[:, :NB], kb], axis=2)
    vv = jnp.concatenate([jnp.pad(vb, pad)[:, :NB], vb], axis=2)
    diff = (jnp.arange(L)[:, None] + L) - jnp.arange(2 * L)[None, :]
    band = (diff >= 0) & (diff < WINDOW)
    has_prev = (jnp.arange(NB)[:, None] > 0) | (jnp.arange(2 * L)[None, :] >= L)
    mask = (band[None, :, :] & has_prev[:, None, :])[None, :, None, None]
    s = jnp.einsum('bnqkgd,bnskd->bnkgqs', qb, kk) * (hd ** -0.5)
    sink = sinks.astype(jnp.float32).reshape(SWA_KV_HEADS, SWA_GROUP)[:, :, None, None]
    p = sink_softmax(s, mask, sink)
    o = jnp.einsum('bnkgqs,bnskd->bnqkgd', p, vv)
    return o.reshape(B, S, SWA_WIDTH).astype(q.dtype)

def swa_sample(q, k, v, cache_k, cache_v, sinks):
    B, T, _, hd = q.shape
    W = cache_k.shape[1]
    kk = jnp.concatenate([cache_k.astype(k.dtype), k], axis=1)
    vv = jnp.concatenate([cache_v.astype(v.dtype), v], axis=1)
    qpos = PAST_LEN + jnp.arange(T)
    kpos = jnp.concatenate([PAST_LEN - W + jnp.arange(W), PAST_LEN + jnp.arange(T)])
    diff = qpos[:, None] - kpos[None, :]
    mask = (diff >= 0) & (diff < WINDOW)
    qf = q.reshape(B, T, SWA_KV_HEADS, SWA_GROUP, hd).astype(jnp.float32)
    s = jnp.einsum('btkgd,bskd->bkgts', qf, kk.astype(jnp.float32)) * (hd ** -0.5)
    sink = sinks.astype(jnp.float32).reshape(SWA_KV_HEADS, SWA_GROUP)[:, :, None, None]
    p = sink_softmax(s, mask, sink)
    o = jnp.einsum('bkgts,bskd->btkgd', p, vv.astype(jnp.float32))
    return o.reshape(B, T, SWA_WIDTH).astype(q.dtype), kk[:, -W:], vv[:, -W:]

def peer(xn, w_q, sub_keys, u, v):
    T, D = xn.shape
    TB = PEER_TOKEN_BLOCK
    pad = (-T) % TB
    xb = jnp.pad(xn, ((0, pad), (0, 0))).reshape(-1, TB, D)
    K = PEER_TOPK

    def block(xt):
        q = (xt @ w_q).reshape(TB, PEER_HEADS, 2, PEER_HALF)
        s = jnp.einsum('thpd,hpnd->thpn', q, sub_keys).astype(jnp.float32)
        sv, si = lax.top_k(s, K)
        cand = sv[:, :, 0, :, None] + sv[:, :, 1, None, :]
        cand_idx = si[:, :, 0, :, None] * PEER_N_KEYS + si[:, :, 1, None, :]
        best, pos = lax.top_k(cand.reshape(TB, PEER_HEADS, K * K), K)
        idx = jnp.take_along_axis(cand_idx.reshape(TB, PEER_HEADS, K * K), pos, axis=-1)
        gate = jax.nn.softmax(best, axis=-1).reshape(TB, PEER_HEADS * K)
        idx = idx.reshape(TB, PEER_HEADS * K)
        u_e = u[idx]
        v_e = v[idx]
        act = jax.nn.gelu(jnp.einsum('td,ted->te', xt, u_e).astype(jnp.float32), approximate=False)
        coef = (gate * act).astype(xt.dtype)
        return jnp.einsum('te,ted->td', coef, v_e)

    return lax.map(block, xb).reshape(-1, D)[:T]

def mix_inputs(x, pos, g_attn, w_in, w_gate_up, b_gate):
    B, S, _ = x.shape
    xn = rms_norm(x, g_attn)
    gq, gk, gv, gr, ga, sq, sk, sv = split_cols(xn @ w_in)
    q = gq.astype(jnp.float32).reshape(B, S, GLA_HEADS, GLA_DK) * (GLA_DK ** -0.5)
    k = gk.astype(jnp.float32).reshape(B, S, GLA_HEADS, GLA_DK)
    v = gv.astype(jnp.float32).reshape(B, S, GLA_HEADS, GLA_DV)
    log_a = jax.nn.log_sigmoid((ga @ w_gate_up + b_gate).astype(jnp.float32)).reshape(
        B, S, GLA_HEADS, GLA_DK) / GLA_TAU
    sq = rope(sq.reshape(B, S, SWA_HEADS, SWA_HEAD_DIM), pos)
    sk = rope(sk.reshape(B, S, SWA_KV_HEADS, SWA_HEAD_DIM), pos)
    sv = sv.reshape(B, S, SWA_KV_HEADS, SWA_HEAD_DIM)
    return q, k, v, log_a, gr, sq, sk, sv

def merge_and_ffn(x, o_gla, gr, o_swa, g_gla_out, w_out, g_ffn, w_peer_q, peer_sub_keys, peer_u, peer_v):
    B, S, D = x.shape
    heads = jnp.concatenate([gla_output(o_gla, gr, g_gla_out), o_swa], axis=-1)
    h = x + heads @ w_out
    hn = rms_norm(h, g_ffn).reshape(B * S, D)
    return h + peer(hn, w_peer_q, peer_sub_keys, peer_u, peer_v).reshape(B, S, D)

def layer_prompt(x, g_attn, w_in, w_gate_up, b_gate, g_gla_out, attn_sinks, w_out,
                 g_ffn, w_peer_q, peer_sub_keys, peer_u, peer_v):
    pos = jnp.arange(x.shape[1])
    q, k, v, log_a, gr, sq, sk, sv = mix_inputs(x, pos, g_attn, w_in, w_gate_up, b_gate)
    o_gla, s_fin = gla_chunked(q, k, v, log_a)
    o_swa = swa_prompt(sq, sk, sv, attn_sinks)
    out = merge_and_ffn(x, o_gla, gr, o_swa, g_gla_out, w_out, g_ffn, w_peer_q, peer_sub_keys, peer_u, peer_v)
    return out, s_fin.astype(x.dtype), sk[:, -WINDOW:], sv[:, -WINDOW:]

def layer_sample(x, s_gla, c_k, c_v, g_attn, w_in, w_gate_up, b_gate, g_gla_out, attn_sinks, w_out,
                 g_ffn, w_peer_q, peer_sub_keys, peer_u, peer_v):
    pos = PAST_LEN + jnp.arange(x.shape[1])
    q, k, v, log_a, gr, sq, sk, sv = mix_inputs(x, pos, g_attn, w_in, w_gate_up, b_gate)
    o_gla, s_fin = gla_recurrent(q, k, v, log_a, s_gla)
    o_swa, new_k, new_v = swa_sample(sq, sk, sv, c_k, c_v, attn_sinks)
    out = merge_and_ffn(x, o_gla, gr, o_swa, g_gla_out, w_out, g_ffn, w_peer_q, peer_sub_keys, peer_u, peer_v)
    return out, s_fin.astype(s_gla.dtype), new_k.astype(c_k.dtype), new_v.astype(c_v.dtype)

def setup_inputs(seed: int = 0) -> dict:
    key = jax.random.key(seed)
    ks = jax.random.split(key, 20)
    f = jnp.float32
    n = lambda i, shape, scale: jax.random.normal(ks[i], shape, f) * scale
    win_c = min(WINDOW, PAST_LEN)
    return {
        'x_prompt': n(0, (BATCH, SEQ, D_MODEL), 1.0),
        'x_sample': n(1, (DEC_BATCH, DEC_SEQ, D_MODEL), 1.0),
        'state_gla': n(2, (DEPTH, DEC_BATCH, GLA_HEADS, GLA_DK, GLA_DV), 0.5),
        'cache_win_k': n(3, (DEPTH, DEC_BATCH, win_c, SWA_KV_HEADS, SWA_HEAD_DIM), 1.0),
        'cache_win_v': n(4, (DEPTH, DEC_BATCH, win_c, SWA_KV_HEADS, SWA_HEAD_DIM), 1.0),
        'g_attn': 1.0 + n(5, (DEPTH, D_MODEL), 0.02),
        'w_in': n(6, (DEPTH, D_MODEL, PROJ_WIDTH), D_MODEL ** -0.5),
        'w_gate_up': n(7, (DEPTH, GLA_GATE_RANK, GLA_HEADS * GLA_DK), GLA_GATE_RANK ** -0.5),
        'b_gate': n(8, (DEPTH, GLA_HEADS * GLA_DK), 0.1),
        'g_gla_out': 1.0 + n(9, (DEPTH, GLA_DV), 0.02),
        'attn_sinks': n(10, (DEPTH, SWA_HEADS), 0.5),
        'w_out': n(11, (DEPTH, MIX_WIDTH, D_MODEL), MIX_WIDTH ** -0.5),
        'g_ffn': 1.0 + n(12, (DEPTH, D_MODEL), 0.02),
        'w_peer_q': n(13, (DEPTH, D_MODEL, PEER_HEADS * PEER_QDIM), D_MODEL ** -0.5),
        'peer_sub_keys': n(14, (DEPTH, PEER_HEADS, 2, PEER_N_KEYS, PEER_HALF), PEER_HALF ** -0.5),
        'peer_u': n(15, (DEPTH, PEER_EXPERTS, D_MODEL), D_MODEL ** -0.5),
        'peer_v': n(16, (DEPTH, PEER_EXPERTS, D_MODEL), PEER_HEADS ** -0.5),
        'g_final': 1.0 + n(17, (D_MODEL,), 0.02),
    }

def reference(x_prompt, x_sample, state_gla, cache_win_k, cache_win_v, g_attn, w_in, w_gate_up, b_gate,
              g_gla_out, attn_sinks, w_out, g_ffn, w_peer_q, peer_sub_keys, peer_u, peer_v, g_final):
    xp, xs = x_prompt, x_sample
    sp_l, kp_l, vp_l, ss_l, ksl, vsl = [], [], [], [], [], []
    for l in range(DEPTH):
        p = (g_attn[l], w_in[l], w_gate_up[l], b_gate[l], g_gla_out[l], attn_sinks[l], w_out[l],
             g_ffn[l], w_peer_q[l], peer_sub_keys[l], peer_u[l], peer_v[l])
        xp, sp, kp, vp = layer_prompt(xp, *p)
        xs, ss, k_s, v_s = layer_sample(xs, state_gla[l], cache_win_k[l], cache_win_v[l], *p)
        sp_l.append(sp); kp_l.append(kp); vp_l.append(vp)
        ss_l.append(ss); ksl.append(k_s); vsl.append(v_s)
    y_prompt = rms_norm(xp, g_final)
    y_sample = rms_norm(xs, g_final)
    return (y_prompt, y_sample, jnp.stack(sp_l), jnp.stack(kp_l), jnp.stack(vp_l),
            jnp.stack(ss_l), jnp.stack(ksl), jnp.stack(vsl))


_drawn_inputs = setup_inputs


def setup_inputs(seed=0):
    import zlib

    import numpy as np

    out = dict(_drawn_inputs(seed))
    spreads = {}
    factors = {'g_gla_out': 3.362, 'attn_sinks': 7.112, 'g_final': 7.967, 'g_ffn': 3.727}
    for name, (base, spread) in spreads.items():
        noise = np.random.default_rng([zlib.crc32(name.encode()), seed]).standard_normal(out[name].shape)
        drawn = base * np.exp(spread * noise) if base else spread * noise
        out[name] = __import__('jax').numpy.asarray(drawn.astype(out[name].dtype))
    for name, factor in factors.items():
        out[name] = (out[name] * factor).astype(out[name].dtype)
    return out
```

```python
from contextlib import ExitStack

import concourse.bass as bass
from concourse import mybir

ALU = mybir.AluOpType
ACT = mybir.ActivationFunctionType
AX_X = mybir.AxisListType.X
F32 = mybir.dt.float32
U32 = mybir.dt.uint32

P = 128
D = 2048
KC = D // P
SEQ = 512
DEC_BATCH, DEC_SEQ = 8, 8
SAMPLES = DEC_BATCH * DEC_SEQ
TOKENS = SEQ + SAMPLES
PROMPT_TILES = SEQ // P
TILES = PROMPT_TILES + 1
ROWS = TILES * P
NW = 512

GLA_HEADS, DK, DV = 4, 128, 256
GATE_RANK = 16
TAU = 16.0
GLA_CHUNK = 64
SWA_HEADS, HD, KV = 16, 64, 2
PAIRS = SWA_HEADS // 2
WINDOW = 128
EPS = 1e-6

Q0 = 0
K0 = Q0 + GLA_HEADS * DK
V0 = K0 + GLA_HEADS * DK
R0 = V0 + GLA_HEADS * DV
SQ0 = R0 + GLA_HEADS * DV
SK0 = SQ0 + SWA_HEADS * HD
SV0 = SK0 + KV * HD
GA0 = SV0 + KV * HD
PROJ = GA0 + GATE_RANK

N_KEYS = 128
PHEADS = 8
TOPK = 16
SEL = PHEADS * TOPK
NEG = -3.0e38


class Chip:
    pass


def stage(nc):
    ctx = ExitStack()
    sems = []

    def clear():
        nc.clear_and_free_semaphores(sems)
        nc.all_engine_barrier()

    ctx.callback(clear)

    def sb(name, shape, dt=F32):
        return ctx.enter_context(nc.sbuf_tensor(name, shape, dt))

    def sem(name):
        sems.append(nc.alloc_semaphore(name))
        return sems[-1]

    return ctx, sb, sem


def load_constants(nc, c):
    ctx, sb, sem = stage(nc)
    with ctx:
        loaded = sem("const_loaded")
        block = ctx.enter_context(nc.Block())

        @block.sync
        def _(sp):
            pairs = [(c.ident, c.d.ident), (c.g_attn, c.d.g_attn), (c.g_ffn, c.d.g_ffn)]
            for dst, src in pairs:
                sp.dma_start(dst[:], src).then_inc(loaded, 16)
            sp.wait_ge(loaded, 16 * len(pairs))


def norm_transpose(nc, c, name, src, gain):
    ctx, sb, sem = stage(nc)
    with ctx:
        rows = sb(name + "_rows", [P, D])
        square = sb(name + "_square", [P, D])
        scaled = sb(name + "_scaled", [P, D])
        stat = sb(name + "_stat", [P, 4])
        loaded, rows_free = sem(name + "_loaded"), sem(name + "_rows_free")
        summed, meaned, rooted, inverted = (sem(name + "_" + s) for s in ("summed", "meaned", "rooted", "inverted"))
        scaled_ready, turned, moved = (sem(name + "_" + s) for s in ("scaled_ready", "turned", "moved"))
        block = ctx.enter_context(nc.Block())

        @block.sync
        def _(sp):
            with sp.Fori(0, TILES) as i:
                sp.wait_ge(rows_free, i + 1)
                sp.sem_inc(c.held, 1)
                sp.dma_start(rows[:, :], src[bass.ds(i * P, P), :]).then_inc(loaded, 16)

        @block.scalar
        def _(act):
            with act.Fori(0, TILES) as i:
                act.wait_ge(loaded, i * 16 + 16)
                act.activation(square[:, :], rows[:, :], ACT.Square, accum_out=stat[:, 0:1]).then_inc(summed, 1)
                act.wait_ge(meaned, i + 1)
                act.activation(stat[:, 2:3], stat[:, 1:2], ACT.Sqrt).then_inc(rooted, 1)

        @block.vector
        def _(dve):
            dve.sem_inc(rows_free, 1)
            dve.sem_inc(moved, 4)
            with dve.Fori(0, TILES) as i:
                dve.wait_ge(summed, i + 1)
                dve.tensor_scalar(stat[:, 1:2], stat[:, 0:1], 1.0 / D, EPS, ALU.mult, ALU.add).then_inc(meaned, 1)
                dve.wait_ge(rooted, i + 1)
                dve.reciprocal(stat[:, 3:4], stat[:, 2:3]).then_inc(inverted, 1)
                dve.wait_ge(inverted, i + 1)
                dve.tensor_scalar(scaled[:, :], rows[:, :], stat[:, 3:4], None, ALU.mult).then_inc(scaled_ready, 1)
                dve.wait_ge(scaled_ready, i + 1)
                dve.sem_inc(rows_free, 1)
                for k in range(4):
                    dve.wait_ge(turned, i * 4 + (k + 1))
                    dve.tensor_tensor(c.act_t[:, 4 * k:4 * k + 4, bass.ds(i * P, P)],
                                      c.bank[:, k, :].rearrange("p (k t) -> p k t", k=4),
                                      gain[:, 4 * k:4 * k + 4].unsqueeze(2).broadcast_to([P, 4, P]),
                                      ALU.mult).then_inc(moved, 1)

        @block.tensor
        def _(pe):
            with pe.Fori(0, TILES) as i:
                pe.wait_ge(scaled_ready, i + 1)
                for k in range(4):
                    pe.wait_ge(moved, i * 4 + (k + 1))
                    for j in range(4):
                        s = 4 * k + j
                        last = pe.transpose(c.bank[:, k, j * P:(j + 1) * P], scaled[:, s * P:(s + 1) * P], c.ident[:, :])
                    last.then_inc(turned, 1)


def project(nc, c, name, weights, chunks, tail, dst, residual=None):
    ctx, sb, sem = stage(nc)
    with ctx:
        w = sb(name + "_w", [P, 2, KC, NW])
        out = sb(name + "_out", [P, TILES, NW])
        res = sb(name + "_res", [P, TILES, NW]) if residual is not None else None
        w_here = [sem(f"{name}_w_here{s}") for s in range(2)]
        w_free, out_free = sem(name + "_w_free"), sem(name + "_out_free")
        res_here, stored = sem(name + "_res_here"), [sem(f"{name}_stored{t}") for t in range(TILES)]
        summed, moved = sem(name + "_summed"), sem(name + "_moved")
        block = ctx.enter_context(nc.Block())
        width = tail.shape[2] if tail is not None else 0

        @block.sync
        def _(sp):
            with sp.Fori(0, chunks // 2) as i:
                for s in range(2):
                    sp.wait_ge(w_free, i * 2 + (s + 1))
                    sp.sem_inc(c.held, 1)
                    sp.dma_start(w[:, s], weights[bass.ds(i * 2 + s, 1)].rearrange("a p k n -> (a p) k n")).then_inc(w_here[s], 16)
            if tail is not None:
                sp.wait_ge(w_free, chunks + 1)
                sp.dma_start(w[:, 0, :, 0:width], tail).then_inc(w_here[0], 16)

        @block.gpsimd
        def _(pool):
            def store(n, col, wide):
                for t in range(TILES):
                    pool.wait_ge(moved, n * TILES + (TILES + t + 1))
                    pool.sem_inc(c.held, 1)
                    pool.dma_start(dst[t * P:(t + 1) * P, col], out[:, t, 0:wide]).then_inc(stored[t], 16)
                for t in range(TILES):
                    pool.wait_ge(stored[t], n * 16 + 16)
                pool.sem_inc(out_free, 1)

            with pool.Fori(0, chunks) as n:
                store(n, bass.ds(n * NW, NW), NW)
            if tail is not None:
                store(chunks, slice(chunks * NW, chunks * NW + width), width)

        @block.scalar
        def _(act):
            if residual is not None:
                with act.Fori(0, chunks) as n:
                    act.wait_ge(w_free, n + 2)
                    act.dma_start(res[:, :, :], residual[:, bass.ds(n * NW, NW)].rearrange("(t p) n -> p t n", p=P)).then_inc(res_here, 16)

        @block.vector
        def _(dve):
            dve.sem_inc(moved, TILES)
            dve.sem_inc(out_free, 1)

            def move(n, wide):
                if residual is not None:
                    dve.wait_ge(res_here, n * 16 + 16)
                dve.wait_ge(out_free, n + 1)
                for t in range(TILES):
                    dve.wait_ge(summed, n * TILES + (t + 1))
                    if residual is None:
                        dve.tensor_copy(out[:, t, 0:wide], c.bank[:, t, 0:wide]).then_inc(moved, 1)
                    else:
                        dve.tensor_tensor(out[:, t, 0:wide], c.bank[:, t, 0:wide], res[:, t, 0:wide], ALU.add).then_inc(moved, 1)
                dve.wait_ge(moved, n * TILES + 2 * TILES)
                dve.sem_inc(w_free, 1)

            dve.sem_inc(w_free, 2)
            with dve.Fori(0, chunks) as n:
                move(n, NW)
            if tail is not None:
                move(chunks, width)

        @block.tensor
        def _(pe):
            def products(n, s, uses, wide):
                pe.wait_ge(w_here[s], uses)
                for t in range(TILES):
                    pe.wait_ge(moved, n * TILES + (t + 1))
                    for k in range(KC):
                        last = pe.matmul(c.bank[:, t, 0:wide], c.act_t[:, k, t * P:(t + 1) * P], w[:, s, k, 0:wide],
                                         start=(k == 0), stop=(k == KC - 1))
                    last.then_inc(summed, 1)

            with pe.Fori(0, chunks // 2) as i:
                for s in range(2):
                    products(i * 2 + s, s, i * 16 + 16, NW)
            if tail is not None:
                products(chunks, 0, 16 * (chunks // 2) + 16, width)


def attend(nc, c, kind):
    prompt = kind == "prompt"
    turns = PROMPT_TILES if prompt else 1
    T = P if prompt else SAMPLES
    CL = GLA_CHUNK if prompt else DEC_SEQ
    NC = T // CL
    NB = SWA_HEADS if prompt else DEC_BATCH
    KW = 2 * WINDOW if prompt else DEC_SEQ + WINDOW
    ctx, sb_, sem_ = stage(nc)
    per = {}

    def sb(name, shape, dt=F32):
        return sb_(kind + "_" + name, shape, dt)

    def sem(name, n=1):
        s = sem_(kind + "_" + name)
        per[id(s)] = n
        return s

    with ctx:
        cur = sb("cur", [P, PROJ])
        tri = sb("tri", [T, T])
        suf = sb("suf", [T, T])
        ind = sb("ind", [T, NC])
        inside = sb("inside", [T, T])
        gate_w = sb("gate_w", [GATE_RANK + 1, GLA_HEADS * DK])
        ga_t = sb("ga_t", [GATE_RANK + 1, T])
        low = sb("low", [T, 512])
        mag = sb("mag", [T, 512])
        log1 = sb("log1", [T, 512])
        log_a = sb("log_a", [T, 512])
        eb = sb("eb", [T, 512])
        enb = sb("enb", [T, 512])
        ebd = sb("ebd", [T, 512])
        decay = sb("decay", [P, GLA_HEADS, NC])
        qg = sb("qg", [T, 512])
        kg = sb("kg", [T, 512])
        ke = sb("ke", [T, 512])
        qg_t = sb("qg_t", [P, GLA_HEADS, T])
        kg_t = sb("kg_t", [P, GLA_HEADS, T])
        q_spread = sb("q_spread", [P, GLA_HEADS, NC * (T + CL)])
        inner = sb("inner", [T, GLA_HEADS, T])
        o_stat = sb("o_stat", [T, 4, GLA_HEADS])
        o_norm = sb("o_norm", [T, GLA_HEADS * DV])
        o_junk = sb("o_junk", [T, DV])
        g_out = sb("g_out", [P, DV])
        er = sb("er", [T, GLA_HEADS * DV])
        silu = sb("silu", [T, GLA_HEADS * DV])
        state = sb("state", [P, 2 if prompt else NC, GLA_HEADS, DV])
        if not prompt:
            k_own = sb("k_own", [T, 2, NC, DK])
            own = sb("own", [T, NC])
        trig = sb("trig", [P, HD])
        roped = sb("roped", [P, SWA_HEADS + KV, HD])
        rt = [sb(f"rt{n}", [P, SWA_HEADS + KV, HD // 2]) for n in range(2)]
        k_twice = sb("k_twice", [P, KV, 2, HD])
        q_t = sb("q_t", [P, PAIRS, T])
        sinks = sb("sinks", [P, NB if prompt else 1])
        mask = sb("mask", [P, KW])
        scores = sb("scores", [P, NB, KW])
        st = sb("st", [P, 6, NB])
        if prompt:
            mask_all = sb("mask_all", [P, KW])
            k_t = sb("k_t", [P, KV, KW])
            v_before = sb("v_before", [P, KV * HD])
            probs_t = sb("probs_t", [P, NB, 2, P])
        else:
            k_t = sb("k_t", [P, NB, KV, KW])
            k_new = sb("k_new", [P, NB, KV * HD])
            v_new = sb("v_new", [P, NB, KV * HD])
            k_old = sb("k_old", [DEC_SEQ, NB, KV * HD])
            v_old = sb("v_old", [DEC_SEQ, NB, KV * HD])
            k2 = sb("k2", [P, 2, KV, 2, HD])
            k2_old = sb("k2_old", [DEC_SEQ, 2, KV, 2, HD])
            probs_t = sb("probs_t", [P, NB, P])
            probs_old_t = sb("probs_old_t", [DEC_SEQ, NB, P])

        const_here = sem("const_here")
        cur_here, trig_here = sem("cur_here", 16), sem("trig_here", 16)
        ga_turned, ga_ready = sem("ga_turned"), sem("ga_ready")
        gate_ready, low_ready, mag_ready = sem("gate_ready"), sem("low_ready"), sem("mag_ready")
        exp1_ready, log1_ready, log_a_ready = sem("exp1_ready"), sem("log1_ready"), sem("log_a_ready")
        sums_ready, exps_ready, gated = sem("sums_ready"), sem("exps_ready", 4), sem("gated", 3)
        gated_turned, qk_ready = sem("gated_turned", 2), sem("qk_ready", 3)
        inner_ready, inner_masked = sem("inner_ready"), sem("inner_masked")
        grown, state_ready = sem("grown", 2 if prompt else GLA_HEADS), sem("state_ready", 2 if prompt else GLA_HEADS)
        k_own_ready = sem("k_own_ready", GLA_HEADS)
        o_ready, o_summed, o_meaned, o_rooted = sem("o_ready"), sem("o_summed", GLA_HEADS), sem("o_meaned"), sem("o_rooted")
        o_inverted, o_normed = sem("o_inverted"), sem("o_normed", GLA_HEADS)
        er_ready, er_one, er_inverted, silu_ready = sem("er_ready"), sem("er_one"), sem("er_inverted"), sem("silu_ready")
        o_gated, o_turned, gla_heads_ready = sem("o_gated"), sem("o_turned", 2), sem("gla_heads_ready", 2)
        rope_step, k_twice_ready = sem("rope_step", 6), sem("k_twice_ready")
        q_turned, q_t_ready = sem("q_turned"), sem("q_t_ready", 2 if prompt else 1)
        k_turned, k_t_ready = sem("k_turned", 1 if prompt else NB), sem("k_t_ready", 1 if prompt else NB)
        SB = 4 if prompt else 2
        scored, score_moved = sem("scored", NB // SB), sem("score_moved", NB)
        topped, negated, sunk = sem("topped"), sem("negated"), sem("sunk")
        exped, sink_exped, totalled, inverted = sem("exped", NB), sem("sink_exped"), sem("totalled"), sem("inverted")
        weighted, p_turned = sem("weighted", 2), sem("p_turned", NB // 2)
        p_ready = [sem("p_ready_even", NB // 4), sem("p_ready_odd", NB // 4)]
        mixed, swa_heads_ready = sem("mixed"), sem("swa_heads_ready", 2 if prompt else 1)
        kept, stored = sem("kept", 3), sem("stored")
        turn_over = sem("turn_over", 4)

        new_here = sem("new_here", 32 * NB)
        all_consts = 16 * (8 + (1 if prompt else 6))
        first_ready = sem("first_ready")

        k2_ready = sem("k2_ready", NB)

        block = ctx.enter_context(nc.Block())
        b0, b1, b2, b3 = (c.bank[:, n, :] for n in range(4))

        def wait(eng, s, i, n=None):
            eng.wait_ge(s, i * per[id(s)] + (per[id(s)] if n is None else n))

        def loop(eng, body):
            def turn(i):
                body(i)
                for s in ((gla_heads_ready, swa_heads_ready, kept, k_twice_ready, state_ready) if prompt else ()):
                    wait(eng, s, i)
                    eng.sem_inc(c.held, 1)

            if turns > 1:
                with eng.Fori(0, turns) as i:
                    turn(i)
            else:
                turn(0)

        def tokens(i):
            return bass.ds(i * P, P) if prompt else slice(SEQ, TOKENS)

        consts = [(tri, c.d.tri[kind]), (suf, c.d.suf[kind]), (ind, c.d.ind[kind]), (inside, c.d.inside[kind]),
                  (gate_w, c.d.gate_w), (g_out, c.d.g_out), (sinks, c.d.sinks[kind]), (mask, c.d.mask[kind])]
        if prompt:
            consts += [(mask_all, c.d.mask["later"])]
        else:
            consts += [(own, c.d.own)]
            ck, cv = c.d.cache_k, c.d.cache_v
            consts += [(state, c.d.state_in.rearrange("b h d v -> d b h v")),
                       (k_old, ck[:, 0:DEC_SEQ, :].rearrange("b t f -> t b f")),
                       (v_old, cv[:, 0:DEC_SEQ, :].rearrange("b t f -> t b f"))]

        def score_bank(n):
            if prompt:
                return c.bank[:, 3 + n // 4 % 2 * 2 + n % 2, n // 2 % 2 * KW:(n // 2 % 2 + 1) * KW]
            return c.bank[:, 3 + n // 2 % 4, n % 2 * 256:n % 2 * 256 + KW]

        def move_probs(eng, i, n):
            wait(eng, p_turned, i, n + 1)
            src = c.bank[:, 3 + n % 4, :].rearrange("p (a b q) -> p a b q", a=2, b=2)
            if not prompt:
                nc.scalar.activation(probs_t[:, 2 * n:2 * n + 2, :], src[:, :, 0, :], ACT.Copy)
                nc.scalar.activation(probs_old_t[:, 2 * n:2 * n + 2, :], src[0:DEC_SEQ, :, 1, :], ACT.Copy).then_inc(p_ready[n % 2], 1)
            elif n % 2:
                nc.vector.tensor_copy(probs_t[:, 2 * n:2 * n + 2, :, :], src).then_inc(p_ready[1], 1)
            else:
                nc.scalar.activation(probs_t[:, 2 * n:2 * n + 2, :, :], src, ACT.Copy).then_inc(p_ready[0], 1)

        def new_state(dve, i, h):
            wait(dve, grown, i, h + 1)
            wait(dve, o_ready, i)
            for b in range(NC):
                ins = dve.scalar_tensor_tensor(out=state[:, b, h, :], in0=state[:, b, h, :], scalar=decay[:, h, b:b + 1],
                                               in1=c.bank[:, 4 + b // 2, (b % 2) * DV:(b % 2 + 1) * DV],
                                               op0=ALU.mult, op1=ALU.add)
            ins.then_inc(state_ready, 1)

        def move_keys(dve, i, b):
            wait(dve, k_turned, i, b + 1)
            bank = c.bank[:, 1 + b % 2, :]
            dve.tensor_copy(k_t[:, b, :, DEC_SEQ:KW], bank[:, 0:KV * P].rearrange("p (g t) -> p g t", g=KV))
            dve.tensor_copy(k_t[:, b, :, 0:DEC_SEQ],
                            bank[:, KV * P:KV * P + KV * DEC_SEQ].rearrange("p (g t) -> p g t", g=KV)).then_inc(k_t_ready, 1)

        @block.sync
        def _(sp):
            for dst, src in consts:
                sp.dma_start(dst[:], src).then_inc(const_here, 16)
            if not prompt:
                for dst, src in ((k_new, ck), (v_new, cv)):
                    sp.dma_start(dst[0:WINDOW - DEC_SEQ, :, :],
                                 src[:, DEC_SEQ:WINDOW, :].rearrange("b t f -> t b f")).then_inc(const_here, 16)

            def body(i):
                if prompt:
                    sp.sem_inc(c.held, 1)
                    sp.dma_start(cur[:, :], c.d.proj[bass.ds(i * P, P), :]).then_inc(cur_here, 16)
                    sp.sem_inc(c.held, 1)
                    sp.dma_start(trig[:, :], c.d.trig[bass.ds(i * P, P), :]).then_inc(trig_here, 16)
                else:
                    sp.dma_start(cur[0:T, :], c.d.proj[SEQ:TOKENS, :]).then_inc(cur_here, 16)
                    sp.dma_start(trig[0:T, :], c.d.trig[SEQ:TOKENS, :]).then_inc(trig_here, 16)

            loop(sp, body)
            if prompt:
                sp.dma_start(c.d.k_out_prompt, roped[:, SWA_HEADS:SWA_HEADS + KV, :].rearrange("t g d -> t (g d)")).then_inc(stored, 16)
                sp.dma_start(c.d.v_out_prompt, cur[:, SV0:SV0 + KV * HD]).then_inc(stored, 16)
                sp.dma_start(c.d.state_out_prompt.rearrange("h d v -> d h v"), state[:, 0, :, :]).then_inc(stored, 16)
                sp.wait_ge(stored, 48)
            else:
                wait(sp, rope_step, 0)
                for b in range(NB):
                    rows = slice(b * DEC_SEQ, (b + 1) * DEC_SEQ)
                    sp.dma_start(k_new[WINDOW - DEC_SEQ:WINDOW, b, :],
                                 roped[rows, SWA_HEADS:SWA_HEADS + KV, :].rearrange("t g d -> t (g d)")).then_inc(new_here, 16)
                    sp.dma_start(v_new[WINDOW - DEC_SEQ:WINDOW, b, :], cur[rows, SV0:SV0 + KV * HD]).then_inc(new_here, 16)
                sp.wait_ge(new_here, 32 * NB)
                sp.wait_ge(const_here, all_consts)
                sp.dma_start(c.d.k_out_sample.rearrange("b t f -> t b f"), k_new[:, :, :]).then_inc(stored, 16)
                sp.dma_start(c.d.v_out_sample.rearrange("b t f -> t b f"), v_new[:, :, :]).then_inc(stored, 16)
                sp.wait_ge(state_ready, GLA_HEADS)
                sp.dma_start(c.d.state_out_sample.rearrange("b h d v -> d b h v"), state[:, :, :, :]).then_inc(stored, 16)
                sp.wait_ge(stored, 48)


        @block.gpsimd
        def _(pool):
            if prompt:
                pool.memset(v_before[:, :], 0.0).then_inc(first_ready, 1)
            half = HD // 2
            heads = SWA_HEADS + KV

            def body(i):
                wait(pool, cur_here, i)
                wait(pool, trig_here, i)
                pool.sem_inc(c.held, 1)
                x = cur[0:T, SQ0:SQ0 + heads * HD].rearrange("t (h d) -> t h d", d=HD)
                x1, x2 = x[:, :, 0:half], x[:, :, half:HD]
                cos = trig[0:T, 0:half].unsqueeze(1).broadcast_to([T, heads, half])
                sin = trig[0:T, half:HD].unsqueeze(1).broadcast_to([T, heads, half])
                t0, t1 = rt[0][0:T], rt[1][0:T]
                out1, out2 = roped[0:T, :, 0:half], roped[0:T, :, half:HD]
                steps = [(t0, x1, cos, ALU.mult), (t1, x2, sin, ALU.mult), (out1, t0, t1, ALU.subtract),
                         (t0, x2, cos, ALU.mult), (t1, x1, sin, ALU.mult), (out2, t0, t1, ALU.add)]
                for n, (o, a, b, op) in enumerate(steps):
                    if n:
                        wait(pool, rope_step, i, n)
                        pool.sem_inc(c.held, 1)
                    pool.tensor_tensor(o, a, b, op).then_inc(rope_step, 1)
                wait(pool, rope_step, i)
                pool.sem_inc(c.held, 1)
                if prompt:
                    keys = roped[:, SWA_HEADS:heads, :]
                    pool.tensor_copy(k_twice[:, :, 0, :], keys)
                    pool.tensor_copy(k_twice[:, :, 1, :], keys).then_inc(k_twice_ready, 1)
                wait(pool, er_inverted, i)
                pool.sem_inc(c.held, 1)
                pool.tensor_tensor(silu[:, :], cur[0:T, R0:R0 + GLA_HEADS * DV], er[:, :], ALU.mult).then_inc(silu_ready, 1)
                wait(pool, inverted, i)
                wait(pool, exped, i)
                pool.sem_inc(c.held, 1)
                for n in range(2):
                    blocks = slice(n * NB // 2, (n + 1) * NB // 2)
                    pool.tensor_tensor(scores[:, blocks, :], scores[:, blocks, :],
                                       st[:, 5, blocks].unsqueeze(2).broadcast_to([P, NB // 2, KW]), ALU.mult).then_inc(weighted, 1)
                if prompt:
                    wait(pool, mixed, i)
                    pool.sem_inc(c.held, 1)
                    pool.tensor_copy(v_before[:, :], cur[:, SV0:SV0 + KV * HD]).then_inc(kept, 1)
                    pool.tensor_copy(k_t[:, :, 0:WINDOW], k_t[:, :, WINDOW:KW]).then_inc(kept, 1)
                    pool.tensor_copy(mask[:, :], mask_all[:, :]).then_inc(kept, 1)

            loop(pool, body)

        @block.scalar
        def _(act):
            act.wait_ge(const_here, all_consts)
            act.sem_inc(c.held, 1)

            def body(i):
                wait(act, mag_ready, i)
                act.activation(log1[:, :], mag[:, :], ACT.Exp).then_inc(exp1_ready, 1)
                wait(act, cur_here, i)
                act.activation(er[:, :], cur[0:T, R0:R0 + GLA_HEADS * DV], ACT.Exp, scale=-1.0).then_inc(er_ready, 1)
                wait(act, exp1_ready, i)
                act.activation(log1[:, :], log1[:, :], ACT.Ln, bias=1.0).then_inc(log1_ready, 1)
                wait(act, sums_ready, i)
                act.activation(eb[:, :], b2[0:T, :], ACT.Exp).then_inc(exps_ready, 1)
                act.activation(enb[:, :], b2[0:T, :], ACT.Exp, scale=-1.0).then_inc(exps_ready, 1)
                act.activation(ebd[:, :], b3[0:T, :], ACT.Exp).then_inc(exps_ready, 1)
                act.activation(decay[:, :, :], b0[:, 0:GLA_HEADS * NC].rearrange("p (h n) -> p h n", h=GLA_HEADS), ACT.Exp).then_inc(exps_ready, 1)
                wait(act, gated_turned, i)
                act.activation(kg_t[:, :, :], c.bank[:, 5, 0:GLA_HEADS * T].rearrange("p (h t) -> p h t", h=GLA_HEADS), ACT.Copy).then_inc(qk_ready, 1)
                wait(act, o_ready, i)
                for h in range(GLA_HEADS):
                    if h:
                        wait(act, o_summed, i, h)
                    act.activation(o_junk[:, :], c.bank[0:T, 2 + h // 2, (h % 2) * DV:(h % 2 + 1) * DV], ACT.Square,
                                   accum_out=o_stat[:, 0, h:h + 1]).then_inc(o_summed, 1)
                wait(act, o_meaned, i)
                act.activation(o_stat[:, 2, :], o_stat[:, 1, :], ACT.Sqrt).then_inc(o_rooted, 1)
                wait(act, o_turned, i)
                act.sem_inc(c.held, 1)
                for n in range(2):
                    act.activation(c.act_t[:, 4 * n:4 * n + 4, tokens(i)],
                                   c.bank[:, 6 + n, 0:4 * T].rearrange("p (k t) -> p k t", k=4), ACT.Copy).then_inc(gla_heads_ready, 1)
                wait(act, q_turned, i)
                if prompt:
                    for n in range(2):
                        act.activation(q_t[:, 4 * n:4 * n + 4, :], c.bank[:, n, :].rearrange("p (k t) -> p k t", k=4), ACT.Copy,
                                       scale=HD ** -0.5).then_inc(q_t_ready, 1)
                else:
                    act.activation(q_t[:, :, :].rearrange("p k t -> p (k t)").rearrange("p (b k t) -> p k b t", b=NB, k=PAIRS),
                                   b0.rearrange("p (k b t) -> p k b t", b=NB, k=PAIRS), ACT.Copy,
                                   scale=HD ** -0.5).then_inc(q_t_ready, 1)
                wait(act, negated, i)
                for n in range(NB):
                    act.activation(scores[:, n, :], scores[:, n, :], ACT.Exp, bias=st[:, 2, n:n + 1],
                                   accum_out=st[:, 3, n:n + 1]).then_inc(exped, 1)
                wait(act, sunk, i)
                act.activation(st[:, 4, :], st[:, 4, :], ACT.Exp).then_inc(sink_exped, 1)
                for n in range(NB // 2):
                    if n % 2 == 0 or not prompt:
                        move_probs(act, i, n)
                wait(act, mixed, i)
                act.sem_inc(c.held, 1)
                if prompt:
                    for n in range(2):
                        act.activation(c.act_t[:, PAIRS + 4 * n:PAIRS + 4 * n + 4, tokens(i)],
                                       c.bank[:, n, :].rearrange("p (k t) -> p k t", k=4), ACT.Copy).then_inc(swa_heads_ready, 1)
                else:
                    act.activation(c.act_t[:, PAIRS:2 * PAIRS, tokens(i)],
                                   c.bank[:, 0, :].rearrange("p (k t) -> p k t", k=PAIRS), ACT.Copy).then_inc(swa_heads_ready, 1)

            loop(act, body)

        @block.vector
        def _(dve):
            dve.memset(ga_t[:, :], 1.0).then_inc(first_ready, 1)
            dve.memset(q_spread[:, :, :], 0.0).then_inc(first_ready, 1)
            if prompt:
                dve.memset(state[:, 0, :, :], 0.0).then_inc(first_ready, 1)
                dve.memset(k_t[:, :, 0:WINDOW], 0.0).then_inc(first_ready, 1)
            dve.wait_ge(const_here, all_consts)
            dve.wait_ge(first_ready, 5 if prompt else 2)
            dve.sem_inc(c.held, 1)

            def body(i):
                wait(dve, ga_turned, i)
                dve.tensor_copy(ga_t[0:GATE_RANK, :], b0[0:GATE_RANK, 0:T]).then_inc(ga_ready, 1)
                wait(dve, gate_ready, i)
                dve.tensor_scalar(low[:, :], b1[0:T, :], 0.0, None, ALU.min).then_inc(low_ready, 1)
                wait(dve, low_ready, i)
                dve.scalar_tensor_tensor(out=mag[:, :], in0=low[:, :], scalar=2.0, in1=b1[0:T, :],
                                         op0=ALU.mult, op1=ALU.subtract).then_inc(mag_ready, 1)
                wait(dve, log1_ready, i)
                dve.tensor_tensor(log_a[:, :], low[:, :], log1[:, :], ALU.subtract).then_inc(log_a_ready, 1)
                wait(dve, er_ready, i)
                dve.tensor_scalar(er[:, :], er[:, :], 1.0, None, ALU.add).then_inc(er_one, 1)
                wait(dve, er_one, i)
                dve.reciprocal(er[:, :], er[:, :]).then_inc(er_inverted, 1)
                wait(dve, exps_ready, i)
                dve.scalar_tensor_tensor(out=qg[:, :], in0=cur[0:T, Q0:Q0 + 512], scalar=DK ** -0.5, in1=eb[:, :],
                                         op0=ALU.mult, op1=ALU.mult).then_inc(gated, 1)
                dve.tensor_tensor(kg[:, :], cur[0:T, K0:K0 + 512], enb[:, :], ALU.mult).then_inc(gated, 1)
                dve.tensor_tensor(ke[:, :], cur[0:T, K0:K0 + 512], ebd[:, :], ALU.mult).then_inc(gated, 1)
                wait(dve, gated_turned, i, 1)
                q_bank = c.bank[:, 4, 0:GLA_HEADS * T].rearrange("p (h t) -> p h t", h=GLA_HEADS)
                dve.tensor_copy(qg_t[:, :, :], q_bank).then_inc(qk_ready, 1)
                for h in range(GLA_HEADS):
                    ins = dve.tensor_copy(q_spread[:, h, :].rearrange("p (n x) -> p n x", n=NC)[:, :, 0:CL],
                                          q_bank[:, h, :].rearrange("p (n x) -> p n x", n=NC))
                ins.then_inc(qk_ready, 1)
                wait(dve, inner_ready, i)
                dve.tensor_tensor(inner[:, :, :], c.bank[0:T, 6, 0:GLA_HEADS * T].rearrange("p (h t) -> p h t", h=GLA_HEADS),
                                  inside[:, :].unsqueeze(1).broadcast_to([T, GLA_HEADS, T]), ALU.mult).then_inc(inner_masked, 1)
                if prompt:
                    wait(dve, grown, i, 1)
                    for h in range(GLA_HEADS):
                        ins = dve.scalar_tensor_tensor(out=state[:, 1, h, :], in0=state[:, 0, h, :], scalar=decay[:, h, 0:1],
                                                       in1=c.bank[:, 4 + h // 2, (h % 2) * DV:(h % 2 + 1) * DV],
                                                       op0=ALU.mult, op1=ALU.add)
                    ins.then_inc(state_ready, 1)
                else:
                    for h in range(GLA_HEADS):
                        if h >= 2:
                            wait(dve, grown, i, h - 1)
                        dve.tensor_tensor(k_own[:, h % 2, :, :],
                                          ke[:, h * DK:(h + 1) * DK].unsqueeze(1).broadcast_to([T, NC, DK]),
                                          own[:, :].unsqueeze(2).broadcast_to([T, NC, DK]), ALU.mult).then_inc(k_own_ready, 1)
                        if h >= 1:
                            new_state(dve, i, h - 1)
                    new_state(dve, i, GLA_HEADS - 1)
                wait(dve, o_summed, i)
                dve.tensor_scalar(o_stat[:, 1, :], o_stat[:, 0, :], 1.0 / DV, EPS, ALU.mult, ALU.add).then_inc(o_meaned, 1)
                if prompt:
                    wait(dve, grown, i, 2)
                    wait(dve, o_ready, i)
                    for h in range(GLA_HEADS):
                        ins = dve.scalar_tensor_tensor(out=state[:, 0, h, :], in0=state[:, 1, h, :], scalar=decay[:, h, 1:2],
                                                       in1=c.bank[:, h // 2, (h % 2) * DV:(h % 2 + 1) * DV],
                                                       op0=ALU.mult, op1=ALU.add)
                    ins.then_inc(state_ready, 1)
                wait(dve, o_rooted, i)
                dve.reciprocal(o_stat[:, 3, :], o_stat[:, 2, :]).then_inc(o_inverted, 1)
                wait(dve, o_inverted, i)
                for h in range(GLA_HEADS):
                    dve.scalar_tensor_tensor(out=o_norm[:, h * DV:(h + 1) * DV],
                                             in0=c.bank[0:T, 2 + h // 2, (h % 2) * DV:(h % 2 + 1) * DV],
                                             scalar=o_stat[:, 3, h:h + 1], in1=g_out[0:T, :],
                                             op0=ALU.mult, op1=ALU.mult).then_inc(o_normed, 1)
                wait(dve, silu_ready, i)
                wait(dve, o_normed, i)
                dve.tensor_tensor(o_norm[:, :], o_norm[:, :], silu[:, :], ALU.mult).then_inc(o_gated, 1)
                if prompt:
                    wait(dve, k_turned, i)
                    dve.tensor_copy(k_t[:, :, WINDOW:KW], c.bank[:, 2, 0:KV * P].rearrange("p (g t) -> p g t", g=KV)).then_inc(k_t_ready, 1)
                else:
                    dve.wait_ge(new_here, 32 * NB)
                    for b in range(NB):
                        if b >= 2:
                            wait(dve, k_turned, i, b - 1)
                        fresh = k_new[:, b, :].rearrange("t (g d) -> t g d", g=KV)
                        old = k_old[:, b, :].rearrange("t (g d) -> t g d", g=KV)
                        for twice in range(2):
                            dve.tensor_copy(k2[:, b % 2, :, twice, :], fresh)
                            ins = dve.tensor_copy(k2_old[:, b % 2, :, twice, :], old)
                        ins.then_inc(k2_ready, 1)
                        if b:
                            move_keys(dve, i, b - 1)
                    move_keys(dve, i, NB - 1)
                for n in range(NB):
                    wait(dve, scored, i, n // SB + 1)
                    dve.sem_inc(c.held, 1)
                    dve.tensor_tensor_reduce(out=scores[:, n, :], in0=score_bank(n),
                                             in1=mask[:, :], scale=1.0, scalar=NEG, op0=ALU.add, op1=ALU.max,
                                             accum_out=st[:, 0, n:n + 1]).then_inc(score_moved, 1)
                wait(dve, score_moved, i)
                sink_row = sinks[:, :] if prompt else sinks[:, :].broadcast_to([P, NB])
                dve.tensor_tensor(st[:, 1, :], st[:, 0, :], sink_row, ALU.max).then_inc(topped, 1)
                wait(dve, topped, i)
                dve.tensor_scalar(st[:, 2, :], st[:, 1, :], -1.0, None, ALU.mult).then_inc(negated, 1)
                dve.tensor_tensor(st[:, 4, :], sink_row, st[:, 1, :], ALU.subtract).then_inc(sunk, 1)
                wait(dve, exped, i)
                wait(dve, sink_exped, i)
                dve.tensor_tensor(st[:, 3, :], st[:, 3, :], st[:, 4, :], ALU.add).then_inc(totalled, 1)
                wait(dve, totalled, i)
                dve.reciprocal(st[:, 5, :], st[:, 3, :]).then_inc(inverted, 1)
                for n in range(1, NB // 2, 2):
                    if prompt:
                        move_probs(dve, i, n)

            loop(dve, body)

        @block.tensor
        def _(pe):
            pe.wait_ge(const_here, all_consts)
            pe.wait_ge(first_ready, 5 if prompt else 2)
            pe.sem_inc(c.held, 1)
            ident = c.ident

            def body(i):
                wait(pe, cur_here, i)
                pe.transpose(b0[0:GATE_RANK, 0:T], cur[0:T, GA0:GA0 + GATE_RANK], ident[0:T, 0:T]).then_inc(ga_turned, 1)
                wait(pe, ga_ready, i)
                pe.matmul(b1[0:T, :], ga_t[:, :], gate_w[:, :], start=True, stop=True).then_inc(gate_ready, 1)
                wait(pe, log_a_ready, i)
                pe.matmul(b2[0:T, :], tri[:, :], log_a[:, :], start=True, stop=True)
                pe.matmul(b3[0:T, :], suf[:, :], log_a[:, :], start=True, stop=True)
                for h in range(GLA_HEADS):
                    last = pe.matmul(b0[:, h * NC:(h + 1) * NC], log_a[:, h * DK:(h + 1) * DK], ind[:, :], start=True, stop=True)
                last.then_inc(sums_ready, 1)
                for bank, x, n in ((4, qg, 1), (5, kg, 2)):
                    wait(pe, gated, i, n)
                    for h in range(GLA_HEADS):
                        last = pe.transpose(c.bank[:, bank, h * T:(h + 1) * T], x[:, h * DK:(h + 1) * DK], ident[0:T, 0:T])
                    last.then_inc(gated_turned, 1)
                wait(pe, qk_ready, i)
                for h in range(GLA_HEADS):
                    last = pe.matmul(c.bank[0:T, 6, h * T:(h + 1) * T], kg_t[:, h, :], qg_t[:, h, :], start=True, stop=True)
                last.then_inc(inner_ready, 1)
                wait(pe, gated, i)
                if prompt:
                    for n, bank in ((0, 4), (1, 0)):
                        rows = slice(n * CL, (n + 1) * CL)
                        for h in range(GLA_HEADS):
                            last = pe.matmul(c.bank[:, bank + h // 2, (h % 2) * DV:(h % 2 + 1) * DV],
                                             ke[rows, h * DK:(h + 1) * DK], cur[rows, V0 + h * DV:V0 + (h + 1) * DV],
                                             start=True, stop=True)
                        last.then_inc(grown, 1)
                    wait(pe, state_ready, i, 1)
                wait(pe, inner_masked, i)
                for h in range(GLA_HEADS):
                    out = c.bank[0:T, 2 + h // 2, (h % 2) * DV:(h % 2 + 1) * DV]
                    pe.matmul(out, inner[:, h, :], cur[0:T, V0 + h * DV:V0 + (h + 1) * DV], start=True, stop=False)
                    for n in range(NC):
                        last = pe.matmul(out, q_spread[:, h, n * T:(n + 1) * T], state[:, n, h, :], start=False, stop=(n == NC - 1))
                last.then_inc(o_ready, 1)
                if not prompt:
                    for h in range(GLA_HEADS):
                        wait(pe, k_own_ready, i, h + 1)
                        if h:
                            wait(pe, state_ready, i, h)
                        for b in range(NC):
                            last = pe.matmul(c.bank[:, 4 + b // 2, (b % 2) * DV:(b % 2 + 1) * DV], k_own[:, h % 2, b, :],
                                             cur[0:T, V0 + h * DV:V0 + (h + 1) * DV], start=True, stop=True)
                        last.then_inc(grown, 1)
                    wait(pe, state_ready, i)
                wait(pe, o_gated, i)
                for n in range(2):
                    for j in range(4):
                        k = 4 * n + j
                        last = pe.transpose(c.bank[:, 6 + n, j * T:(j + 1) * T], o_norm[:, k * P:(k + 1) * P], ident[0:T, 0:T])
                    last.then_inc(o_turned, 1)
                wait(pe, rope_step, i)
                wait(pe, state_ready, i)
                per_bank = 4 if prompt else PAIRS
                for k in range(PAIRS):
                    last = pe.transpose(c.bank[:, k // per_bank, k % per_bank * T:(k % per_bank + 1) * T],
                                        roped[0:T, 2 * k:2 * k + 2, :].rearrange("t h d -> t (h d)"), ident[0:T, 0:T])
                last.then_inc(q_turned, 1)
                if prompt:
                    wait(pe, k_twice_ready, i)
                    wait(pe, o_normed, i)
                    for g in range(KV):
                        last = pe.transpose(c.bank[:, 2, g * P:(g + 1) * P], k_twice[:, g, :, :].rearrange("t a d -> t (a d)"), ident[:, :])
                    last.then_inc(k_turned, 1)
                    wait(pe, q_t_ready, i)
                    wait(pe, k_t_ready, i)
                    wait(pe, gla_heads_ready, i)
                    for h in range(SWA_HEADS):
                        n, par, g = h // 2, h % 2, h // (SWA_HEADS // KV)
                        if h % SB == 0 and h >= 2 * SB:
                            wait(pe, score_moved, i, h - SB)
                        rows = slice(par * HD, (par + 1) * HD)
                        last = pe.matmul(score_bank(h), q_t[rows, h // 2, :], k_t[rows, g, :],
                                         start=True, stop=True)
                        if h % SB == SB - 1:
                            last.then_inc(scored, 1)
                else:
                    wait(pe, o_normed, i)
                    for b in range(NB):
                        wait(pe, k2_ready, i, b + 1)
                        if b >= 2:
                            wait(pe, k_t_ready, i, b - 1)
                        bank = c.bank[:, 1 + b % 2, :]
                        for g in range(KV):
                            pe.transpose(bank[:, g * P:(g + 1) * P], k2[:, b % 2, g, :, :].rearrange("t a d -> t (a d)"), ident[:, :])
                            at = KV * P + g * DEC_SEQ
                            last = pe.transpose(bank[:, at:at + DEC_SEQ], k2_old[:, b % 2, g, :, :].rearrange("t a d -> t (a d)"),
                                                ident[0:DEC_SEQ, 0:DEC_SEQ])
                        last.then_inc(k_turned, 1)
                    wait(pe, q_t_ready, i)
                    wait(pe, gla_heads_ready, i)
                    for b in range(NB):
                        n = b // 2
                        wait(pe, k_t_ready, i, b + 1)
                        for g in range(KV):
                            for par in range(2):
                                rows = slice(par * HD, (par + 1) * HD)
                                at = g * HD + par * 32
                                last = pe.matmul(c.bank[at:at + 32, 3 + n % 4, (b % 2) * 256:(b % 2) * 256 + KW],
                                                 q_t[rows, b, 32 * g:32 * g + 32],
                                                 k_t[rows, b, g, :], start=True, stop=True)
                        if b % 2:
                            last.then_inc(scored, 1)
                for n in range(NB // 2):
                    wait(pe, weighted, i, 1 if n < NB // 4 else 2)
                    if n == 0:
                        wait(pe, score_moved, i)
                    if n >= 4:
                        wait(pe, p_ready[n % 2], i, (n - 4) // 2 + 1)
                    for a in range(2):
                        for half in range(2):
                            dst = c.bank[:, 3 + n % 4, (2 * a + half) * P:(2 * a + half + 1) * P]
                            if prompt:
                                last = pe.transpose(dst, scores[:, 2 * n + a, half * P:(half + 1) * P], ident[:, :])
                            elif half == 0:
                                last = pe.transpose(dst, scores[:, 2 * n + a, DEC_SEQ:KW], ident[:, :])
                            else:
                                last = pe.transpose(dst[0:DEC_SEQ, :], scores[:, 2 * n + a, 0:DEC_SEQ], ident[:, :])
                    last.then_inc(p_turned, 1)
                wait(pe, p_ready[0], i)
                wait(pe, p_ready[1], i)
                if prompt:
                    for h in range(SWA_HEADS):
                        par, g = h % 2, h // (SWA_HEADS // KV)
                        out = c.bank[par * HD:(par + 1) * HD, h // 8, h // 2 % 4 * P:(h // 2 % 4 + 1) * P]
                        pe.matmul(out, v_before[:, g * HD:(g + 1) * HD], probs_t[:, h, 0, :], start=True, stop=False)
                        last = pe.matmul(out, cur[:, SV0 + g * HD:SV0 + (g + 1) * HD], probs_t[:, h, 1, :], start=False, stop=True)
                else:
                    for b in range(NB):
                        for g in range(KV):
                            for par in range(2):
                                at = g * HD + par * 32
                                out = c.bank[par * HD:(par + 1) * HD, 0, :].rearrange("p (k t) -> p k t", k=PAIRS)[
                                    :, 4 * g:4 * g + 4, b * DEC_SEQ:(b + 1) * DEC_SEQ]
                                pe.matmul(out, v_new[:, b, g * HD:(g + 1) * HD],
                                          probs_t[:, b, at:at + 32].rearrange("p (k t) -> p k t", k=4), start=True, stop=False)
                                last = pe.matmul(out, v_old[:, b, g * HD:(g + 1) * HD],
                                                 probs_old_t[:, b, at:at + 32].rearrange("p (k t) -> p k t", k=4),
                                                 start=False, stop=True)
                last.then_inc(mixed, 1)

            loop(pe, body)


def expert_queries(nc, c):
    ctx, sb, sem = stage(nc)
    with ctx:
        w = sb("pq_w", [P, 2, KC, P])
        w_here = [sem(f"pq_w_here{s}") for s in range(2)]
        summed, moved = sem("pq_summed"), sem("pq_moved")
        block = ctx.enter_context(nc.Block())
        half = TOKENS // 2

        @block.sync
        def _(sp):
            with sp.Fori(0, PHEADS // 2) as i:
                for s in range(2):
                    sp.wait_ge(moved, i * 4 + 2 * (s + 1))
                    sp.sem_inc(c.held, 1)
                    sp.dma_start(w[:, s], c.d.w_peer_q[bass.ds(i * 2 + s, 1)].rearrange("a p k n -> (a p) k n")).then_inc(w_here[s], 16)

        @block.vector
        def _(dve):
            dve.memset(c.query_t[:, :, TOKENS:ROWS], 0.0)
            dve.sem_inc(moved, 4)
            with dve.Fori(0, PHEADS // 2) as i:
                for s in range(2):
                    for n in range(2):
                        dve.wait_ge(summed, i * 4 + (2 * s + n + 1))
                        dve.sem_inc(c.held, 1)
                        dve.tensor_copy(c.query_t[:, bass.ds(i * 2 + s, 1), n * half:(n + 1) * half],
                                        c.bank[:, 2 * s + n, 0:half].unsqueeze(1)).then_inc(moved, 1)

        @block.tensor
        def _(pe):
            with pe.Fori(0, PHEADS // 2) as i:
                for s in range(2):
                    pe.wait_ge(w_here[s], i * 16 + 16)
                    for n in range(2):
                        pe.wait_ge(moved, i * 4 + (2 * s + n + 1))
                        for k in range(KC):
                            last = pe.matmul(c.bank[:, 2 * s + n, 0:half], w[:, s, k, :], c.act_t[:, k, n * half:(n + 1) * half],
                                             start=(k == 0), stop=(k == KC - 1))
                        last.then_inc(summed, 1)


def route(nc, c):
    ctx, sb, sem = stage(nc)
    HP = 2 * PHEADS
    with ctx:
        query = sb("rt_query", [P, PHEADS, P])
        keys = sb("rt_keys", [P, PHEADS, N_KEYS])
        score = sb("rt_score", [P, HP, N_KEYS])
        top = sb("rt_top", [P, HP, TOPK])
        top_at = sb("rt_top_at", [P, HP, TOPK], U32)
        top_atf = sb("rt_top_atf", [P, HP, TOPK])
        pair = sb("rt_pair", [P, PHEADS, TOPK * TOPK])
        best = sb("rt_best", [P, PHEADS, TOPK])
        best_at = sb("rt_best_at", [P, PHEADS, TOPK], U32)
        rank = sb("rt_rank", [P, 2, SEL], U32)
        rankf = sb("rt_rankf", [P, 2, SEL])
        rank16 = sb("rt_rank16", [P, TOPK])
        hit = sb("rt_hit", [P, PHEADS, TOPK, TOPK])
        picks = sb("rt_picks", [P, 3, SEL])
        total = sb("rt_total", [P, 2, PHEADS])
        const_here, query_ready, scored, score_ready = sem("rt_const"), sem("rt_query_ready"), sem("rt_scored"), sem("rt_score_ready")
        found, shifted, exped, picked = sem("rt_found"), sem("rt_shifted"), sem("rt_exped"), sem("rt_picked")
        turned, moved = sem("rt_turned"), sem("rt_moved")
        block = ctx.enter_context(nc.Block())

        @block.sync
        def _(sp):
            sp.dma_start(keys[:, :, :], c.d.sub_keys).then_inc(const_here, 16)
            sp.dma_start(rank16[:, :], c.d.rank16).then_inc(const_here, 16)

        @block.scalar
        def _(act):
            act.sem_inc(query_ready, 1)
            with act.Fori(0, TILES) as i:
                act.wait_ge(moved, i + 1)
                act.sem_inc(c.held, 1)
                act.activation(query[:, :, :], c.query_t[:, :, bass.ds(i * P, P)], ACT.Copy).then_inc(query_ready, 1)
                act.wait_ge(scored, i + 1)
                act.activation(score[:, :, :], c.bank[:, 0:4, :].rearrange("p b (s n) -> p (b s) n", n=N_KEYS), ACT.Copy).then_inc(score_ready, 1)
                act.wait_ge(shifted, i + 1)
                act.activation(best[:, :, :], best[:, :, :], ACT.Exp).then_inc(exped, 1)

        @block.vector
        def _(dve):
            n_steps = [0]

            def steps(i, instructions):
                for make in instructions:
                    dve.wait_ge(found, i * STEPS + n_steps[0]) if n_steps[0] else None
                    if n_steps[0]:
                        dve.sem_inc(c.held, 1)
                    make().then_inc(found, 1)
                    n_steps[0] += 1

            def top16(values, out, at, n):
                def each(make):
                    def run():
                        for r in range(n):
                            last = make(r)
                        return last
                    return run
                return [each(lambda r: dve.max(out[:, r, 0:8], values[:, r, :])),
                        each(lambda r: dve.max_index(at[:, r, 0:8], out[:, r, 0:8], values[:, r, :])),
                        each(lambda r: dve.match_replace(values[:, r, :], out[:, r, 0:8], values[:, r, :], NEG)),
                        each(lambda r: dve.max(out[:, r, 8:16], values[:, r, :])),
                        each(lambda r: dve.max_index(at[:, r, 8:16], out[:, r, 8:16], values[:, r, :]))]

            top4 = top[:, :, :].rearrange("p (s h) k -> p s h k", s=2)
            at4 = top_atf[:, :, :].rearrange("p (s h) k -> p s h k", s=2)
            four = [P, PHEADS, TOPK, TOPK]
            gate = picks[:, 2, :].rearrange("p (h k) -> p h k", h=PHEADS)

            def after_keys():
                out = [lambda: dve.tensor_copy(top_atf[:, :, :], top_at[:, :, :]),
                       lambda: dve.tensor_tensor(pair[:, :, :].rearrange("p h (a b) -> p h a b", b=TOPK),
                                                 top4[:, 0, :, :].unsqueeze(3).broadcast_to(four),
                                                 top4[:, 1, :, :].unsqueeze(2).broadcast_to(four), ALU.add)]
                out += top16(pair, best, best_at, PHEADS)
                flat = best_at[:, :, :].rearrange("p h k -> p (h k)")
                out += [lambda: dve.tensor_scalar(rank[:, 0, :], flat, 4, None, ALU.logical_shift_right),
                        lambda: dve.tensor_scalar(rank[:, 1, :], flat, TOPK - 1, None, ALU.bitwise_and),
                        lambda: dve.tensor_copy(rankf[:, :, :], rank[:, :, :])]
                for s in range(2):
                    mine = rankf[:, s, :].rearrange("p (h k) -> p h k", h=PHEADS).unsqueeze(3).broadcast_to(four)
                    out += [lambda mine=mine: dve.tensor_tensor(hit[:, :, :, :], mine,
                                                                rank16[:, :].unsqueeze(1).unsqueeze(1).broadcast_to(four), ALU.is_equal),
                            lambda s=s: dve.tensor_tensor(hit[:, :, :, :], hit[:, :, :, :],
                                                          at4[:, s, :, :].unsqueeze(2).broadcast_to(four), ALU.mult),
                            lambda s=s: dve.tensor_reduce(picks[:, s, :].rearrange("p (h k) -> p h k", h=PHEADS), hit[:, :, :, :], AX_X, ALU.add)]
                return out

            def after_exp():
                wide = [P, PHEADS, TOPK]
                return [lambda: dve.tensor_reduce(total[:, 0, :], best[:, :, :], AX_X, ALU.add),
                        lambda: dve.reciprocal(total[:, 1, :], total[:, 0, :]),
                        lambda: dve.tensor_tensor(gate, best[:, :, :], total[:, 1, :].unsqueeze(2).broadcast_to(wide), ALU.mult)]

            first = top16(score, top, top_at, HP)
            second = after_keys()
            STEPS = len(first) + len(second) + 1 + 3
            dve.wait_ge(const_here, 32)
            dve.sem_inc(moved, 1)
            with dve.Fori(0, TILES) as i:
                n_steps[0] = 0
                dve.wait_ge(score_ready, i + 1)
                dve.sem_inc(c.held, 1)
                steps(i, first)
                steps(i, second)
                steps(i, [lambda: dve.tensor_tensor(gate, best[:, :, :], best[:, :, 0:1].broadcast_to([P, PHEADS, TOPK]), ALU.subtract)])
                dve.wait_ge(found, i * STEPS + n_steps[0])
                dve.tensor_copy(best[:, :, :], gate).then_inc(shifted, 1)
                dve.wait_ge(exped, i + 1)
                steps(i, after_exp())
                dve.wait_ge(found, i * STEPS + STEPS)
                dve.sem_inc(picked, 1)
                dve.wait_ge(turned, i + 1)
                dve.sem_inc(c.held, 1)
                dve.tensor_copy(c.picks_t[:, :, bass.ds(i * P, P)], c.bank[:, 4, 0:3 * P].rearrange("p (a t) -> p a t", a=3)).then_inc(moved, 1)

        @block.tensor
        def _(pe):
            pe.wait_ge(const_here, 32)
            with pe.Fori(0, TILES) as i:
                pe.wait_ge(query_ready, i + 2)
                for h in range(PHEADS):
                    for s in range(2):
                        rows = slice(64 * s, 64 * s + 64)
                        n = PHEADS * s + h
                        last = pe.matmul(c.bank[:, n // 4, n % 4 * P:(n % 4 + 1) * P], query[rows, h, :], keys[rows, h, :],
                                         start=True, stop=True)
                last.then_inc(scored, 1)
                pe.wait_ge(picked, i + 1)
                for n in range(3):
                    last = pe.transpose(c.bank[:, 4, n * P:(n + 1) * P], picks[:, n, :], c.ident[:, :])
                last.then_inc(turned, 1)


GROUP = 64
GROUPS = TOKENS // GROUP
QUAD = 4


def gate_arrays(nc, c):
    ctx, sb, sem = stage(nc)
    QUADS = GROUP // QUAD
    with ctx:
        number = sb("ga_number", [P, N_KEYS])
        second = sb("ga_second", [P, 2, QUAD, N_KEYS])
        first = sb("ga_first", [P, 2, QUAD, N_KEYS])
        out = sb("ga_out", [P, 2, N_KEYS, GROUP])
        number_here, rows_ready, summed, moved = sem("ga_number_here"), sem("ga_rows_ready"), sem("ga_summed"), sem("ga_moved")
        stored, slot_free = [sem(f"ga_stored{s}") for s in range(2)], sem("ga_slot_free")
        block = ctx.enter_context(nc.Block())

        @block.sync
        def _(sp):
            sp.dma_start(number[:, :], c.d.number).then_inc(number_here, 16)

            def store(g, s, uses):
                sp.wait_ge(moved, g * QUADS + (QUADS + 2))
                sp.sem_inc(c.held, 1)
                sp.dma_start(c.d.gates[bass.ds(g, 1)].rearrange("a j i t -> (a j) i t"), out[:, s, :, :]).then_inc(stored[s], 16)
                sp.wait_ge(stored[s], uses)
                sp.sem_inc(slot_free, 1)

            with sp.Fori(0, GROUPS // 2) as i:
                for s in range(2):
                    store(i * 2 + s, s, i * 16 + 16)
            if GROUPS % 2:
                sp.wait_ge(moved, GROUPS * QUADS + 2)
                sp.dma_start(c.d.gates[GROUPS - 1], out[:, 0, :, :]).then_inc(stored[0], 16)
                sp.wait_ge(stored[0], 16 * (GROUPS // 2) + 16)

        @block.vector
        def _(dve):
            dve.wait_ge(number_here, 16)
            with dve.Fori(0, TOKENS // (2 * QUAD)) as i:
                for s in range(2):
                    for n in range(QUAD):
                        t = i * 2 * QUAD + (s * QUAD + n)
                        if n == 0:
                            dve.wait_ge(summed, i * 2 + (s + 1))
                            dve.sem_inc(c.held, 1)
                        dve.tensor_scalar(second[:, s, n, :], number[:, :], c.picks_t[:, 1, bass.ds(t, 1)], None, ALU.is_equal)
                        last = dve.tensor_scalar(first[:, s, n, :], number[:, :], c.picks_t[:, 0, bass.ds(t, 1)],
                                                 c.picks_t[:, 2, bass.ds(t, 1)], ALU.is_equal, ALU.mult)
                    last.then_inc(rows_ready, 1)

        @block.tensor
        def _(pe):
            pe.wait_ge(number_here, 16)
            pe.sem_inc(summed, 2)
            with pe.Fori(0, TOKENS // (2 * QUAD)) as i:
                for s in range(2):
                    pe.wait_ge(rows_ready, i * 2 + (s + 1))
                    pe.wait_ge(moved, i * 2 + (s + 1))
                    for n in range(QUAD):
                        last = pe.matmul(c.bank[:, s, n * P:(n + 1) * P], second[:, s, n, :], first[:, s, n, :], start=True, stop=True)
                    last.then_inc(summed, 1)

        @block.scalar
        def _(act):
            act.sem_inc(moved, 2)
            act.sem_inc(slot_free, 2)

            def group(i, s, count):
                act.wait_ge(slot_free, i * 2 + (s + 1))
                for q in range(count):
                    base = (i * 2 + s) * QUADS
                    act.wait_ge(summed, base + (q + 1 + 2))
                    b = q % 2
                    act.activation(out[:, s, :, q * QUAD:(q + 1) * QUAD],
                                   c.bank[:, b, :].rearrange("p (t i) -> p i t", t=QUAD), ACT.Copy).then_inc(moved, 1)

            with act.Fori(0, GROUPS // 2) as i:
                for s in range(2):
                    group(i, s, QUADS)
            if GROUPS % 2:
                group(GROUPS // 2, 0, QUADS)


BLOCK = 4
BLOCKS = N_KEYS // BLOCK
HALF = TOKENS // 2


def experts(nc, c):
    ctx, sb, sem = stage(nc)
    with ctx:
        u = sb("u", [P, BLOCK, KC, P])
        v = sb("v", [P, BLOCK, D])
        gates = sb("gates", [P, GROUPS, BLOCK, GROUP])
        hot = sb("hot", [P, 2, TOKENS])
        coef = sb("coef", [P, BLOCK, TOKENS])
        u_here = [sem(f"u_here{r}") for r in range(BLOCK)]
        v_here = [sem(f"v_here{r}") for r in range(BLOCK)]
        g_here = sem("g_here")
        dotted, hot_ready, weighed = sem("dotted"), sem("hot_ready"), sem("weighed")
        mixed, added = sem("mixed"), sem("added")
        first_ready = sem("y_first")
        OUTS = KC * 2
        block = ctx.enter_context(nc.Block())

        @block.sync
        def _(sp):
            with sp.Fori(0, BLOCKS) as b:
                for r in range(BLOCK):
                    sp.wait_ge(dotted, b * (2 * BLOCK) + 2 * (r + 1))
                    sp.sem_inc(c.held, 1)
                    sp.dma_start(u[:, r], c.d.u_t[bass.ds(b * BLOCK + r, 1)].rearrange("a p k e -> (a p) k e")).then_inc(u_here[r], 16)
                sp.wait_ge(mixed, b * OUTS + 1)
                for r in range(BLOCK):
                    sp.sem_inc(c.held, 1)
                    sp.dma_start(v[:, r], c.d.v[bass.ds(b * BLOCK * P + r * P, P), :]).then_inc(v_here[r], 16)

        @block.gpsimd
        def _(pool):
            with pool.Fori(0, BLOCKS) as b:
                pool.wait_ge(weighed, b * BLOCK + 2)
                pool.sem_inc(c.held, 1)
                for g in range(GROUPS):
                    pool.dma_start(gates[:, g], c.d.gates[g, :, bass.ds(b * BLOCK, BLOCK), :]).then_inc(g_here, 16)

        @block.scalar
        def _(act):
            with act.Fori(0, BLOCKS) as b:
                for r in range(BLOCK):
                    act.wait_ge(weighed, b * BLOCK + (r + 1))
                    for n in range(2):
                        act.wait_ge(dotted, b * (2 * BLOCK) + (2 * BLOCK + 2 * r + n + 1))
                        act.activation(hot[:, r % 2, n * HALF:(n + 1) * HALF], c.bank[:, 2 * (r % 2) + n, 0:HALF], ACT.Gelu).then_inc(hot_ready, 1)
                    act.wait_ge(hot_ready, b * (2 * BLOCK) + 2 * (r + 1) + 4)

        @block.vector
        def _(dve):
            dve.memset(c.y_t[:, :, :], 0.0).then_inc(first_ready, 1)
            dve.wait_ge(first_ready, 1)
            dve.sem_inc(weighed, 2)
            dve.sem_inc(added, 4)
            with dve.Fori(0, BLOCKS) as b:
                dve.wait_ge(g_here, b * (16 * GROUPS) + 16 * GROUPS)
                for r in range(BLOCK):
                    dve.wait_ge(hot_ready, b * (2 * BLOCK) + 2 * (r + 1) + 4)
                    dve.tensor_tensor(coef[:, r, :].rearrange("p (g t) -> p g t", t=GROUP),
                                      hot[:, r % 2, :].rearrange("p (g t) -> p g t", t=GROUP), gates[:, :, r, :],
                                      ALU.mult).then_inc(weighed, 1)
                for m in range(OUTS):
                    k, n = m // 2, m % 2
                    dve.wait_ge(mixed, b * OUTS + (m + 2))
                    y = c.y_t[:, k, n * HALF:(n + 1) * HALF]
                    dve.tensor_tensor(y, y, c.bank[:, 4 + m % 4, 0:HALF], ALU.add).then_inc(added, 1)

        @block.tensor
        def _(pe):
            pe.sem_inc(dotted, 2 * BLOCK)
            pe.sem_inc(mixed, 1)
            pe.sem_inc(hot_ready, 4)
            with pe.Fori(0, BLOCKS) as b:
                for r in range(BLOCK):
                    pe.wait_ge(u_here[r], b * 16 + 16)
                    for n in range(2):
                        pe.wait_ge(hot_ready, b * (2 * BLOCK) + (2 * r + n + 1))
                        for k in range(KC):
                            last = pe.matmul(c.bank[:, 2 * (r % 2) + n, 0:HALF], u[:, r, k, :], c.act_t[:, k, n * HALF:(n + 1) * HALF],
                                             start=(k == 0), stop=(k == KC - 1))
                        last.then_inc(dotted, 1)
                for r in range(BLOCK):
                    pe.wait_ge(v_here[r], b * 16 + 16)
                pe.wait_ge(weighed, b * BLOCK + (BLOCK + 2))
                for m in range(OUTS):
                    k, n = m // 2, m % 2
                    pe.wait_ge(added, b * OUTS + (m + 1))
                    for r in range(BLOCK):
                        last = pe.matmul(c.bank[:, 4 + m % 4, 0:HALF], v[:, r, k * P:(k + 1) * P], coef[:, r, n * HALF:(n + 1) * HALF],
                                         start=(r == 0), stop=(r == BLOCK - 1))
                    last.then_inc(mixed, 1)


def finish(nc, c):
    ctx, sb, sem = stage(nc)
    with ctx:
        y_part = sb("fi_y", [P, KC, P])
        h = sb("fi_h", [P, D])
        square = sb("fi_square", [P, D])
        out = sb("fi_out", [P, D])
        gain = sb("fi_gain", [P, D])
        stat = sb("fi_stat", [P, 4])
        gain_here, h_here, y_ready, turned, added = (sem("fi_" + s) for s in ("gain_here", "h_here", "y_ready", "turned", "added"))
        summed, meaned, rooted, inverted, scaled, stored, out_free = (
            sem("fi_" + s) for s in ("summed", "meaned", "rooted", "inverted", "scaled", "stored", "out_free"))
        block = ctx.enter_context(nc.Block())

        @block.sync
        def _(sp):
            sp.dma_start(gain[:, :], c.d.g_final).then_inc(gain_here, 16)
            with sp.Fori(0, TILES) as i:
                sp.wait_ge(scaled, i + 1)
                sp.sem_inc(c.held, 1)
                sp.dma_start(h[:, :], c.d.h[bass.ds(i * P, P), :]).then_inc(h_here, 16)
                sp.wait_ge(scaled, i + 2)
                sp.sem_inc(c.held, 1)
                sp.dma_start(c.d.y[bass.ds(i * P, P), :], out[:, :]).then_inc(stored, 16)
                sp.wait_ge(stored, i * 16 + 16)
                sp.sem_inc(out_free, 1)

        @block.scalar
        def _(act):
            with act.Fori(0, TILES) as i:
                act.wait_ge(turned, i * 4 + 4)
                act.sem_inc(c.held, 1)
                act.activation(y_part[:, :, :], c.y_t[:, :, bass.ds(i * P, P)], ACT.Copy).then_inc(y_ready, 1)
                act.wait_ge(added, i * 4 + 8)
                act.activation(square[:, :], h[:, :], ACT.Square, accum_out=stat[:, 0:1]).then_inc(summed, 1)
                act.wait_ge(meaned, i + 1)
                act.activation(stat[:, 2:3], stat[:, 1:2], ACT.Sqrt).then_inc(rooted, 1)

        @block.vector
        def _(dve):
            dve.sem_inc(scaled, 1)
            dve.sem_inc(added, 4)
            dve.sem_inc(out_free, 1)
            dve.wait_ge(gain_here, 16)
            dve.sem_inc(c.held, 1)
            with dve.Fori(0, TILES) as i:
                dve.wait_ge(h_here, i * 16 + 16)
                for k in range(4):
                    dve.wait_ge(turned, i * 4 + (4 + k + 1))
                    dve.tensor_tensor(h[:, k * NW:(k + 1) * NW], h[:, k * NW:(k + 1) * NW], c.bank[:, k, :], ALU.add).then_inc(added, 1)
                dve.wait_ge(summed, i + 1)
                dve.tensor_scalar(stat[:, 1:2], stat[:, 0:1], 1.0 / D, EPS, ALU.mult, ALU.add).then_inc(meaned, 1)
                dve.wait_ge(rooted, i + 1)
                dve.reciprocal(stat[:, 3:4], stat[:, 2:3]).then_inc(inverted, 1)
                dve.wait_ge(inverted, i + 1)
                dve.wait_ge(out_free, i + 1)
                dve.scalar_tensor_tensor(out=out[:, :], in0=h[:, :], scalar=stat[:, 3:4], in1=gain[:, :],
                                         op0=ALU.mult, op1=ALU.mult).then_inc(scaled, 1)

        @block.tensor
        def _(pe):
            pe.sem_inc(turned, 4)
            with pe.Fori(0, TILES) as i:
                pe.wait_ge(y_ready, i + 1)
                for k in range(4):
                    pe.wait_ge(added, i * 4 + (k + 1))
                    for j in range(4):
                        last = pe.transpose(c.bank[:, k, j * P:(j + 1) * P], y_part[:, 4 * k + j, :], c.ident[:, :])
                    last.then_inc(turned, 1)


def build(nc, d):
    c = Chip()
    c.d = d
    with ExitStack() as ctx:
        c.bank = ctx.enter_context(nc.psum_tensor("bank", [P, 8, 512], F32))
        c.act_t = ctx.enter_context(nc.sbuf_tensor("act_t", [P, KC, ROWS], F32))
        c.ident = ctx.enter_context(nc.sbuf_tensor("ident", [P, P], F32))
        c.g_attn = ctx.enter_context(nc.sbuf_tensor("g_attn", [P, KC], F32))
        c.g_ffn = ctx.enter_context(nc.sbuf_tensor("g_ffn", [P, KC], F32))
        c.held = ctx.enter_context(nc.semaphore("held"))
        load_constants(nc, c)
        norm_transpose(nc, c, "norm1", d.x, c.g_attn)
        project(nc, c, "proj", d.w_in, 8, d.w_in_tail, d.proj)
        attend(nc, c, "prompt")
        attend(nc, c, "sample")
        project(nc, c, "merge", d.w_out, 4, None, d.h, residual=d.x)
        norm_transpose(nc, c, "norm2", d.h, c.g_ffn)
        with ExitStack() as routing:
            c.picks_t = routing.enter_context(nc.sbuf_tensor("picks_t", [P, 3, ROWS], F32))
            with nc.sbuf_tensor("query_t", [P, PHEADS, ROWS], F32) as c.query_t:
                expert_queries(nc, c)
                route(nc, c)
            gate_arrays(nc, c)
        c.y_t = ctx.enter_context(nc.sbuf_tensor("y_t", [P, KC, ROWS], F32))
        experts(nc, c)
        finish(nc, c)



def _chunk_arrays(T, CL):
    import numpy as np
    s, t = np.arange(T)[:, None], np.arange(T)[None, :]
    same = s // CL == t // CL
    one = lambda m: np.ascontiguousarray(m.astype(np.float32))
    inside = one(same & (s <= t))
    own = one(s // CL == np.arange(T // CL)[None, :])
    return inside / np.float32(TAU), one(same & (s > t)) / np.float32(TAU), own / np.float32(TAU), inside, own


def _trig():
    import math
    import numpy as np
    half = HD // 2
    inv = np.exp(np.float32(-math.log(10000.0)) * np.arange(half, dtype=np.float32) * np.float32(2.0 / HD)).astype(np.float32)
    pos = np.concatenate([np.arange(SEQ), 1024 + np.arange(SAMPLES) % DEC_SEQ]).astype(np.float32)
    ang = (pos[:, None] * inv[None, :]).astype(np.float32)
    out = np.zeros((ROWS, HD), np.float32)
    out[:TOKENS] = np.concatenate([np.cos(ang), np.sin(ang)], axis=1)
    return out


def _masks():
    import numpy as np
    masked = np.float32(-1e30)
    q, s = np.arange(P)[:, None], np.arange(2 * WINDOW)[None, :]
    later = np.where((s > q) & (s <= q + WINDOW), np.float32(0), masked)
    first = np.where(s >= WINDOW, later, masked)
    t, j = np.arange(P)[:, None] % DEC_SEQ, np.arange(DEC_SEQ + WINDOW)[None, :]
    sample = np.where((j > t) & (j <= t + WINDOW), np.float32(0), masked)
    return first.astype(np.float32), later.astype(np.float32), sample.astype(np.float32)


def kernel(**inputs):
    import types
    import numpy as np
    import concourse.bacc as bacc
    from concourse.bass_utils import run_bass_kernel_spmd

    a = {k: np.asarray(x) for k, x in inputs.items()}
    put = np.ascontiguousarray
    x = np.zeros((ROWS, D), np.float32)
    x[:SEQ] = a["x_prompt"].reshape(SEQ, D)
    x[SEQ:TOKENS] = a["x_sample"].reshape(SAMPLES, D)
    w = a["w_in"][0]
    ga = 2 * GLA_HEADS * DK + 2 * GLA_HEADS * DV
    w = np.concatenate([w[:, :ga], w[:, ga + GATE_RANK:], w[:, ga:ga + GATE_RANK]], axis=1)

    def slices(m, n):
        return put(m.reshape(KC, P, m.shape[1] // n, n).transpose(2, 1, 0, 3))

    def rows(v):
        return put(np.broadcast_to(v.reshape(1, -1), (P, v.size)))

    tri_p, suf_p, ind_p, inside_p, _ = _chunk_arrays(P, GLA_CHUNK)
    tri_s, suf_s, ind_s, inside_s, own = _chunk_arrays(SAMPLES, DEC_SEQ)
    first, later, sample = _masks()
    sinks = a["attn_sinks"][0]
    by_row = sinks.reshape(KV, PAIRS // KV, 2).transpose(0, 2, 1).reshape(-1)
    arrays = {
        "x": x,
        "w_in": slices(w[:, :8 * NW], NW),
        "w_in_tail": slices(w[:, 8 * NW:], PROJ - 8 * NW)[0],
        "w_out": slices(a["w_out"][0], NW),
        "w_peer_q": slices(a["w_peer_q"][0], P),
        "g_attn": put(a["g_attn"][0].reshape(KC, P).T), "g_ffn": put(a["g_ffn"][0].reshape(KC, P).T),
        "g_out": rows(a["g_gla_out"][0]), "g_final": rows(a["g_final"]),
        "gate_w": np.concatenate([a["w_gate_up"][0], a["b_gate"]], axis=0),
        "sinks_prompt": rows(sinks), "sinks_sample": put(np.repeat(by_row, DEC_SEQ).reshape(P, 1)),
        "cache_k": a["cache_win_k"][0].reshape(DEC_BATCH, WINDOW, KV * HD),
        "cache_v": a["cache_win_v"][0].reshape(DEC_BATCH, WINDOW, KV * HD),
        "state_in": a["state_gla"][0],
        "sub_keys": put(a["peer_sub_keys"][0].transpose(1, 3, 0, 2).reshape(P, PHEADS, N_KEYS)),
        "u_t": put(a["peer_u"][0].reshape(N_KEYS, P, KC, P).transpose(0, 3, 2, 1)),
        "v": a["peer_v"][0],
        "ident": np.eye(P, dtype=np.float32), "trig": _trig(),
        "tri_prompt": tri_p, "suf_prompt": suf_p, "ind_prompt": ind_p, "inside_prompt": inside_p,
        "tri_sample": tri_s, "suf_sample": suf_s, "ind_sample": ind_s, "inside_sample": inside_s, "own": own,
        "mask_prompt": first, "mask_later": later, "mask_sample": sample,
        "rank16": rows(np.arange(TOPK, dtype=np.float32)), "number": rows(np.arange(N_KEYS, dtype=np.float32)),
    }
    arrays = {k: put(v) for k, v in arrays.items()}
    outs = {
        "y": (ROWS, D),
        "state_out_prompt": (GLA_HEADS, DK, DV), "k_out_prompt": (WINDOW, KV * HD), "v_out_prompt": (WINDOW, KV * HD),
        "state_out_sample": (DEC_BATCH, GLA_HEADS, DK, DV),
        "k_out_sample": (DEC_BATCH, WINDOW, KV * HD), "v_out_sample": (DEC_BATCH, WINDOW, KV * HD),
    }
    scratch = {"proj": (ROWS, PROJ), "h": (ROWS, D), "gates": (GROUPS, N_KEYS, N_KEYS, GROUP)}

    nc = bacc.Bacc("TRN2", target_bir_lowering=False, num_devices=1)
    d = types.SimpleNamespace()
    for k, v in arrays.items():
        vars(d)[k] = nc.dram_tensor("in_" + k, v.shape, mybir.dt.from_np(v.dtype), kind="ExternalInput").ap()
    for k, shape in outs.items():
        vars(d)[k] = nc.dram_tensor("out_" + k, shape, F32, kind="ExternalOutput").ap()
    for k, shape in scratch.items():
        vars(d)[k] = nc.dram_tensor(k + "_scratch", shape, F32, kind="Internal").ap()
    d.tri = {"prompt": d.tri_prompt, "sample": d.tri_sample}
    d.suf = {"prompt": d.suf_prompt, "sample": d.suf_sample}
    d.ind = {"prompt": d.ind_prompt, "sample": d.ind_sample}
    d.inside = {"prompt": d.inside_prompt, "sample": d.inside_sample}
    d.sinks = {"prompt": d.sinks_prompt, "sample": d.sinks_sample}
    d.mask = {"prompt": d.mask_prompt, "later": d.mask_later, "sample": d.mask_sample}
    build(nc, d)
    r = run_bass_kernel_spmd(nc, [{"in_" + k: v for k, v in arrays.items()}], core_ids=[0]).results[0]
    y = r["out_y"]
    return (y[:SEQ].reshape(1, SEQ, D), y[SEQ:TOKENS].reshape(DEC_BATCH, DEC_SEQ, D),
            r["out_state_out_prompt"].reshape(1, 1, GLA_HEADS, DK, DV),
            r["out_k_out_prompt"].reshape(1, 1, WINDOW, KV, HD), r["out_v_out_prompt"].reshape(1, 1, WINDOW, KV, HD),
            r["out_state_out_sample"].reshape(1, DEC_BATCH, GLA_HEADS, DK, DV),
            r["out_k_out_sample"].reshape(1, DEC_BATCH, WINDOW, KV, HD),
            r["out_v_out_sample"].reshape(1, DEC_BATCH, WINDOW, KV, HD))
```

```python
from contextlib import ExitStack

import concourse.bass as bass
from concourse import mybir

ALU = mybir.AluOpType
ACT = mybir.ActivationFunctionType
AX_X = mybir.AxisListType.X
F32 = mybir.dt.float32
F32R = mybir.dt.float32r
U32 = mybir.dt.uint32

P = 128
D = 2048
KC = D // P
SEQ = 512
DEC_BATCH, DEC_SEQ = 8, 8
SAMPLES = DEC_BATCH * DEC_SEQ
TOKENS = SEQ + SAMPLES
PROMPT_TILES = SEQ // P
TILES = 5
STRIDE = (TOKENS - P) // (TILES - 1)
NW = 256
HI, LO = 0, 1
PASSES = ((HI, HI), (HI, LO), (LO, HI))

GLA_HEADS, DK, DV = 4, 128, 256
GATE_RANK = 16
TAU = 16.0
GLA_CHUNK = 64
SWA_HEADS, HD, KV = 16, 64, 2
PAIRS = SWA_HEADS // 2
WINDOW = 128
EPS = 1e-6

Q0 = 0
K0 = Q0 + GLA_HEADS * DK
V0 = K0 + GLA_HEADS * DK
R0 = V0 + GLA_HEADS * DV
SQ0 = R0 + GLA_HEADS * DV
SK0 = SQ0 + SWA_HEADS * HD
SV0 = SK0 + KV * HD
GA0 = SV0 + KV * HD
PROJ = GA0 + GATE_RANK

N_KEYS = 128
PHEADS = 8
TOPK = 16
SEL = PHEADS * TOPK
NEG = -3.0e38


class Chip:
    pass


def stage(nc):
    ctx = ExitStack()
    sems = []

    def clear():
        nc.clear_and_free_semaphores(sems)
        nc.all_engine_barrier()

    ctx.callback(clear)

    def sb(name, shape, dt=F32):
        return ctx.enter_context(nc.sbuf_tensor(name, shape, dt))

    def sem(name):
        sems.append(nc.alloc_semaphore(name))
        return sems[-1]

    return ctx, sb, sem


def load_constants(nc, c):
    ctx, sb, sem = stage(nc)
    with ctx:
        loaded = sem("const_loaded")
        block = ctx.enter_context(nc.Block())

        @block.sync
        def _(sp):
            pairs = [(c.ident, c.d.ident), (c.g_attn, c.d.g_attn), (c.g_ffn, c.d.g_ffn)]
            for dst, src in pairs:
                sp.dma_start(dst[:], src).then_inc(loaded, 16)
            sp.wait_ge(loaded, 16 * len(pairs))


def product(pe, out, stationary, moving):
    for k in range(KC):
        for n, (a, b) in enumerate(PASSES):
            last = pe.matmul(out, stationary(a, k), moving(b, k), start=(k == 0 and n == 0),
                             stop=(k == KC - 1 and n == len(PASSES) - 1))
    return last


def norm_transpose(nc, c, name, src, gain):
    ctx, sb, sem = stage(nc)
    with ctx:
        rows = sb(name + "_rows", [P, D])
        square = sb(name + "_square", [P, D])
        scaled = sb(name + "_scaled", [P, D])
        gained = sb(name + "_gained", [P, KC, P])
        stat = sb(name + "_stat", [P, 4])
        loaded, rows_free = sem(name + "_loaded"), sem(name + "_rows_free")
        summed, meaned, rooted, inverted = (sem(name + "_" + s) for s in ("summed", "meaned", "rooted", "inverted"))
        scaled_ready, turned, moved, rounded, split = (
            sem(name + "_" + s) for s in ("scaled_ready", "turned", "moved", "rounded", "split"))
        block = ctx.enter_context(nc.Block())

        @block.sync
        def _(sp):
            with sp.Fori(0, TILES) as i:
                sp.wait_ge(rows_free, i + 1)
                sp.sem_inc(c.held, 1)
                sp.dma_start(rows[:, :], src[bass.ds(i * STRIDE, P), :]).then_inc(loaded, 16)

        @block.scalar
        def _(act):
            with act.Fori(0, TILES) as i:
                act.wait_ge(loaded, i * 16 + 16)
                act.activation(square[:, :], rows[:, :], ACT.Square, accum_out=stat[:, 0:1]).then_inc(summed, 1)
                act.wait_ge(meaned, i + 1)
                act.activation(stat[:, 2:3], stat[:, 1:2], ACT.Sqrt).then_inc(rooted, 1)
                for k in range(4):
                    act.wait_ge(moved, i * 4 + (k + 5))
                    act.wait_ge(split, i * 4 + (k + 1))
                    act.sem_inc(c.held, 1)
                    act.activation(c.act[HI][:, 4 * k:4 * k + 4, bass.ds(i * STRIDE, P)], gained[:, 4 * k:4 * k + 4, :],
                                   ACT.Copy).then_inc(rounded, 1)

        @block.vector
        def _(dve):
            dve.sem_inc(rows_free, 1)
            dve.sem_inc(moved, 4)
            dve.sem_inc(split, 4)
            with dve.Fori(0, TILES) as i:
                dve.wait_ge(summed, i + 1)
                dve.tensor_scalar(stat[:, 1:2], stat[:, 0:1], 1.0 / D, EPS, ALU.mult, ALU.add).then_inc(meaned, 1)
                dve.wait_ge(rooted, i + 1)
                dve.reciprocal(stat[:, 3:4], stat[:, 2:3]).then_inc(inverted, 1)
                dve.wait_ge(inverted, i + 1)
                dve.tensor_scalar(scaled[:, :], rows[:, :], stat[:, 3:4], None, ALU.mult).then_inc(scaled_ready, 1)
                dve.wait_ge(scaled_ready, i + 1)
                dve.sem_inc(rows_free, 1)
                for k in range(4):
                    dve.wait_ge(turned, i * 4 + (k + 1))
                    dve.tensor_tensor(gained[:, 4 * k:4 * k + 4, :], c.bank[:, k, :].rearrange("p (k t) -> p k t", k=4),
                                      gain[:, 4 * k:4 * k + 4].unsqueeze(2).broadcast_to([P, 4, P]),
                                      ALU.mult).then_inc(moved, 1)
                for k in range(4):
                    dve.wait_ge(rounded, i * 4 + (k + 1))
                    at = (slice(None), slice(4 * k, 4 * k + 4), bass.ds(i * STRIDE, P))
                    dve.tensor_tensor(c.act[LO][at], gained[:, 4 * k:4 * k + 4, :], c.act[HI][at].bitcast(F32),
                                      ALU.subtract).then_inc(split, 1)

        @block.tensor
        def _(pe):
            with pe.Fori(0, TILES) as i:
                pe.wait_ge(scaled_ready, i + 1)
                for k in range(4):
                    pe.wait_ge(moved, i * 4 + (k + 1))
                    for j in range(4):
                        s = 4 * k + j
                        last = pe.transpose(c.bank[:, k, j * P:(j + 1) * P], scaled[:, s * P:(s + 1) * P], c.ident[:, :])
                    last.then_inc(turned, 1)


def project(nc, c, name, weights, chunks, tail, dst, residual=None):
    ctx, sb, sem = stage(nc)
    with ctx:
        width = tail.shape[2] if tail is not None else NW
        wide = max(NW, width)
        raw = sb(name + "_raw", [P, 2, KC, wide])
        w = [sb(name + part, [P, 2, KC, wide], F32R) for part in ("_hi", "_lo")]
        out = sb(name + "_out", [P, TILES, wide])
        res = sb(name + "_res", [P, TILES, NW]) if residual is not None else None
        raw_here = [sem(f"{name}_raw_here{s}") for s in range(2)]
        out_free, rounded, split = sem(name + "_out_free"), sem(name + "_rounded"), sem(name + "_split")
        res_here, stored = [[sem(f"{name}_{x}{t}") for t in range(TILES)] for x in ("res_here", "stored")]
        summed, moved = sem(name + "_summed"), sem(name + "_moved")
        block = ctx.enter_context(nc.Block())

        def slices(eng, step):
            with eng.Fori(0, chunks // 2) as i:
                for s in range(2):
                    step(i * 2 + s, s, i + 1, NW)
            if tail is not None:
                step(chunks, 0, chunks // 2 + 1, width)

        @block.sync
        def _(sp):
            def load(n, s, uses, cols):
                sp.wait_ge(split, n + 1)
                sp.sem_inc(c.held, 1)
                src = weights[bass.ds(n, 1)].rearrange("a p k n -> (a p) k n") if cols == NW or tail is None else tail
                sp.dma_start(raw[:, s, :, 0:cols], src).then_inc(raw_here[s], 16)

            slices(sp, load)

        @block.gpsimd
        def _(pool):
            def store(n, s, uses, cols):
                for t in range(TILES):
                    rows = P if t == TILES - 1 else STRIDE
                    pool.wait_ge(moved, n * TILES + (TILES + t + 1))
                    pool.sem_inc(c.held, 1)
                    to = bass.ds(n * NW, cols) if not isinstance(n, int) else slice(n * NW, n * NW + cols)
                    pool.dma_start(dst[t * STRIDE:t * STRIDE + rows, to], out[0:rows, t, 0:cols]).then_inc(stored[t], 16)
                for t in range(TILES):
                    pool.wait_ge(stored[t], n * 16 + 16)
                pool.sem_inc(out_free, 1)

            slices(pool, store)

        @block.scalar
        def _(act):
            def hi(n, s, uses, cols):
                act.wait_ge(raw_here[s], uses * 16)
                act.wait_ge(summed, n * TILES + TILES)
                act.activation(w[HI][:, s, :, 0:cols], raw[:, s, :, 0:cols], ACT.Copy).then_inc(rounded, 1)
                if residual is not None:
                    act.wait_ge(out_free, n + 1)
                    act.sem_inc(c.held, 1)
                    for t in range(TILES):
                        act.dma_start(res[:, t, :], residual[t * STRIDE:t * STRIDE + P, bass.ds(n * NW, NW)]).then_inc(res_here[t], 16)

            slices(act, hi)

        @block.vector
        def _(dve):
            dve.sem_inc(split, 2)
            dve.sem_inc(moved, TILES)
            dve.sem_inc(out_free, 1)

            def lo(n, s, cols):
                dve.wait_ge(rounded, n + 1)
                dve.tensor_tensor(w[LO][:, s, :, 0:cols], raw[:, s, :, 0:cols], w[HI][:, s, :, 0:cols].bitcast(F32),
                                  ALU.subtract).then_inc(split, 1)

            def move(n, s, uses, cols):
                lo(n, s, cols)
                dve.wait_ge(out_free, n + 1)
                for t in range(TILES):
                    dve.wait_ge(summed, n * TILES + (2 * TILES + t + 1))
                    if residual is None:
                        dve.tensor_copy(out[:, t, 0:cols], c.bank[:, t, 0:cols]).then_inc(moved, 1)
                    else:
                        dve.wait_ge(res_here[t], n * 16 + 16)
                        dve.tensor_tensor(out[:, t, 0:cols], c.bank[:, t, 0:cols], res[:, t, 0:cols], ALU.add).then_inc(moved, 1)

            slices(dve, move)

        @block.tensor
        def _(pe):
            pe.sem_inc(summed, 2 * TILES)

            def products(n, s, uses, cols):
                pe.wait_ge(split, n + 3)
                for t in range(TILES):
                    pe.wait_ge(moved, n * TILES + (t + 1))
                    product(pe, c.bank[:, t, 0:cols], lambda part, k: c.act[part][:, k, t * STRIDE:t * STRIDE + P],
                            lambda part, k: w[part][:, s, k, 0:cols]).then_inc(summed, 1)

            slices(pe, products)


def attend(nc, c, kind):
    prompt = kind == "prompt"
    turns = PROMPT_TILES if prompt else 1
    T = P if prompt else SAMPLES
    CL = GLA_CHUNK if prompt else DEC_SEQ
    NC = T // CL
    NB = SWA_HEADS if prompt else DEC_BATCH
    KW = 2 * WINDOW if prompt else DEC_SEQ + WINDOW
    ctx, sb_, sem_ = stage(nc)
    per = {}

    def sb(name, shape, dt=F32):
        return sb_(kind + "_" + name, shape, dt)

    def sem(name, n=1):
        s = sem_(kind + "_" + name)
        per[id(s)] = n
        return s

    with ctx:
        cur = sb("cur", [P, PROJ])
        tri = sb("tri", [T, T])
        suf = sb("suf", [T, T])
        ind = sb("ind", [T, NC])
        inside = sb("inside", [T, T])
        gate_w = sb("gate_w", [GATE_RANK + 1, GLA_HEADS * DK])
        ga_t = sb("ga_t", [GATE_RANK + 1, T])
        low = sb("low", [T, 512])
        mag = sb("mag", [T, 512])
        log_a = sb("log_a", [T, 512])
        eb = sb("eb", [T, 512])
        enb = sb("enb", [T, 512])
        ebd = sb("ebd", [T, 512])
        qg, kg, ke = eb, enb, ebd
        decay = sb("decay", [P, GLA_HEADS, NC])
        qg_t = sb("qg_t", [P, GLA_HEADS, T])
        kg_t = sb("kg_t", [P, GLA_HEADS, T])
        q_spread = sb("q_spread", [P, GLA_HEADS, NC * (T + CL)])
        inner = sb("inner", [T, GLA_HEADS, T])
        o_stat = sb("o_stat", [T, 4, GLA_HEADS])
        o_norm = sb("o_norm", [T, GLA_HEADS * DV])
        g_out = sb("g_out", [P, DV])
        er = sb("er", [T, GLA_HEADS * DV])
        silu, log1, o_junk = er, mag, low[:, 0:DV]
        state = sb("state", [P, 2 if prompt else NC, GLA_HEADS, DV])
        if not prompt:
            own = sb("own", [T, NC])
            spare = sb("spare", [P, 2 * NC * DK])
            k_own = spare[0:T, :].rearrange("t (a n d) -> t a n d", a=2, n=NC)
            probs_t = spare[:, 0:NB * P].rearrange("p (b q) -> p b q", b=NB)
            probs_old_t = spare[0:DEC_SEQ, NB * P:2 * NB * P].rearrange("p (b q) -> p b q", b=NB)
        trig = sb("trig", [P, HD])
        roped = sb("roped", [P, SWA_HEADS + KV, HD])
        rt = [sb(f"rt{n}", [P, SWA_HEADS + KV, HD // 2]) for n in range(2)]
        k_twice = sb("k_twice", [P, KV, 2, HD])
        q_t = sb("q_t", [P, PAIRS, T])
        sinks = sb("sinks", [P, NB if prompt else 1])
        mask = sb("mask", [P, KW])
        scores = sb("scores", [P, NB, KW])
        st = sb("st", [P, 6, NB])
        if prompt:
            mask_all = sb("mask_all", [P, KW])
            k_t = sb("k_t", [P, KV, KW])
            v_before = sb("v_before", [P, KV * HD])
            probs_t = sb("probs_t", [P, NB, 2, P])
        else:
            k_t = q_spread[:, :, :].rearrange("p h x -> p (h x)")[:, 0:NB * KV * KW].rearrange("p (b g k) -> p b g k", b=NB, g=KV)
            k_new = sb("k_new", [P, NB, KV * HD])
            v_new = sb("v_new", [P, NB, KV * HD])
            k_old = sb("k_old", [DEC_SEQ, NB, KV * HD])
            v_old = sb("v_old", [DEC_SEQ, NB, KV * HD])
            k2 = sb("k2", [P, 2, KV, 2, HD])
            k2_old = sb("k2_old", [DEC_SEQ, 2, KV, 2, HD])

        const_here = sem("const_here")
        cur_here, trig_here = sem("cur_here", 16), sem("trig_here", 16)
        ga_turned, ga_ready = sem("ga_turned"), sem("ga_ready")
        gate_ready, low_ready, mag_ready = sem("gate_ready"), sem("low_ready"), sem("mag_ready")
        exp1_ready, log1_ready, log_a_ready = sem("exp1_ready"), sem("log1_ready"), sem("log_a_ready")
        sums_ready, exps_ready, gated = sem("sums_ready"), sem("exps_ready", 4), sem("gated", 3)
        gated_turned, qk_ready = sem("gated_turned", 2), sem("qk_ready", 3)
        inner_ready, inner_masked = sem("inner_ready"), sem("inner_masked")
        grown, state_ready = sem("grown", 2 if prompt else GLA_HEADS), sem("state_ready", 2 if prompt else GLA_HEADS)
        k_own_ready = sem("k_own_ready", GLA_HEADS)
        o_ready, o_summed, o_meaned, o_rooted = sem("o_ready"), sem("o_summed", GLA_HEADS), sem("o_meaned"), sem("o_rooted")
        o_inverted, o_normed = sem("o_inverted"), sem("o_normed", GLA_HEADS)
        er_ready, er_one, er_inverted, silu_ready = sem("er_ready"), sem("er_one"), sem("er_inverted"), sem("silu_ready")
        o_gated, o_turned, gla_heads_ready = sem("o_gated"), sem("o_turned", 2), sem("gla_heads_ready", 2)
        gla_rounded, swa_rounded = sem("gla_rounded", 2), sem("swa_rounded", 2 if prompt else 1)
        rope_step, k_twice_ready = sem("rope_step", 6), sem("k_twice_ready")
        q_turned, q_t_ready = sem("q_turned"), sem("q_t_ready", 2 if prompt else 1)
        k_turned, k_t_ready = sem("k_turned", 1 if prompt else NB), sem("k_t_ready", 1 if prompt else NB)
        SB = 4 if prompt else 2
        scored, score_moved = sem("scored", NB // SB), sem("score_moved", NB)
        topped, negated, sunk = sem("topped"), sem("negated"), sem("sunk")
        exped, sink_exped, totalled, inverted = sem("exped", NB), sem("sink_exped"), sem("totalled"), sem("inverted")
        weighted, p_turned = sem("weighted", 2), sem("p_turned", NB // 2)
        p_ready = [sem("p_ready_even", NB // 4), sem("p_ready_odd", NB // 4)]
        mixed, swa_heads_ready = sem("mixed"), sem("swa_heads_ready", 2 if prompt else 1)
        kept, stored = sem("kept", 3), sem("stored")
        turn_over = sem("turn_over", 4)

        new_here = sem("new_here", 32 * NB)
        all_consts = 16 * (8 + (1 if prompt else 6))
        first_ready = sem("first_ready")

        k2_ready = sem("k2_ready", NB)

        block = ctx.enter_context(nc.Block())
        b0, b1, b2, b3 = (c.bank[:, n, :] for n in range(4))

        def wait(eng, s, i, n=None):
            eng.wait_ge(s, i * per[id(s)] + (per[id(s)] if n is None else n))

        def loop(eng, body):
            def turn(i):
                body(i)
                for s in ((gla_heads_ready, swa_heads_ready, kept, k_twice_ready, state_ready) if prompt else ()):
                    wait(eng, s, i)
                    eng.sem_inc(c.held, 1)

            if turns > 1:
                with eng.Fori(0, turns) as i:
                    turn(i)
            else:
                turn(0)

        def tokens(i):
            return bass.ds(i * P, P) if prompt else slice(SEQ, TOKENS)

        consts = [(tri, c.d.tri[kind]), (suf, c.d.suf[kind]), (ind, c.d.ind[kind]), (inside, c.d.inside[kind]),
                  (gate_w, c.d.gate_w), (g_out, c.d.g_out), (sinks, c.d.sinks[kind]), (mask, c.d.mask[kind])]
        if prompt:
            consts += [(mask_all, c.d.mask["later"])]
        else:
            consts += [(own, c.d.own)]
            ck, cv = c.d.cache_k, c.d.cache_v
            consts += [(state, c.d.state_in.rearrange("b h d v -> d b h v")),
                       (k_old, ck[:, 0:DEC_SEQ, :].rearrange("b t f -> t b f")),
                       (v_old, cv[:, 0:DEC_SEQ, :].rearrange("b t f -> t b f"))]

        if prompt:
            swa_out = [(slice(PAIRS + 4 * n, PAIRS + 4 * n + 4), c.bank[:, n, :].rearrange("p (k t) -> p k t", k=4)) for n in range(2)]
        else:
            swa_out = [(slice(PAIRS, 2 * PAIRS), c.bank[:, 0, :].rearrange("p (k t) -> p k t", k=PAIRS))]

        def score_bank(n):
            if prompt:
                return c.bank[:, 3 + n // 4 % 2 * 2 + n % 2, n // 2 % 2 * KW:(n // 2 % 2 + 1) * KW]
            return c.bank[:, 3 + n // 2 % 4, n % 2 * 256:n % 2 * 256 + KW]

        def move_probs(eng, i, n):
            wait(eng, p_turned, i, n + 1)
            src = c.bank[:, 3 + n % 4, :].rearrange("p (a b q) -> p a b q", a=2, b=2)
            if not prompt:
                nc.scalar.activation(probs_t[:, 2 * n:2 * n + 2, :], src[:, :, 0, :], ACT.Copy)
                nc.scalar.activation(probs_old_t[:, 2 * n:2 * n + 2, :], src[0:DEC_SEQ, :, 1, :], ACT.Copy).then_inc(p_ready[n % 2], 1)
            elif n % 2:
                nc.vector.tensor_copy(probs_t[:, 2 * n:2 * n + 2, :, :], src).then_inc(p_ready[1], 1)
            else:
                nc.scalar.activation(probs_t[:, 2 * n:2 * n + 2, :, :], src, ACT.Copy).then_inc(p_ready[0], 1)

        def new_state(dve, i, h):
            wait(dve, grown, i, h + 1)
            wait(dve, o_ready, i)
            for b in range(NC):
                ins = dve.scalar_tensor_tensor(out=state[:, b, h, :], in0=state[:, b, h, :], scalar=decay[:, h, b:b + 1],
                                               in1=c.bank[:, 4 + b // 2, (b % 2) * DV:(b % 2 + 1) * DV],
                                               op0=ALU.mult, op1=ALU.add)
            ins.then_inc(state_ready, 1)

        def move_keys(dve, i, b):
            wait(dve, k_turned, i, b + 1)
            bank = c.bank[:, 1 + b % 2, :]
            dve.tensor_copy(k_t[:, b, :, DEC_SEQ:KW], bank[:, 0:KV * P].rearrange("p (g t) -> p g t", g=KV))
            dve.tensor_copy(k_t[:, b, :, 0:DEC_SEQ],
                            bank[:, KV * P:KV * P + KV * DEC_SEQ].rearrange("p (g t) -> p g t", g=KV)).then_inc(k_t_ready, 1)

        @block.sync
        def _(sp):
            for dst, src in consts:
                sp.dma_start(dst[:], src).then_inc(const_here, 16)
            if not prompt:
                for dst, src in ((k_new, ck), (v_new, cv)):
                    sp.dma_start(dst[0:WINDOW - DEC_SEQ, :, :],
                                 src[:, DEC_SEQ:WINDOW, :].rearrange("b t f -> t b f")).then_inc(const_here, 16)

            def body(i):
                if prompt:
                    sp.sem_inc(c.held, 1)
                    sp.dma_start(cur[:, :], c.d.proj[bass.ds(i * P, P), :]).then_inc(cur_here, 16)
                    sp.sem_inc(c.held, 1)
                    sp.dma_start(trig[:, :], c.d.trig[bass.ds(i * P, P), :]).then_inc(trig_here, 16)
                else:
                    sp.dma_start(cur[0:T, :], c.d.proj[SEQ:TOKENS, :]).then_inc(cur_here, 16)
                    sp.dma_start(trig[0:T, :], c.d.trig[SEQ:TOKENS, :]).then_inc(trig_here, 16)

            loop(sp, body)
            if prompt:
                sp.dma_start(c.d.k_out_prompt, roped[:, SWA_HEADS:SWA_HEADS + KV, :].rearrange("t g d -> t (g d)")).then_inc(stored, 16)
                sp.dma_start(c.d.v_out_prompt, cur[:, SV0:SV0 + KV * HD]).then_inc(stored, 16)
                sp.dma_start(c.d.state_out_prompt.rearrange("h d v -> d h v"), state[:, 0, :, :]).then_inc(stored, 16)
                sp.wait_ge(stored, 48)
            else:
                wait(sp, rope_step, 0)
                for b in range(NB):
                    rows = slice(b * DEC_SEQ, (b + 1) * DEC_SEQ)
                    sp.dma_start(k_new[WINDOW - DEC_SEQ:WINDOW, b, :],
                                 roped[rows, SWA_HEADS:SWA_HEADS + KV, :].rearrange("t g d -> t (g d)")).then_inc(new_here, 16)
                    sp.dma_start(v_new[WINDOW - DEC_SEQ:WINDOW, b, :], cur[rows, SV0:SV0 + KV * HD]).then_inc(new_here, 16)
                sp.wait_ge(new_here, 32 * NB)
                sp.wait_ge(const_here, all_consts)
                sp.dma_start(c.d.k_out_sample.rearrange("b t f -> t b f"), k_new[:, :, :]).then_inc(stored, 16)
                sp.dma_start(c.d.v_out_sample.rearrange("b t f -> t b f"), v_new[:, :, :]).then_inc(stored, 16)
                sp.wait_ge(state_ready, GLA_HEADS)
                sp.dma_start(c.d.state_out_sample.rearrange("b h d v -> d b h v"), state[:, :, :, :]).then_inc(stored, 16)
                sp.wait_ge(stored, 48)


        @block.gpsimd
        def _(pool):
            if prompt:
                pool.memset(v_before[:, :], 0.0).then_inc(first_ready, 1)
            half = HD // 2
            heads = SWA_HEADS + KV

            def body(i):
                wait(pool, cur_here, i)
                wait(pool, trig_here, i)
                pool.sem_inc(c.held, 1)
                x = cur[0:T, SQ0:SQ0 + heads * HD].rearrange("t (h d) -> t h d", d=HD)
                x1, x2 = x[:, :, 0:half], x[:, :, half:HD]
                cos = trig[0:T, 0:half].unsqueeze(1).broadcast_to([T, heads, half])
                sin = trig[0:T, half:HD].unsqueeze(1).broadcast_to([T, heads, half])
                t0, t1 = rt[0][0:T], rt[1][0:T]
                out1, out2 = roped[0:T, :, 0:half], roped[0:T, :, half:HD]
                steps = [(t0, x1, cos, ALU.mult), (t1, x2, sin, ALU.mult), (out1, t0, t1, ALU.subtract),
                         (t0, x2, cos, ALU.mult), (t1, x1, sin, ALU.mult), (out2, t0, t1, ALU.add)]
                for n, (o, a, b, op) in enumerate(steps):
                    if n:
                        wait(pool, rope_step, i, n)
                        pool.sem_inc(c.held, 1)
                    pool.tensor_tensor(o, a, b, op).then_inc(rope_step, 1)
                wait(pool, rope_step, i)
                pool.sem_inc(c.held, 1)
                if prompt:
                    keys = roped[:, SWA_HEADS:heads, :]
                    pool.tensor_copy(k_twice[:, :, 0, :], keys)
                    pool.tensor_copy(k_twice[:, :, 1, :], keys).then_inc(k_twice_ready, 1)
                wait(pool, er_inverted, i)
                pool.sem_inc(c.held, 1)
                pool.tensor_tensor(silu[:, :], cur[0:T, R0:R0 + GLA_HEADS * DV], er[:, :], ALU.mult).then_inc(silu_ready, 1)
                wait(pool, inverted, i)
                wait(pool, exped, i)
                pool.sem_inc(c.held, 1)
                for n in range(2):
                    blocks = slice(n * NB // 2, (n + 1) * NB // 2)
                    pool.tensor_tensor(scores[:, blocks, :], scores[:, blocks, :],
                                       st[:, 5, blocks].unsqueeze(2).broadcast_to([P, NB // 2, KW]), ALU.mult).then_inc(weighted, 1)
                if prompt:
                    wait(pool, mixed, i)
                    pool.sem_inc(c.held, 1)
                    pool.tensor_copy(v_before[:, :], cur[:, SV0:SV0 + KV * HD]).then_inc(kept, 1)
                    pool.tensor_copy(k_t[:, :, 0:WINDOW], k_t[:, :, WINDOW:KW]).then_inc(kept, 1)
                    pool.tensor_copy(mask[:, :], mask_all[:, :]).then_inc(kept, 1)

            loop(pool, body)

        @block.scalar
        def _(act):
            act.wait_ge(const_here, all_consts)
            act.sem_inc(c.held, 1)

            def body(i):
                wait(act, mag_ready, i)
                act.activation(log1[:, :], mag[:, :], ACT.Exp).then_inc(exp1_ready, 1)
                wait(act, cur_here, i)
                act.activation(er[:, :], cur[0:T, R0:R0 + GLA_HEADS * DV], ACT.Exp, scale=-1.0).then_inc(er_ready, 1)
                wait(act, exp1_ready, i)
                act.activation(log1[:, :], log1[:, :], ACT.Ln, bias=1.0).then_inc(log1_ready, 1)
                wait(act, sums_ready, i)
                act.activation(eb[:, :], b2[0:T, :], ACT.Exp).then_inc(exps_ready, 1)
                act.activation(enb[:, :], b2[0:T, :], ACT.Exp, scale=-1.0).then_inc(exps_ready, 1)
                act.activation(ebd[:, :], b3[0:T, :], ACT.Exp).then_inc(exps_ready, 1)
                act.activation(decay[:, :, :], b0[:, 0:GLA_HEADS * NC].rearrange("p (h n) -> p h n", h=GLA_HEADS), ACT.Exp).then_inc(exps_ready, 1)
                wait(act, gated_turned, i)
                act.activation(kg_t[:, :, :], c.bank[:, 5, 0:GLA_HEADS * T].rearrange("p (h t) -> p h t", h=GLA_HEADS), ACT.Copy).then_inc(qk_ready, 1)
                wait(act, o_ready, i)
                for h in range(GLA_HEADS):
                    if h:
                        wait(act, o_summed, i, h)
                    act.activation(o_junk, c.bank[0:T, 2 + h // 2, (h % 2) * DV:(h % 2 + 1) * DV], ACT.Square,
                                   accum_out=o_stat[:, 0, h:h + 1]).then_inc(o_summed, 1)
                wait(act, o_meaned, i)
                act.activation(o_stat[:, 2, :], o_stat[:, 1, :], ACT.Sqrt).then_inc(o_rooted, 1)
                wait(act, o_turned, i)
                act.sem_inc(c.held, 1)
                for n in range(2):
                    act.activation(c.act[HI][:, 4 * n:4 * n + 4, tokens(i)],
                                   c.bank[:, 6 + n, 0:4 * T].rearrange("p (k t) -> p k t", k=4), ACT.Copy).then_inc(gla_rounded, 1)
                wait(act, q_turned, i)
                if prompt:
                    for n in range(2):
                        act.activation(q_t[:, 4 * n:4 * n + 4, :], c.bank[:, n, :].rearrange("p (k t) -> p k t", k=4), ACT.Copy,
                                       scale=HD ** -0.5).then_inc(q_t_ready, 1)
                else:
                    act.activation(q_t[:, :, :].rearrange("p k t -> p (k t)").rearrange("p (b k t) -> p k b t", b=NB, k=PAIRS),
                                   b0.rearrange("p (k b t) -> p k b t", b=NB, k=PAIRS), ACT.Copy,
                                   scale=HD ** -0.5).then_inc(q_t_ready, 1)
                wait(act, negated, i)
                for n in range(NB):
                    act.activation(scores[:, n, :], scores[:, n, :], ACT.Exp, bias=st[:, 2, n:n + 1],
                                   accum_out=st[:, 3, n:n + 1]).then_inc(exped, 1)
                wait(act, sunk, i)
                act.activation(st[:, 4, :], st[:, 4, :], ACT.Exp).then_inc(sink_exped, 1)
                for n in range(NB // 2):
                    if n % 2 == 0 or not prompt:
                        move_probs(act, i, n)
                wait(act, mixed, i)
                act.sem_inc(c.held, 1)
                for at, src in swa_out:
                    act.activation(c.act[HI][:, at, tokens(i)], src, ACT.Copy).then_inc(swa_rounded, 1)

            loop(act, body)

        @block.vector
        def _(dve):
            dve.memset(ga_t[:, :], 1.0).then_inc(first_ready, 1)
            dve.memset(q_spread[:, :, :], 0.0).then_inc(first_ready, 1)
            if prompt:
                dve.memset(state[:, 0, :, :], 0.0).then_inc(first_ready, 1)
                dve.memset(k_t[:, :, 0:WINDOW], 0.0).then_inc(first_ready, 1)
            dve.wait_ge(const_here, all_consts)
            dve.wait_ge(first_ready, 5 if prompt else 2)
            dve.sem_inc(c.held, 1)

            def body(i):
                wait(dve, ga_turned, i)
                dve.tensor_copy(ga_t[0:GATE_RANK, :], b0[0:GATE_RANK, 0:T]).then_inc(ga_ready, 1)
                wait(dve, gate_ready, i)
                dve.tensor_scalar(low[:, :], b1[0:T, :], 0.0, None, ALU.min).then_inc(low_ready, 1)
                wait(dve, low_ready, i)
                dve.scalar_tensor_tensor(out=mag[:, :], in0=low[:, :], scalar=2.0, in1=b1[0:T, :],
                                         op0=ALU.mult, op1=ALU.subtract).then_inc(mag_ready, 1)
                wait(dve, log1_ready, i)
                dve.tensor_tensor(log_a[:, :], low[:, :], log1[:, :], ALU.subtract).then_inc(log_a_ready, 1)
                wait(dve, er_ready, i)
                dve.tensor_scalar(er[:, :], er[:, :], 1.0, None, ALU.add).then_inc(er_one, 1)
                wait(dve, er_one, i)
                dve.reciprocal(er[:, :], er[:, :]).then_inc(er_inverted, 1)
                wait(dve, exps_ready, i)
                dve.scalar_tensor_tensor(out=qg[:, :], in0=cur[0:T, Q0:Q0 + 512], scalar=DK ** -0.5, in1=eb[:, :],
                                         op0=ALU.mult, op1=ALU.mult).then_inc(gated, 1)
                dve.tensor_tensor(kg[:, :], cur[0:T, K0:K0 + 512], enb[:, :], ALU.mult).then_inc(gated, 1)
                dve.tensor_tensor(ke[:, :], cur[0:T, K0:K0 + 512], ebd[:, :], ALU.mult).then_inc(gated, 1)
                wait(dve, gated_turned, i, 1)
                q_bank = c.bank[:, 4, 0:GLA_HEADS * T].rearrange("p (h t) -> p h t", h=GLA_HEADS)
                dve.tensor_copy(qg_t[:, :, :], q_bank).then_inc(qk_ready, 1)
                for h in range(GLA_HEADS):
                    ins = dve.tensor_copy(q_spread[:, h, :].rearrange("p (n x) -> p n x", n=NC)[:, :, 0:CL],
                                          q_bank[:, h, :].rearrange("p (n x) -> p n x", n=NC))
                ins.then_inc(qk_ready, 1)
                wait(dve, inner_ready, i)
                dve.tensor_tensor(inner[:, :, :], c.bank[0:T, 6, 0:GLA_HEADS * T].rearrange("p (h t) -> p h t", h=GLA_HEADS),
                                  inside[:, :].unsqueeze(1).broadcast_to([T, GLA_HEADS, T]), ALU.mult).then_inc(inner_masked, 1)
                if prompt:
                    wait(dve, grown, i, 1)
                    for h in range(GLA_HEADS):
                        ins = dve.scalar_tensor_tensor(out=state[:, 1, h, :], in0=state[:, 0, h, :], scalar=decay[:, h, 0:1],
                                                       in1=c.bank[:, 4 + h // 2, (h % 2) * DV:(h % 2 + 1) * DV],
                                                       op0=ALU.mult, op1=ALU.add)
                    ins.then_inc(state_ready, 1)
                else:
                    for h in range(GLA_HEADS):
                        if h >= 2:
                            wait(dve, grown, i, h - 1)
                        dve.tensor_tensor(k_own[:, h % 2, :, :],
                                          ke[:, h * DK:(h + 1) * DK].unsqueeze(1).broadcast_to([T, NC, DK]),
                                          own[:, :].unsqueeze(2).broadcast_to([T, NC, DK]), ALU.mult).then_inc(k_own_ready, 1)
                        if h >= 1:
                            new_state(dve, i, h - 1)
                    new_state(dve, i, GLA_HEADS - 1)
                wait(dve, o_summed, i)
                dve.tensor_scalar(o_stat[:, 1, :], o_stat[:, 0, :], 1.0 / DV, EPS, ALU.mult, ALU.add).then_inc(o_meaned, 1)
                if prompt:
                    wait(dve, grown, i, 2)
                    wait(dve, o_ready, i)
                    for h in range(GLA_HEADS):
                        ins = dve.scalar_tensor_tensor(out=state[:, 0, h, :], in0=state[:, 1, h, :], scalar=decay[:, h, 1:2],
                                                       in1=c.bank[:, h // 2, (h % 2) * DV:(h % 2 + 1) * DV],
                                                       op0=ALU.mult, op1=ALU.add)
                    ins.then_inc(state_ready, 1)
                wait(dve, o_rooted, i)
                dve.reciprocal(o_stat[:, 3, :], o_stat[:, 2, :]).then_inc(o_inverted, 1)
                wait(dve, o_inverted, i)
                for h in range(GLA_HEADS):
                    dve.scalar_tensor_tensor(out=o_norm[:, h * DV:(h + 1) * DV],
                                             in0=c.bank[0:T, 2 + h // 2, (h % 2) * DV:(h % 2 + 1) * DV],
                                             scalar=o_stat[:, 3, h:h + 1], in1=g_out[0:T, :],
                                             op0=ALU.mult, op1=ALU.mult).then_inc(o_normed, 1)
                wait(dve, silu_ready, i)
                wait(dve, o_normed, i)
                dve.tensor_tensor(o_norm[:, :], o_norm[:, :], silu[:, :], ALU.mult).then_inc(o_gated, 1)
                wait(dve, gla_rounded, i)
                dve.sem_inc(c.held, 1)
                for n in range(2):
                    at = (slice(None), slice(4 * n, 4 * n + 4), tokens(i))
                    dve.tensor_tensor(c.act[LO][at], c.bank[:, 6 + n, 0:4 * T].rearrange("p (k t) -> p k t", k=4),
                                      c.act[HI][at].bitcast(F32), ALU.subtract).then_inc(gla_heads_ready, 1)
                if prompt:
                    wait(dve, k_turned, i)
                    dve.tensor_copy(k_t[:, :, WINDOW:KW], c.bank[:, 2, 0:KV * P].rearrange("p (g t) -> p g t", g=KV)).then_inc(k_t_ready, 1)
                else:
                    dve.wait_ge(new_here, 32 * NB)
                    for b in range(NB):
                        if b >= 2:
                            wait(dve, k_turned, i, b - 1)
                        fresh = k_new[:, b, :].rearrange("t (g d) -> t g d", g=KV)
                        old = k_old[:, b, :].rearrange("t (g d) -> t g d", g=KV)
                        for twice in range(2):
                            dve.tensor_copy(k2[:, b % 2, :, twice, :], fresh)
                            ins = dve.tensor_copy(k2_old[:, b % 2, :, twice, :], old)
                        ins.then_inc(k2_ready, 1)
                        if b:
                            move_keys(dve, i, b - 1)
                    move_keys(dve, i, NB - 1)
                for n in range(NB):
                    wait(dve, scored, i, n // SB + 1)
                    dve.sem_inc(c.held, 1)
                    dve.tensor_tensor_reduce(out=scores[:, n, :], in0=score_bank(n),
                                             in1=mask[:, :], scale=1.0, scalar=NEG, op0=ALU.add, op1=ALU.max,
                                             accum_out=st[:, 0, n:n + 1]).then_inc(score_moved, 1)
                wait(dve, score_moved, i)
                sink_row = sinks[:, :] if prompt else sinks[:, :].broadcast_to([P, NB])
                dve.tensor_tensor(st[:, 1, :], st[:, 0, :], sink_row, ALU.max).then_inc(topped, 1)
                wait(dve, topped, i)
                dve.tensor_scalar(st[:, 2, :], st[:, 1, :], -1.0, None, ALU.mult).then_inc(negated, 1)
                dve.tensor_tensor(st[:, 4, :], sink_row, st[:, 1, :], ALU.subtract).then_inc(sunk, 1)
                wait(dve, exped, i)
                wait(dve, sink_exped, i)
                dve.tensor_tensor(st[:, 3, :], st[:, 3, :], st[:, 4, :], ALU.add).then_inc(totalled, 1)
                wait(dve, totalled, i)
                dve.reciprocal(st[:, 5, :], st[:, 3, :]).then_inc(inverted, 1)
                for n in range(1, NB // 2, 2):
                    if prompt:
                        move_probs(dve, i, n)
                wait(dve, swa_rounded, i)
                dve.sem_inc(c.held, 1)
                for at, src in swa_out:
                    dve.tensor_tensor(c.act[LO][:, at, tokens(i)], src, c.act[HI][:, at, tokens(i)].bitcast(F32),
                                      ALU.subtract).then_inc(swa_heads_ready, 1)

            loop(dve, body)

        @block.tensor
        def _(pe):
            pe.wait_ge(const_here, all_consts)
            pe.wait_ge(first_ready, 5 if prompt else 2)
            pe.sem_inc(c.held, 1)
            ident = c.ident

            def body(i):
                wait(pe, cur_here, i)
                pe.transpose(b0[0:GATE_RANK, 0:T], cur[0:T, GA0:GA0 + GATE_RANK], ident[0:T, 0:T]).then_inc(ga_turned, 1)
                wait(pe, ga_ready, i)
                pe.matmul(b1[0:T, :], ga_t[:, :], gate_w[:, :], start=True, stop=True).then_inc(gate_ready, 1)
                wait(pe, log_a_ready, i)
                pe.matmul(b2[0:T, :], tri[:, :], log_a[:, :], start=True, stop=True)
                pe.matmul(b3[0:T, :], suf[:, :], log_a[:, :], start=True, stop=True)
                for h in range(GLA_HEADS):
                    last = pe.matmul(b0[:, h * NC:(h + 1) * NC], log_a[:, h * DK:(h + 1) * DK], ind[:, :], start=True, stop=True)
                last.then_inc(sums_ready, 1)
                for bank, x, n in ((4, qg, 1), (5, kg, 2)):
                    wait(pe, gated, i, n)
                    for h in range(GLA_HEADS):
                        last = pe.transpose(c.bank[:, bank, h * T:(h + 1) * T], x[:, h * DK:(h + 1) * DK], ident[0:T, 0:T])
                    last.then_inc(gated_turned, 1)
                wait(pe, qk_ready, i)
                for h in range(GLA_HEADS):
                    last = pe.matmul(c.bank[0:T, 6, h * T:(h + 1) * T], kg_t[:, h, :], qg_t[:, h, :], start=True, stop=True)
                last.then_inc(inner_ready, 1)
                wait(pe, gated, i)
                if prompt:
                    for n, bank in ((0, 4), (1, 0)):
                        rows = slice(n * CL, (n + 1) * CL)
                        for h in range(GLA_HEADS):
                            last = pe.matmul(c.bank[:, bank + h // 2, (h % 2) * DV:(h % 2 + 1) * DV],
                                             ke[rows, h * DK:(h + 1) * DK], cur[rows, V0 + h * DV:V0 + (h + 1) * DV],
                                             start=True, stop=True)
                        last.then_inc(grown, 1)
                    wait(pe, state_ready, i, 1)
                wait(pe, inner_masked, i)
                for h in range(GLA_HEADS):
                    out = c.bank[0:T, 2 + h // 2, (h % 2) * DV:(h % 2 + 1) * DV]
                    pe.matmul(out, inner[:, h, :], cur[0:T, V0 + h * DV:V0 + (h + 1) * DV], start=True, stop=False)
                    for n in range(NC):
                        last = pe.matmul(out, q_spread[:, h, n * T:(n + 1) * T], state[:, n, h, :], start=False, stop=(n == NC - 1))
                last.then_inc(o_ready, 1)
                if not prompt:
                    for h in range(GLA_HEADS):
                        wait(pe, k_own_ready, i, h + 1)
                        if h:
                            wait(pe, state_ready, i, h)
                        for b in range(NC):
                            last = pe.matmul(c.bank[:, 4 + b // 2, (b % 2) * DV:(b % 2 + 1) * DV], k_own[:, h % 2, b, :],
                                             cur[0:T, V0 + h * DV:V0 + (h + 1) * DV], start=True, stop=True)
                        last.then_inc(grown, 1)
                    wait(pe, state_ready, i)
                wait(pe, o_gated, i)
                for n in range(2):
                    for j in range(4):
                        k = 4 * n + j
                        last = pe.transpose(c.bank[:, 6 + n, j * T:(j + 1) * T], o_norm[:, k * P:(k + 1) * P], ident[0:T, 0:T])
                    last.then_inc(o_turned, 1)
                wait(pe, rope_step, i)
                wait(pe, state_ready, i)
                per_bank = 4 if prompt else PAIRS
                for k in range(PAIRS):
                    last = pe.transpose(c.bank[:, k // per_bank, k % per_bank * T:(k % per_bank + 1) * T],
                                        roped[0:T, 2 * k:2 * k + 2, :].rearrange("t h d -> t (h d)"), ident[0:T, 0:T])
                last.then_inc(q_turned, 1)
                if prompt:
                    wait(pe, k_twice_ready, i)
                    wait(pe, o_normed, i)
                    for g in range(KV):
                        last = pe.transpose(c.bank[:, 2, g * P:(g + 1) * P], k_twice[:, g, :, :].rearrange("t a d -> t (a d)"), ident[:, :])
                    last.then_inc(k_turned, 1)
                    wait(pe, q_t_ready, i)
                    wait(pe, k_t_ready, i)
                    wait(pe, gla_heads_ready, i)
                    for h in range(SWA_HEADS):
                        n, par, g = h // 2, h % 2, h // (SWA_HEADS // KV)
                        if h % SB == 0 and h >= 2 * SB:
                            wait(pe, score_moved, i, h - SB)
                        rows = slice(par * HD, (par + 1) * HD)
                        last = pe.matmul(score_bank(h), q_t[rows, h // 2, :], k_t[rows, g, :],
                                         start=True, stop=True)
                        if h % SB == SB - 1:
                            last.then_inc(scored, 1)
                else:
                    wait(pe, o_normed, i)
                    for b in range(NB):
                        wait(pe, k2_ready, i, b + 1)
                        if b >= 2:
                            wait(pe, k_t_ready, i, b - 1)
                        bank = c.bank[:, 1 + b % 2, :]
                        for g in range(KV):
                            pe.transpose(bank[:, g * P:(g + 1) * P], k2[:, b % 2, g, :, :].rearrange("t a d -> t (a d)"), ident[:, :])
                            at = KV * P + g * DEC_SEQ
                            last = pe.transpose(bank[:, at:at + DEC_SEQ], k2_old[:, b % 2, g, :, :].rearrange("t a d -> t (a d)"),
                                                ident[0:DEC_SEQ, 0:DEC_SEQ])
                        last.then_inc(k_turned, 1)
                    wait(pe, q_t_ready, i)
                    wait(pe, gla_heads_ready, i)
                    for b in range(NB):
                        n = b // 2
                        wait(pe, k_t_ready, i, b + 1)
                        for g in range(KV):
                            for par in range(2):
                                rows = slice(par * HD, (par + 1) * HD)
                                at = g * HD + par * 32
                                last = pe.matmul(c.bank[at:at + 32, 3 + n % 4, (b % 2) * 256:(b % 2) * 256 + KW],
                                                 q_t[rows, b, 32 * g:32 * g + 32],
                                                 k_t[rows, b, g, :], start=True, stop=True)
                        if b % 2:
                            last.then_inc(scored, 1)
                for n in range(NB // 2):
                    wait(pe, weighted, i, 1 if n < NB // 4 else 2)
                    if n == 0:
                        wait(pe, score_moved, i)
                    if n >= 4:
                        wait(pe, p_ready[n % 2], i, (n - 4) // 2 + 1)
                    for a in range(2):
                        for half in range(2):
                            dst = c.bank[:, 3 + n % 4, (2 * a + half) * P:(2 * a + half + 1) * P]
                            if prompt:
                                last = pe.transpose(dst, scores[:, 2 * n + a, half * P:(half + 1) * P], ident[:, :])
                            elif half == 0:
                                last = pe.transpose(dst, scores[:, 2 * n + a, DEC_SEQ:KW], ident[:, :])
                            else:
                                last = pe.transpose(dst[0:DEC_SEQ, :], scores[:, 2 * n + a, 0:DEC_SEQ], ident[:, :])
                    last.then_inc(p_turned, 1)
                wait(pe, p_ready[0], i)
                wait(pe, p_ready[1], i)
                if prompt:
                    for h in range(SWA_HEADS):
                        par, g = h % 2, h // (SWA_HEADS // KV)
                        out = c.bank[par * HD:(par + 1) * HD, h // 8, h // 2 % 4 * P:(h // 2 % 4 + 1) * P]
                        pe.matmul(out, v_before[:, g * HD:(g + 1) * HD], probs_t[:, h, 0, :], start=True, stop=False)
                        last = pe.matmul(out, cur[:, SV0 + g * HD:SV0 + (g + 1) * HD], probs_t[:, h, 1, :], start=False, stop=True)
                else:
                    for b in range(NB):
                        for g in range(KV):
                            for par in range(2):
                                at = g * HD + par * 32
                                out = c.bank[par * HD:(par + 1) * HD, 0, :].rearrange("p (k t) -> p k t", k=PAIRS)[
                                    :, 4 * g:4 * g + 4, b * DEC_SEQ:(b + 1) * DEC_SEQ]
                                pe.matmul(out, v_new[:, b, g * HD:(g + 1) * HD],
                                          probs_t[:, b, at:at + 32].rearrange("p (k t) -> p k t", k=4), start=True, stop=False)
                                last = pe.matmul(out, v_old[:, b, g * HD:(g + 1) * HD],
                                                 probs_old_t[:, b, at:at + 32].rearrange("p (k t) -> p k t", k=4),
                                                 start=False, stop=True)
                last.then_inc(mixed, 1)

            loop(pe, body)


def expert_queries(nc, c):
    ctx, sb, sem = stage(nc)
    with ctx:
        raw = sb("pq_raw", [P, 2, KC, P])
        w = [sb("pq" + part, [P, 2, KC, P], F32R) for part in ("_hi", "_lo")]
        raw_here = [sem(f"pq_raw_here{s}") for s in range(2)]
        rounded, split, summed, moved = sem("pq_rounded"), sem("pq_split"), sem("pq_summed"), sem("pq_moved")
        block = ctx.enter_context(nc.Block())

        @block.sync
        def _(sp):
            with sp.Fori(0, PHEADS // 2) as i:
                for s in range(2):
                    sp.wait_ge(split, i * 2 + (s + 1))
                    sp.sem_inc(c.held, 1)
                    sp.dma_start(raw[:, s], c.d.w_peer_q[bass.ds(i * 2 + s, 1)].rearrange("a p k n -> (a p) k n")).then_inc(raw_here[s], 16)

        @block.scalar
        def _(act):
            with act.Fori(0, PHEADS // 2) as i:
                for s in range(2):
                    act.wait_ge(raw_here[s], i * 16 + 16)
                    act.wait_ge(summed, i * 4 + (2 * s + 2))
                    act.activation(w[HI][:, s], raw[:, s], ACT.Copy).then_inc(rounded, 1)

        @block.gpsimd
        def _(pool):
            with pool.Fori(0, PHEADS // 2) as i:
                for s in range(2):
                    pool.wait_ge(rounded, i * 2 + (s + 1))
                    pool.tensor_tensor(w[LO][:, s], raw[:, s], w[HI][:, s].bitcast(F32), ALU.subtract).then_inc(split, 1)

        @block.vector
        def _(dve):
            dve.sem_inc(moved, 4)
            dve.sem_inc(split, 2)
            with dve.Fori(0, PHEADS // 2) as i:
                for s in range(2):
                    for n in range(2):
                        dve.wait_ge(summed, i * 4 + (4 + 2 * s + n + 1))
                        dve.sem_inc(c.held, 1)
                        dve.tensor_copy(c.query_t[:, bass.ds(i * 2 + s, 1), n * HALF:(n + 1) * HALF],
                                        c.bank[:, 2 * s + n, 0:HALF].unsqueeze(1)).then_inc(moved, 1)

        @block.tensor
        def _(pe):
            pe.sem_inc(summed, 4)
            with pe.Fori(0, PHEADS // 2) as i:
                for s in range(2):
                    pe.wait_ge(split, i * 2 + (s + 3))
                    for n in range(2):
                        pe.wait_ge(moved, i * 4 + (2 * s + n + 1))
                        product(pe, c.bank[:, 2 * s + n, 0:HALF], lambda part, k: w[part][:, s, k, :],
                                lambda part, k: c.act[part][:, k, n * HALF:(n + 1) * HALF]).then_inc(summed, 1)


def route(nc, c):
    ctx, sb, sem = stage(nc)
    HP = 2 * PHEADS
    with ctx:
        query = sb("rt_query", [P, PHEADS, P])
        keys = sb("rt_keys", [P, PHEADS, N_KEYS])
        score = sb("rt_score", [P, HP, N_KEYS])
        top = sb("rt_top", [P, HP, TOPK])
        top_at = sb("rt_top_at", [P, HP, TOPK], U32)
        top_atf = sb("rt_top_atf", [P, HP, TOPK])
        pair = sb("rt_pair", [P, PHEADS, TOPK * TOPK])
        best = sb("rt_best", [P, PHEADS, TOPK])
        best_at = sb("rt_best_at", [P, PHEADS, TOPK], U32)
        rank = sb("rt_rank", [P, 2, SEL], U32)
        rankf = sb("rt_rankf", [P, 2, SEL])
        rank16 = sb("rt_rank16", [P, TOPK])
        hit = sb("rt_hit", [P, PHEADS, TOPK, TOPK])
        picks = sb("rt_picks", [P, 3, SEL])
        total = sb("rt_total", [P, 2, PHEADS])
        const_here, query_ready, scored, score_ready = sem("rt_const"), sem("rt_query_ready"), sem("rt_scored"), sem("rt_score_ready")
        found, shifted, exped, picked = sem("rt_found"), sem("rt_shifted"), sem("rt_exped"), sem("rt_picked")
        turned, moved = sem("rt_turned"), sem("rt_moved")
        block = ctx.enter_context(nc.Block())

        @block.sync
        def _(sp):
            sp.dma_start(keys[:, :, :], c.d.sub_keys).then_inc(const_here, 16)
            sp.dma_start(rank16[:, :], c.d.rank16).then_inc(const_here, 16)

        @block.scalar
        def _(act):
            act.sem_inc(query_ready, 1)
            with act.Fori(0, TILES) as i:
                act.wait_ge(moved, i + 1)
                act.sem_inc(c.held, 1)
                act.activation(query[:, :, :], c.query_t[:, :, bass.ds(i * STRIDE, P)], ACT.Copy).then_inc(query_ready, 1)
                act.wait_ge(scored, i + 1)
                act.activation(score[:, :, :], c.bank[:, 0:4, :].rearrange("p b (s n) -> p (b s) n", n=N_KEYS), ACT.Copy).then_inc(score_ready, 1)
                act.wait_ge(shifted, i + 1)
                act.activation(best[:, :, :], best[:, :, :], ACT.Exp).then_inc(exped, 1)

        @block.vector
        def _(dve):
            n_steps = [0]

            def steps(i, instructions):
                for make in instructions:
                    dve.wait_ge(found, i * STEPS + n_steps[0]) if n_steps[0] else None
                    if n_steps[0]:
                        dve.sem_inc(c.held, 1)
                    make().then_inc(found, 1)
                    n_steps[0] += 1

            def top16(values, out, at, n):
                def each(make):
                    def run():
                        for r in range(n):
                            last = make(r)
                        return last
                    return run
                return [each(lambda r: dve.max(out[:, r, 0:8], values[:, r, :])),
                        each(lambda r: dve.max_index(at[:, r, 0:8], out[:, r, 0:8], values[:, r, :])),
                        each(lambda r: dve.match_replace(values[:, r, :], out[:, r, 0:8], values[:, r, :], NEG)),
                        each(lambda r: dve.max(out[:, r, 8:16], values[:, r, :])),
                        each(lambda r: dve.max_index(at[:, r, 8:16], out[:, r, 8:16], values[:, r, :]))]

            top4 = top[:, :, :].rearrange("p (s h) k -> p s h k", s=2)
            at4 = top_atf[:, :, :].rearrange("p (s h) k -> p s h k", s=2)
            four = [P, PHEADS, TOPK, TOPK]
            gate = picks[:, 2, :].rearrange("p (h k) -> p h k", h=PHEADS)

            def after_keys():
                out = [lambda: dve.tensor_copy(top_atf[:, :, :], top_at[:, :, :]),
                       lambda: dve.tensor_tensor(pair[:, :, :].rearrange("p h (a b) -> p h a b", b=TOPK),
                                                 top4[:, 0, :, :].unsqueeze(3).broadcast_to(four),
                                                 top4[:, 1, :, :].unsqueeze(2).broadcast_to(four), ALU.add)]
                out += top16(pair, best, best_at, PHEADS)
                flat = best_at[:, :, :].rearrange("p h k -> p (h k)")
                out += [lambda: dve.tensor_scalar(rank[:, 0, :], flat, 4, None, ALU.logical_shift_right),
                        lambda: dve.tensor_scalar(rank[:, 1, :], flat, TOPK - 1, None, ALU.bitwise_and),
                        lambda: dve.tensor_copy(rankf[:, :, :], rank[:, :, :])]
                for s in range(2):
                    mine = rankf[:, s, :].rearrange("p (h k) -> p h k", h=PHEADS).unsqueeze(3).broadcast_to(four)
                    out += [lambda mine=mine: dve.tensor_tensor(hit[:, :, :, :], mine,
                                                                rank16[:, :].unsqueeze(1).unsqueeze(1).broadcast_to(four), ALU.is_equal),
                            lambda s=s: dve.tensor_tensor(hit[:, :, :, :], hit[:, :, :, :],
                                                          at4[:, s, :, :].unsqueeze(2).broadcast_to(four), ALU.mult),
                            lambda s=s: dve.tensor_reduce(picks[:, s, :].rearrange("p (h k) -> p h k", h=PHEADS), hit[:, :, :, :], AX_X, ALU.add)]
                return out

            def after_exp():
                wide = [P, PHEADS, TOPK]
                return [lambda: dve.tensor_reduce(total[:, 0, :], best[:, :, :], AX_X, ALU.add),
                        lambda: dve.reciprocal(total[:, 1, :], total[:, 0, :]),
                        lambda: dve.tensor_tensor(gate, best[:, :, :], total[:, 1, :].unsqueeze(2).broadcast_to(wide), ALU.mult)]

            first = top16(score, top, top_at, HP)
            second = after_keys()
            STEPS = len(first) + len(second) + 1 + 3
            dve.wait_ge(const_here, 32)
            dve.sem_inc(moved, 1)
            with dve.Fori(0, TILES) as i:
                n_steps[0] = 0
                dve.wait_ge(score_ready, i + 1)
                dve.sem_inc(c.held, 1)
                steps(i, first)
                steps(i, second)
                steps(i, [lambda: dve.tensor_tensor(gate, best[:, :, :], best[:, :, 0:1].broadcast_to([P, PHEADS, TOPK]), ALU.subtract)])
                dve.wait_ge(found, i * STEPS + n_steps[0])
                dve.tensor_copy(best[:, :, :], gate).then_inc(shifted, 1)
                dve.wait_ge(exped, i + 1)
                steps(i, after_exp())
                dve.wait_ge(found, i * STEPS + STEPS)
                dve.sem_inc(picked, 1)
                dve.wait_ge(turned, i + 1)
                dve.sem_inc(c.held, 1)
                dve.tensor_copy(c.picks_t[:, :, bass.ds(i * STRIDE, P)], c.bank[:, 4, 0:3 * P].rearrange("p (a t) -> p a t", a=3)).then_inc(moved, 1)

        @block.tensor
        def _(pe):
            pe.wait_ge(const_here, 32)
            with pe.Fori(0, TILES) as i:
                pe.wait_ge(query_ready, i + 2)
                for h in range(PHEADS):
                    for s in range(2):
                        rows = slice(64 * s, 64 * s + 64)
                        n = PHEADS * s + h
                        last = pe.matmul(c.bank[:, n // 4, n % 4 * P:(n % 4 + 1) * P], query[rows, h, :], keys[rows, h, :],
                                         start=True, stop=True)
                last.then_inc(scored, 1)
                pe.wait_ge(picked, i + 1)
                for n in range(3):
                    last = pe.transpose(c.bank[:, 4, n * P:(n + 1) * P], picks[:, n, :], c.ident[:, :])
                last.then_inc(turned, 1)


HALF = TOKENS // 2
GROUP = 64
GROUPS = TOKENS // GROUP
QUAD = 4


def gate_arrays(nc, c):
    ctx, sb, sem = stage(nc)
    QUADS = GROUP // QUAD
    with ctx:
        number = sb("ga_number", [P, N_KEYS])
        second = sb("ga_second", [P, 2, QUAD, N_KEYS])
        first = sb("ga_first", [P, 2, QUAD, N_KEYS])
        out = sb("ga_out", [P, 2, N_KEYS, GROUP])
        number_here, rows_ready, summed, moved = sem("ga_number_here"), sem("ga_rows_ready"), sem("ga_summed"), sem("ga_moved")
        stored, slot_free = [sem(f"ga_stored{s}") for s in range(2)], sem("ga_slot_free")
        block = ctx.enter_context(nc.Block())

        @block.sync
        def _(sp):
            sp.dma_start(number[:, :], c.d.number).then_inc(number_here, 16)

            def store(g, s, uses):
                sp.wait_ge(moved, g * QUADS + (QUADS + 2))
                sp.sem_inc(c.held, 1)
                sp.dma_start(c.d.gates[bass.ds(g, 1)].rearrange("a j i t -> (a j) i t"), out[:, s, :, :]).then_inc(stored[s], 16)
                sp.wait_ge(stored[s], uses)
                sp.sem_inc(slot_free, 1)

            with sp.Fori(0, GROUPS // 2) as i:
                for s in range(2):
                    store(i * 2 + s, s, i * 16 + 16)
            if GROUPS % 2:
                sp.wait_ge(moved, GROUPS * QUADS + 2)
                sp.dma_start(c.d.gates[GROUPS - 1], out[:, 0, :, :]).then_inc(stored[0], 16)
                sp.wait_ge(stored[0], 16 * (GROUPS // 2) + 16)

        @block.vector
        def _(dve):
            dve.wait_ge(number_here, 16)
            with dve.Fori(0, TOKENS // (2 * QUAD)) as i:
                for s in range(2):
                    for n in range(QUAD):
                        t = i * 2 * QUAD + (s * QUAD + n)
                        if n == 0:
                            dve.wait_ge(summed, i * 2 + (s + 1))
                            dve.sem_inc(c.held, 1)
                        dve.tensor_scalar(second[:, s, n, :], number[:, :], c.picks_t[:, 1, bass.ds(t, 1)], None, ALU.is_equal)
                        last = dve.tensor_scalar(first[:, s, n, :], number[:, :], c.picks_t[:, 0, bass.ds(t, 1)],
                                                 c.picks_t[:, 2, bass.ds(t, 1)], ALU.is_equal, ALU.mult)
                    last.then_inc(rows_ready, 1)

        @block.tensor
        def _(pe):
            pe.wait_ge(number_here, 16)
            pe.sem_inc(summed, 2)
            with pe.Fori(0, TOKENS // (2 * QUAD)) as i:
                for s in range(2):
                    pe.wait_ge(rows_ready, i * 2 + (s + 1))
                    pe.wait_ge(moved, i * 2 + (s + 1))
                    for n in range(QUAD):
                        last = pe.matmul(c.bank[:, s, n * P:(n + 1) * P], second[:, s, n, :], first[:, s, n, :], start=True, stop=True)
                    last.then_inc(summed, 1)

        @block.scalar
        def _(act):
            act.sem_inc(moved, 2)
            act.sem_inc(slot_free, 2)

            def group(i, s, count):
                act.wait_ge(slot_free, i * 2 + (s + 1))
                for q in range(count):
                    base = (i * 2 + s) * QUADS
                    act.wait_ge(summed, base + (q + 1 + 2))
                    b = q % 2
                    act.activation(out[:, s, :, q * QUAD:(q + 1) * QUAD],
                                   c.bank[:, b, :].rearrange("p (t i) -> p i t", t=QUAD), ACT.Copy).then_inc(moved, 1)

            with act.Fori(0, GROUPS // 2) as i:
                for s in range(2):
                    group(i, s, QUADS)
            if GROUPS % 2:
                group(GROUPS // 2, 0, QUADS)


ROW_PAIR = 2
BLOCKS = N_KEYS // ROW_PAIR
OUTS = 2 * KC


def experts(nc, c):
    ctx, sb, sem = stage(nc)
    with ctx:
        raw = sb("raw", [P, 2, D])
        u = [sb("u" + part, [P, 2, KC, P], F32R) for part in ("_hi", "_lo")]
        v = [sb("v" + part, [P, 2, D], F32R) for part in ("_hi", "_lo")]
        gates = sb("gates", [P, GROUPS, 2, GROUP])
        hot = sb("hot", [P, 2, TOKENS])
        coef = [sb("coef" + part, [P, 2, TOKENS], F32R) for part in ("_hi", "_lo")]
        raw_here = [sem(f"raw_here{s}") for s in range(2)]
        g_here = sem("g_here")
        u_rounded, u_split, v_rounded, v_split = sem("u_rounded"), sem("u_split"), sem("v_rounded"), sem("v_split")
        dotted, hot_ready, weighed = sem("dotted"), sem("hot_ready"), sem("weighed")
        coef_rounded, coef_split = sem("coef_rounded"), sem("coef_split")
        mixed, added, cleared = sem("mixed"), sem("added"), sem("cleared")
        block = ctx.enter_context(nc.Block())


        def turns(eng, turn):
            with eng.Fori(0, BLOCKS - 2) as b:
                turn(b, True, True)
            turn(BLOCKS - 2, True, False)
            turn(BLOCKS - 1, False, False)

        @block.sync
        def _(sp):
            def load_u(i, s):
                src = c.d.u_t[bass.ds(i, 1)].rearrange("a p k e -> (a p) (k e)")
                sp.dma_start(raw[:, s, :], src).then_inc(raw_here[s], 16)

            sp.dma_start(gates[:, :, 1, :], c.d.gates[:, :, 0, :].rearrange("g j t -> j g t")).then_inc(g_here, 16)
            load_u(0, 1)
            load_u(1, 0)
            sp.wait_ge(u_split, 1)
            load_u(2, 1)

            def turn(b, more1, more0):
                sp.wait_ge(weighed, b * 2 + 1)
                sp.sem_inc(c.held, 1)
                if more1:
                    sp.dma_start(gates[:, :, :, :].rearrange("j g i t -> j g (i t)"),
                                 c.d.gates[:, :, bass.ds(b * 2 + 1, 2), :].rearrange("g j i t -> j g (i t)")).then_inc(g_here, 16)
                else:
                    sp.dma_start(gates[:, :, 0, :], c.d.gates[:, :, N_KEYS - 1, :].rearrange("g j t -> j g t")).then_inc(g_here, 16)
                for r in range(2):
                    if r == 0 or more1:
                        sp.wait_ge(u_split, b * 2 + (2 + r))
                    else:
                        sp.wait_ge(v_split, b * 2)
                    sp.sem_inc(c.held, 1)
                    sp.dma_start(raw[:, r, :], c.d.v[bass.ds(b * (2 * P) + r * P, P), :]).then_inc(raw_here[r], 16)
                for r, more in ((0, more1), (1, more0)):
                    if more:
                        sp.wait_ge(v_split, b * 2 + (1 + r))
                        sp.sem_inc(c.held, 1)
                        load_u(b * 2 + (3 + r), r)

            turns(sp, turn)

        @block.scalar
        def _(act):
            def u_hi(slot, row, uses, dots):
                act.wait_ge(raw_here[slot], uses)
                act.wait_ge(dotted, dots)
                act.activation(u[HI][:, row].rearrange("p k e -> p (k e)"), raw[:, slot, :], ACT.Copy).then_inc(u_rounded, 1)

            def gelu(row, first):
                for n in range(2):
                    act.wait_ge(dotted, first + n + 4)
                    act.activation(hot[:, row, n * HALF:(n + 1) * HALF], c.bank[:, 2 * row + n, 0:HALF], ACT.Gelu).then_inc(hot_ready, 1)

            def coef_hi(row, number):
                act.wait_ge(weighed, number)
                act.activation(coef[HI][:, row, :], hot[:, row, :], ACT.Copy).then_inc(coef_rounded, 1)

            u_hi(1, 0, 16, 1)
            u_hi(0, 1, 16, 1)
            gelu(0, 1)
            u_hi(1, 0, 32, 6)

            def turn(b, more1, more0):
                act.wait_ge(mixed, b * OUTS + 1)
                coef_hi(0, b * 2 + 1)
                for r in range(2):
                    act.wait_ge(raw_here[r], b * 32 + 16 * (2 + r - (r == 1 and not more1)))
                    act.activation(v[HI][:, r, :], raw[:, r, :], ACT.Copy).then_inc(v_rounded, 1)
                act.wait_ge(coef_split, b * 2 + 1)
                gelu(1, b * 4 + 3)
                if more1:
                    u_hi(0, 1, b * 32 + 48, b * 4 + 8)
                coef_hi(1, b * 2 + 2)
                if more1:
                    gelu(0, b * 4 + 5)
                if more0:
                    u_hi(1, 0, b * 32 + 64, b * 4 + 10)

            turns(act, turn)

        @block.gpsimd
        def _(pool):
            def u_lo(slot, row, number):
                pool.wait_ge(u_rounded, number)
                pool.tensor_tensor(u[LO][:, row].rearrange("p k e -> p (k e)"), raw[:, slot, :],
                                   u[HI][:, row].rearrange("p k e -> p (k e)").bitcast(F32), ALU.subtract).then_inc(u_split, 1)

            u_lo(1, 0, 1)
            u_lo(0, 1, 2)
            u_lo(1, 0, 3)

            def turn(b, more1, more0):
                if more1:
                    u_lo(0, 1, b * 2 + 4)
                if more0:
                    u_lo(1, 0, b * 2 + 5)

            turns(pool, turn)

        @block.vector
        def _(dve):
            def weigh(row, at, gelus, loads):
                dve.wait_ge(hot_ready, gelus)
                dve.wait_ge(g_here, loads)
                x = hot[:, row, :].rearrange("p (g t) -> p g t", t=GROUP)
                dve.tensor_tensor(x, x, gates[:, :, at, :], ALU.mult).then_inc(weighed, 1)

            def coef_lo(row, number):
                dve.wait_ge(coef_rounded, number)
                dve.tensor_tensor(coef[LO][:, row, :], hot[:, row, :], coef[HI][:, row, :].bitcast(F32), ALU.subtract).then_inc(coef_split, 1)

            dve.memset(c.y_t[:, :, :], 0.0).then_inc(cleared, 1)
            dve.wait_ge(cleared, 1)
            dve.sem_inc(added, 4)
            weigh(0, 1, 6, 16)

            def turn(b, more1, more0):
                coef_lo(0, b * 2 + 1)
                for r in range(2):
                    dve.wait_ge(v_rounded, b * 2 + (r + 1))
                    dve.tensor_tensor(v[LO][:, r, :], raw[:, r, :], v[HI][:, r, :].bitcast(F32), ALU.subtract).then_inc(v_split, 1)
                weigh(1, 0, b * 4 + 8, b * 16 + 32)
                coef_lo(1, b * 2 + 2)
                if more1:
                    weigh(0, 1, b * 4 + 10, b * 16 + 32)
                for m in range(OUTS):
                    k, n = m // 2, m % 2
                    dve.wait_ge(mixed, b * OUTS + (m + 2))
                    y = c.y_t[:, k, n * HALF:(n + 1) * HALF]
                    dve.tensor_tensor(y, y, c.bank[:, 4 + m % 4, 0:HALF], ALU.add).then_inc(added, 1)

            turns(dve, turn)

        @block.tensor
        def _(pe):
            pe.sem_inc(dotted, 4)
            pe.sem_inc(mixed, 1)
            pe.sem_inc(hot_ready, 4)

            def dots(row, number, gelus):
                pe.wait_ge(u_split, number)
                for n in range(2):
                    pe.wait_ge(hot_ready, gelus + n)
                    product(pe, c.bank[:, 2 * row + n, 0:HALF], lambda part, k: u[part][:, row, k, :],
                            lambda part, k: c.act[part][:, k, n * HALF:(n + 1) * HALF]).then_inc(dotted, 1)

            dots(0, 1, 1)

            def turn(b, more1, more0):
                dots(1, b * 2 + 2, b * 4 + 3)
                if more1:
                    dots(0, b * 2 + 3, b * 4 + 5)
                pe.wait_ge(v_split, b * 2 + 2)
                pe.wait_ge(coef_split, b * 2 + 2)
                for m in range(OUTS):
                    k, n = m // 2, m % 2
                    pe.wait_ge(added, b * OUTS + (m + 1))
                    for r in range(2):
                        for q, (a, z) in enumerate(PASSES):
                            last = pe.matmul(c.bank[:, 4 + m % 4, 0:HALF], v[a][:, r, k * P:(k + 1) * P],
                                             coef[z][:, r, n * HALF:(n + 1) * HALF],
                                             start=(r == 0 and q == 0), stop=(r == 1 and q == len(PASSES) - 1))
                    last.then_inc(mixed, 1)

            turns(pe, turn)


def finish(nc, c):
    ctx, sb, sem = stage(nc)
    with ctx:
        y_part = sb("fi_y", [P, KC, P])
        h = sb("fi_h", [P, D])
        square = sb("fi_square", [P, D])
        out = sb("fi_out", [P, D])
        gain = sb("fi_gain", [P, D])
        stat = sb("fi_stat", [P, 4])
        gain_here, h_here, y_ready, turned, added = (sem("fi_" + s) for s in ("gain_here", "h_here", "y_ready", "turned", "added"))
        summed, meaned, rooted, inverted, scaled, stored, out_free = (
            sem("fi_" + s) for s in ("summed", "meaned", "rooted", "inverted", "scaled", "stored", "out_free"))
        block = ctx.enter_context(nc.Block())

        @block.sync
        def _(sp):
            sp.dma_start(gain[:, :], c.d.g_final).then_inc(gain_here, 16)
            with sp.Fori(0, TILES) as i:
                sp.wait_ge(scaled, i + 1)
                sp.sem_inc(c.held, 1)
                sp.dma_start(h[:, :], c.d.h[bass.ds(i * STRIDE, P), :]).then_inc(h_here, 16)
                sp.wait_ge(scaled, i + 2)
                sp.sem_inc(c.held, 1)
                sp.dma_start(c.d.y[bass.ds(i * STRIDE, P), :], out[:, :]).then_inc(stored, 16)
                sp.wait_ge(stored, i * 16 + 16)
                sp.sem_inc(out_free, 1)

        @block.scalar
        def _(act):
            with act.Fori(0, TILES) as i:
                act.wait_ge(turned, i * 4 + 4)
                act.sem_inc(c.held, 1)
                act.activation(y_part[:, :, :], c.y_t[:, :, bass.ds(i * STRIDE, P)], ACT.Copy).then_inc(y_ready, 1)
                act.wait_ge(added, i * 4 + 8)
                act.activation(square[:, :], h[:, :], ACT.Square, accum_out=stat[:, 0:1]).then_inc(summed, 1)
                act.wait_ge(meaned, i + 1)
                act.activation(stat[:, 2:3], stat[:, 1:2], ACT.Sqrt).then_inc(rooted, 1)

        @block.vector
        def _(dve):
            dve.sem_inc(scaled, 1)
            dve.sem_inc(added, 4)
            dve.sem_inc(out_free, 1)
            dve.wait_ge(gain_here, 16)
            dve.sem_inc(c.held, 1)
            with dve.Fori(0, TILES) as i:
                dve.wait_ge(h_here, i * 16 + 16)
                for k in range(4):
                    dve.wait_ge(turned, i * 4 + (4 + k + 1))
                    dve.tensor_tensor(h[:, k * 512:(k + 1) * 512], h[:, k * 512:(k + 1) * 512], c.bank[:, k, :], ALU.add).then_inc(added, 1)
                dve.wait_ge(summed, i + 1)
                dve.tensor_scalar(stat[:, 1:2], stat[:, 0:1], 1.0 / D, EPS, ALU.mult, ALU.add).then_inc(meaned, 1)
                dve.wait_ge(rooted, i + 1)
                dve.reciprocal(stat[:, 3:4], stat[:, 2:3]).then_inc(inverted, 1)
                dve.wait_ge(inverted, i + 1)
                dve.wait_ge(out_free, i + 1)
                dve.scalar_tensor_tensor(out=out[:, :], in0=h[:, :], scalar=stat[:, 3:4], in1=gain[:, :],
                                         op0=ALU.mult, op1=ALU.mult).then_inc(scaled, 1)

        @block.tensor
        def _(pe):
            pe.sem_inc(turned, 4)
            with pe.Fori(0, TILES) as i:
                pe.wait_ge(y_ready, i + 1)
                for k in range(4):
                    pe.wait_ge(added, i * 4 + (k + 1))
                    for j in range(4):
                        last = pe.transpose(c.bank[:, k, j * P:(j + 1) * P], y_part[:, 4 * k + j, :], c.ident[:, :])
                    last.then_inc(turned, 1)


def build(nc, d):
    c = Chip()
    c.d = d
    with ExitStack() as ctx:
        c.bank = ctx.enter_context(nc.psum_tensor("bank", [P, 8, 512], F32))
        c.act = [ctx.enter_context(nc.sbuf_tensor(name, [P, KC, TOKENS], F32R)) for name in ("act_hi", "act_lo")]
        c.ident = ctx.enter_context(nc.sbuf_tensor("ident", [P, P], F32))
        c.g_attn = ctx.enter_context(nc.sbuf_tensor("g_attn", [P, KC], F32))
        c.g_ffn = ctx.enter_context(nc.sbuf_tensor("g_ffn", [P, KC], F32))
        c.held = ctx.enter_context(nc.semaphore("held"))
        load_constants(nc, c)
        norm_transpose(nc, c, "norm1", d.x, c.g_attn)
        project(nc, c, "proj", d.w_in, 16, d.w_in_tail, d.proj)
        attend(nc, c, "prompt")
        attend(nc, c, "sample")
        project(nc, c, "merge", d.w_out, 8, None, d.h, residual=d.x)
        norm_transpose(nc, c, "norm2", d.h, c.g_ffn)
        with ExitStack() as routing:
            c.picks_t = routing.enter_context(nc.sbuf_tensor("picks_t", [P, 3, TOKENS], F32))
            with nc.sbuf_tensor("query_t", [P, PHEADS, TOKENS], F32) as c.query_t:
                expert_queries(nc, c)
                route(nc, c)
            gate_arrays(nc, c)
        c.y_t = ctx.enter_context(nc.sbuf_tensor("y_t", [P, KC, TOKENS], F32))
        experts(nc, c)
        finish(nc, c)



def _chunk_arrays(T, CL):
    import numpy as np
    s, t = np.arange(T)[:, None], np.arange(T)[None, :]
    same = s // CL == t // CL
    one = lambda m: np.ascontiguousarray(m.astype(np.float32))
    inside = one(same & (s <= t))
    own = one(s // CL == np.arange(T // CL)[None, :])
    return inside / np.float32(TAU), one(same & (s > t)) / np.float32(TAU), own / np.float32(TAU), inside, own


def _trig():
    import math
    import numpy as np
    half = HD // 2
    inv = np.exp(np.float32(-math.log(10000.0)) * np.arange(half, dtype=np.float32) * np.float32(2.0 / HD)).astype(np.float32)
    pos = np.concatenate([np.arange(SEQ), 1024 + np.arange(SAMPLES) % DEC_SEQ]).astype(np.float32)
    ang = (pos[:, None] * inv[None, :]).astype(np.float32)
    return np.concatenate([np.cos(ang), np.sin(ang)], axis=1)


def _masks():
    import numpy as np
    masked = np.float32(-1e30)
    q, s = np.arange(P)[:, None], np.arange(2 * WINDOW)[None, :]
    later = np.where((s > q) & (s <= q + WINDOW), np.float32(0), masked)
    first = np.where(s >= WINDOW, later, masked)
    t, j = np.arange(P)[:, None] % DEC_SEQ, np.arange(DEC_SEQ + WINDOW)[None, :]
    sample = np.where((j > t) & (j <= t + WINDOW), np.float32(0), masked)
    return first.astype(np.float32), later.astype(np.float32), sample.astype(np.float32)


def kernel(**inputs):
    import types
    import numpy as np
    import concourse.bacc as bacc
    from concourse.bass_utils import run_bass_kernel_spmd

    a = {k: np.asarray(x) for k, x in inputs.items()}
    put = np.ascontiguousarray
    x = np.concatenate([a["x_prompt"].reshape(SEQ, D), a["x_sample"].reshape(SAMPLES, D)])
    w = a["w_in"][0]
    ga = 2 * GLA_HEADS * DK + 2 * GLA_HEADS * DV
    w = np.concatenate([w[:, :ga], w[:, ga + GATE_RANK:], w[:, ga:ga + GATE_RANK]], axis=1)

    def slices(m, n):
        return put(m.reshape(KC, P, m.shape[1] // n, n).transpose(2, 1, 0, 3))

    def rows(v):
        return put(np.broadcast_to(v.reshape(1, -1), (P, v.size)))

    tri_p, suf_p, ind_p, inside_p, _ = _chunk_arrays(P, GLA_CHUNK)
    tri_s, suf_s, ind_s, inside_s, own = _chunk_arrays(SAMPLES, DEC_SEQ)
    first, later, sample = _masks()
    sinks = a["attn_sinks"][0]
    by_row = sinks.reshape(KV, PAIRS // KV, 2).transpose(0, 2, 1).reshape(-1)
    arrays = {
        "x": x,
        "w_in": slices(w[:, :16 * NW], NW),
        "w_in_tail": slices(w[:, 16 * NW:], PROJ - 16 * NW)[0],
        "w_out": slices(a["w_out"][0], NW),
        "w_peer_q": slices(a["w_peer_q"][0], P),
        "g_attn": put(a["g_attn"][0].reshape(KC, P).T), "g_ffn": put(a["g_ffn"][0].reshape(KC, P).T),
        "g_out": rows(a["g_gla_out"][0]), "g_final": rows(a["g_final"]),
        "gate_w": np.concatenate([a["w_gate_up"][0], a["b_gate"]], axis=0),
        "sinks_prompt": rows(sinks), "sinks_sample": put(np.repeat(by_row, DEC_SEQ).reshape(P, 1)),
        "cache_k": a["cache_win_k"][0].reshape(DEC_BATCH, WINDOW, KV * HD),
        "cache_v": a["cache_win_v"][0].reshape(DEC_BATCH, WINDOW, KV * HD),
        "state_in": a["state_gla"][0],
        "sub_keys": put(a["peer_sub_keys"][0].transpose(1, 3, 0, 2).reshape(P, PHEADS, N_KEYS)),
        "u_t": put(a["peer_u"][0].reshape(N_KEYS, P, KC, P).transpose(0, 3, 2, 1)),
        "v": a["peer_v"][0],
        "ident": np.eye(P, dtype=np.float32), "trig": _trig(),
        "tri_prompt": tri_p, "suf_prompt": suf_p, "ind_prompt": ind_p, "inside_prompt": inside_p,
        "tri_sample": tri_s, "suf_sample": suf_s, "ind_sample": ind_s, "inside_sample": inside_s, "own": own,
        "mask_prompt": first, "mask_later": later, "mask_sample": sample,
        "rank16": rows(np.arange(TOPK, dtype=np.float32)), "number": rows(np.arange(N_KEYS, dtype=np.float32)),
    }
    arrays = {k: put(v) for k, v in arrays.items()}
    outs = {
        "y": (TOKENS, D),
        "state_out_prompt": (GLA_HEADS, DK, DV), "k_out_prompt": (WINDOW, KV * HD), "v_out_prompt": (WINDOW, KV * HD),
        "state_out_sample": (DEC_BATCH, GLA_HEADS, DK, DV),
        "k_out_sample": (DEC_BATCH, WINDOW, KV * HD), "v_out_sample": (DEC_BATCH, WINDOW, KV * HD),
    }
    scratch = {"proj": (TOKENS, PROJ), "h": (TOKENS, D), "gates": (GROUPS, N_KEYS, N_KEYS, GROUP)}

    nc = bacc.Bacc("TRN2", target_bir_lowering=False, num_devices=1)
    d = types.SimpleNamespace()
    for k, v in arrays.items():
        vars(d)[k] = nc.dram_tensor("in_" + k, v.shape, mybir.dt.from_np(v.dtype), kind="ExternalInput").ap()
    for k, shape in outs.items():
        vars(d)[k] = nc.dram_tensor("out_" + k, shape, F32, kind="ExternalOutput").ap()
    for k, shape in scratch.items():
        vars(d)[k] = nc.dram_tensor(k + "_scratch", shape, F32, kind="Internal").ap()
    d.tri = {"prompt": d.tri_prompt, "sample": d.tri_sample}
    d.suf = {"prompt": d.suf_prompt, "sample": d.suf_sample}
    d.ind = {"prompt": d.ind_prompt, "sample": d.ind_sample}
    d.inside = {"prompt": d.inside_prompt, "sample": d.inside_sample}
    d.sinks = {"prompt": d.sinks_prompt, "sample": d.sinks_sample}
    d.mask = {"prompt": d.mask_prompt, "later": d.mask_later, "sample": d.mask_sample}
    build(nc, d)
    r = run_bass_kernel_spmd(nc, [{"in_" + k: v for k, v in arrays.items()}], core_ids=[0]).results[0]
    y = r["out_y"]
    return (y[:SEQ].reshape(1, SEQ, D), y[SEQ:TOKENS].reshape(DEC_BATCH, DEC_SEQ, D),
            r["out_state_out_prompt"].reshape(1, 1, GLA_HEADS, DK, DV),
            r["out_k_out_prompt"].reshape(1, 1, WINDOW, KV, HD), r["out_v_out_prompt"].reshape(1, 1, WINDOW, KV, HD),
            r["out_state_out_sample"].reshape(1, DEC_BATCH, GLA_HEADS, DK, DV),
            r["out_k_out_sample"].reshape(1, DEC_BATCH, WINDOW, KV, HD),
            r["out_v_out_sample"].reshape(1, DEC_BATCH, WINDOW, KV, HD))
```

```python
from contextlib import ExitStack

import concourse.bass as bass
from concourse import mybir

ALU = mybir.AluOpType
ACT = mybir.ActivationFunctionType
AX_X = mybir.AxisListType.X
F32 = mybir.dt.float32
F32R = mybir.dt.float32r
U32 = mybir.dt.uint32

P = 128
D = 2048
KC = D // P
SEQ = 512
DEC_BATCH, DEC_SEQ = 8, 8
SAMPLES = DEC_BATCH * DEC_SEQ
TOKENS = SEQ + SAMPLES
PROMPT_TILES = SEQ // P
TILES = 5
STRIDE = (TOKENS - P) // (TILES - 1)
W_IN_SLICES = 14
HALF = TOKENS // 2
HI, LO = 0, 1
PASSES = ((HI, HI), (HI, LO), (LO, HI))

GLA_HEADS, DK, DV = 4, 128, 256
GATE_RANK = 16
TAU = 16.0
GLA_CHUNK = 64
SWA_HEADS, HD, KV = 16, 64, 2
PAIRS = SWA_HEADS // 2
WINDOW = 128
EPS = 1e-6

GA0 = 0
Q0 = GA0 + GATE_RANK
K0 = Q0 + GLA_HEADS * DK
V0 = K0 + GLA_HEADS * DK
R0 = V0 + GLA_HEADS * DV
SQ0 = R0 + GLA_HEADS * DV
SK0 = SQ0 + SWA_HEADS * HD
SV0 = SK0 + KV * HD
PROJ = SV0 + KV * HD

N_KEYS = 128
PHEADS = 8
TOPK = 16
SEL = PHEADS * TOPK
NEG = -3.0e38


class Chip:
    pass


def stage(nc):
    ctx = ExitStack()
    sems = []

    def clear():
        nc.clear_and_free_semaphores(sems)
        nc.all_engine_barrier()

    ctx.callback(clear)

    def sb(name, shape, dt=F32):
        return ctx.enter_context(nc.sbuf_tensor(name, shape, dt))

    def sem(name):
        sems.append(nc.alloc_semaphore(name))
        return sems[-1]

    return ctx, sb, sem


def each_tile(eng, turn):
    with eng.Fori(0, TILES // 2) as i:
        for s in range(2):
            turn(i * 2 + s, s, True)
    turn(TILES - 1, 0, False)


def in_pairs(eng, count, step):
    with eng.Fori(0, count // 2 - 1) as i:
        for s in range(2):
            step(i * 2 + s, s, True)
    for s in range(2):
        step(count - 2 + s, s, s == 0)


def product(pe, out, stationary, moving):
    for k in range(KC):
        for n, (a, b) in enumerate(PASSES):
            last = pe.matmul(out, stationary(a, k), moving(b, k), start=(k == 0 and n == 0),
                             stop=(k == KC - 1 and n == len(PASSES) - 1))
    return last


def norm_transpose(nc, c, name, src, gain, weights, first):
    ctx, sb, sem = stage(nc)
    with ctx:
        rows = sb(name + "_rows", [P, 2, D])
        square = sb(name + "_square", [P, D])
        scaled = sb(name + "_scaled", [P, D])
        gained = sb(name + "_gained", [P, KC, P])
        stat = sb(name + "_stat", [P, 2, 4])
        loaded = [sem(f"{name}_loaded{s}") for s in range(2)]
        summed, meaned, rooted, inverted = (sem(name + "_" + s) for s in ("summed", "meaned", "rooted", "inverted"))
        scaled_ready, turned, moved, rounded, split = (
            sem(name + "_" + s) for s in ("scaled_ready", "turned", "moved", "rounded", "split"))
        first_here, first_rounded, first_split = (sem(name + "_first_" + s) for s in ("here", "rounded", "split"))
        const_here = sem(name + "_const_here")
        consts = [(c.ident, c.d.ident), (c.g_attn, c.d.g_attn), (c.g_ffn, c.d.g_ffn)]
        block = ctx.enter_context(nc.Block())
        raw, hi, lo = first

        @block.gpsimd
        def _(pool):
            pool.wait_ge(loaded[0], 16)
            pool.sem_inc(c.held, 1)
            pool.dma_start(raw[:, :, :], weights[0]).then_inc(first_here, 16)
            with pool.Fori(0, TILES - 1) as i:
                pool.wait_ge(first_rounded, i + 1)
                pool.sem_inc(c.held, 1)
                at = slice(None), bass.ds(i * 4, 4), slice(None)
                pool.tensor_tensor(lo[at], raw[at], hi[at].bitcast(F32), ALU.subtract).then_inc(first_split, 1)

        @block.sync
        def _(sp):
            def load(i, s, more):
                sp.wait_ge(scaled_ready, i + 1)
                sp.sem_inc(c.held, 1)
                sp.dma_start(rows[:, s, :], src[bass.ds(i * STRIDE, P), :]).then_inc(loaded[s], 16)

            each_tile(sp, load)

        @block.scalar
        def _(act):
            def root(i, s):
                act.wait_ge(loaded[s], i * 8 + 8 * (2 - s))
                act.activation(square[:, :], rows[:, s, :], ACT.Square, accum_out=stat[:, s, 0:1]).then_inc(summed, 1)
                act.wait_ge(meaned, i + 1)
                act.activation(stat[:, s, 2:3], stat[:, s, 1:2], ACT.Sqrt).then_inc(rooted, 1)

            def turn(i, s, more):
                if more:
                    root(i + 1, 1 - s)
                for k in range(4):
                    act.wait_ge(moved, i * 4 + (k + 5))
                    act.wait_ge(split, i * 4 + (k + 1))
                    act.sem_inc(c.held, 1)
                    act.activation(c.act[HI][:, 4 * k:4 * k + 4, bass.ds(i * STRIDE, P)], gained[:, 4 * k:4 * k + 4, :],
                                   ACT.Copy).then_inc(rounded, 1)
                if more:
                    at = slice(None), bass.ds(i * 4, 4), slice(None)
                    act.wait_ge(first_here, 16)
                    act.sem_inc(c.held, 1)
                    act.activation(hi[at], raw[at], ACT.Copy).then_inc(first_rounded, 1)

            for dst, from_dram in consts:
                act.dma_start(dst[:], from_dram).then_inc(const_here, 16)
            root(0, 0)
            each_tile(act, turn)

        @block.vector
        def _(dve):
            def mean(i, s):
                dve.wait_ge(summed, i + 1)
                dve.tensor_scalar(stat[:, s, 1:2], stat[:, s, 0:1], 1.0 / D, EPS, ALU.mult, ALU.add).then_inc(meaned, 1)

            def scale(i, s):
                dve.wait_ge(rooted, i + 1)
                dve.reciprocal(stat[:, s, 3:4], stat[:, s, 2:3]).then_inc(inverted, 1)
                dve.wait_ge(inverted, i + 1)
                dve.tensor_scalar(scaled[:, :], rows[:, s, :], stat[:, s, 3:4], None, ALU.mult).then_inc(scaled_ready, 1)

            def turn(i, s, more):
                if more:
                    mean(i + 1, 1 - s)
                for k in range(4):
                    dve.wait_ge(turned, i * 4 + (k + 1))
                    dve.wait_ge(split, i * 4 + (k + 1))
                    dve.tensor_tensor(gained[:, 4 * k:4 * k + 4, :], c.bank[:, k, :].rearrange("p (k t) -> p k t", k=4),
                                      gain[:, 4 * k:4 * k + 4].unsqueeze(2).broadcast_to([P, 4, P]),
                                      ALU.mult).then_inc(moved, 1)
                if more:
                    scale(i + 1, 1 - s)
                for k in range(4):
                    dve.wait_ge(rounded, i * 4 + (k + 1))
                    at = (slice(None), slice(4 * k, 4 * k + 4), bass.ds(i * STRIDE, P))
                    dve.tensor_tensor(c.act[LO][at], gained[:, 4 * k:4 * k + 4, :], c.act[HI][at].bitcast(F32),
                                      ALU.subtract).then_inc(split, 1)

            dve.sem_inc(scaled_ready, 2)
            dve.sem_inc(moved, 4)
            dve.sem_inc(split, 4)
            mean(0, 0)
            scale(0, 0)
            dve.wait_ge(const_here, 16 * len(consts))
            dve.sem_inc(c.held, 1)
            each_tile(dve, turn)

        @block.tensor
        def _(pe):
            def turn(i, s, more):
                pe.wait_ge(scaled_ready, i + 3)
                for k in range(4):
                    pe.wait_ge(moved, i * 4 + (k + 1))
                    for j in range(4):
                        n = 4 * k + j
                        last = pe.transpose(c.bank[:, k, j * P:(j + 1) * P], scaled[:, n * P:(n + 1) * P], c.ident[:, :])
                    last.then_inc(turned, 1)

            pe.wait_ge(const_here, 16 * len(consts))
            each_tile(pe, turn)


def project(nc, c, name, weights, first, dst):
    ctx, sb, sem = stage(nc)
    with ctx:
        slices, cols = weights.shape[0], weights.shape[3]
        raw = [first[0], sb(name + "_raw", [P, KC, cols])]
        w = [[first[1 + part], sb(name + tag, [P, KC, cols], F32R)] for part, tag in ((HI, "_hi"), (LO, "_lo"))]
        out = sb(name + "_out", [P, TILES, cols])
        raw_here = [sem(f"{name}_raw_here{s}") for s in range(2)]
        rounded, split = sem(name + "_rounded"), sem(name + "_split")
        stored, out_free = [[sem(f"{name}_{x}{t}") for t in range(TILES)] for x in ("stored", "out_free")]
        summed, moved = sem(name + "_summed"), sem(name + "_moved")
        block = ctx.enter_context(nc.Block())

        @block.sync
        def _(sp):
            def load(n, s, more):
                if more:
                    sp.wait_ge(split, n + 1)
                    sp.sem_inc(c.held, 1)
                    sp.dma_start(raw[1 - s][:, :, :], weights[bass.ds(n + 1, 1)].rearrange("a p k n -> (a p) k n")).then_inc(raw_here[1 - s], 16)

            in_pairs(sp, slices, load)

        @block.gpsimd
        def _(pool):
            def store(n, s, more):
                for t in range(TILES):
                    rows = P if t == TILES - 1 else STRIDE
                    pool.wait_ge(moved, n * TILES + (TILES + t + 1))
                    pool.sem_inc(c.held, 1)
                    pool.dma_start(dst[t * STRIDE:t * STRIDE + rows, bass.ds(n * cols, cols)], out[0:rows, t, :]).then_inc(stored[t], 16)
                for t in range(TILES):
                    pool.wait_ge(stored[t], n * 16 + 16)
                    pool.sem_inc(out_free[t], 1)

            in_pairs(pool, slices, store)

        @block.scalar
        def _(act):
            def hi(n, s, more):
                if more:
                    act.wait_ge(raw_here[1 - s], n * 8 + (16 - 8 * s))
                    act.wait_ge(summed, n * TILES + 2 * TILES)
                    act.activation(w[HI][1 - s][:, :, :], raw[1 - s][:, :, :], ACT.Copy).then_inc(rounded, 1)

            in_pairs(act, slices, hi)

        @block.vector
        def _(dve):
            dve.sem_inc(split, 2)
            dve.sem_inc(moved, TILES)
            for t in range(TILES):
                dve.sem_inc(out_free[t], 1)

            def lo(n, s):
                dve.wait_ge(rounded, n)
                dve.tensor_tensor(w[LO][s][:, :, :], raw[s][:, :, :], w[HI][s][:, :, :].bitcast(F32),
                                  ALU.subtract).then_inc(split, 1)

            def move(n, s, more):
                if more:
                    lo(n + 1, 1 - s)
                for t in range(TILES):
                    dve.wait_ge(out_free[t], n + 1)
                    dve.wait_ge(summed, n * TILES + (2 * TILES + t + 1))
                    dve.tensor_copy(out[:, t, :], c.bank[:, t, 0:cols]).then_inc(moved, 1)

            in_pairs(dve, slices, move)

        @block.tensor
        def _(pe):
            pe.sem_inc(summed, 2 * TILES)

            def products(n, s, more):
                pe.wait_ge(split, n + 2)
                for t in range(TILES):
                    pe.wait_ge(moved, n * TILES + (t + 1))
                    product(pe, c.bank[:, t, 0:cols], lambda part, k: c.act[part][:, k, t * STRIDE:t * STRIDE + P],
                            lambda part, k: w[part][s][:, k, :]).then_inc(summed, 1)

            in_pairs(pe, slices, products)


def merge_heads(nc, c, next_weights, first):
    ctx, sb, sem = stage(nc)
    with ctx:
        raw = sb("mh_raw", [P, 2, KC, P])
        w = [sb("mh" + part, [P, 2, KC, P], F32R) for part in ("_hi", "_lo")]
        h_t = sb("mh_h_t", [P, KC, TOKENS])
        normed_here = sb("mh_normed", [P, 2, 4, TOKENS])
        square = sb("mh_square", [P, 2, TOKENS])
        squares = sb("mh_squares", [P, TOKENS])
        scale = square[:, 0, :]
        ones = sb("mh_ones", [P, P])
        here, h_stored = [[sem(f"mh_{x}{s}") for s in range(2)] for x in ("here", "h_stored")]
        rounded, split, summed, moved = sem("mh_rounded"), sem("mh_split"), sem("mh_summed"), sem("mh_moved")
        squared, tallied, cleared, whole = sem("mh_squared"), sem("mh_tallied"), sem("mh_cleared"), sem("mh_whole")
        meaned, rooted, inverted, scaled = sem("mh_meaned"), sem("mh_rooted"), sem("mh_inverted"), sem("mh_scaled")
        hi_ready, lo_ready, lo_too = sem("mh_hi_ready"), sem("mh_lo_ready"), sem("mh_lo_too")
        block = ctx.enter_context(nc.Block())
        first_here, first_rounded, first_split = (sem("mh_first_" + s) for s in ("here", "rounded", "split"))
        first_raw, first_hi, first_lo = first
        parts = KC // 4

        in_raw = raw[:, :, :, :].rearrange("p s k n -> p (s k n)")[:, 0:4 * TOKENS].rearrange("p (k t) -> p k t", k=4)
        normed = [normed_here[:, 0], normed_here[:, 1], in_raw, normed_here[:, 0]]

        def part(k):
            return slice(None), slice(4 * k, 4 * k + 4), slice(None)

        @block.sync
        def _(sp):
            def load(n, s, more):
                sp.wait_ge(split, n + 1)
                sp.sem_inc(c.held, 1)
                sp.dma_start(raw[:, s], c.d.w_out[bass.ds(n, 1)].rearrange("a p k n -> (a p) k n")).then_inc(here[s], 16)
                sp.sem_inc(c.held, 1)
                sp.dma_start(h_t[:, bass.ds(n, 1), :], c.d.x_t[:, bass.ds(n, 1), :]).then_inc(here[s], 16)

            in_pairs(sp, KC, load)
            sp.dma_start(first_raw[:, :, :], next_weights[0]).then_inc(first_here, 16)

        @block.scalar
        def _(act):
            def hi(n, s):
                act.wait_ge(here[s], n * 16 + 16 * (2 - s))
                act.wait_ge(summed, n * 2 + 2)
                act.activation(w[HI][:, s], raw[:, s], ACT.Copy).then_inc(rounded, 1)

            def step(n, s, more):
                if more:
                    hi(n + 1, 1 - s)
                act.wait_ge(moved, n * 2 + 6)
                act.wait_ge(tallied, n + 1)
                act.sem_inc(c.held, 1)
                act.activation(square[:, s, :].unsqueeze(1), h_t[:, bass.ds(n, 1), :], ACT.Square).then_inc(squared, 1)
                act.sem_inc(c.held, 1)
                act.dma_start(c.d.h_t[:, bass.ds(n, 1), :], h_t[:, bass.ds(n, 1), :]).then_inc(h_stored[s], 16)

            hi(0, 0)
            in_pairs(act, KC, step)
            act.wait_ge(first_here, 16)
            act.activation(first_hi[:, :, :], first_raw[:, :, :], ACT.Copy).then_inc(first_rounded, 1)
            act.wait_ge(meaned, 2)
            act.activation(scale[:, :], scale[:, :], ACT.Sqrt).then_inc(rooted, 1)
            for k in range(parts):
                act.wait_ge(scaled, k + 1)
                act.activation(c.act[HI][part(k)], normed[k], ACT.Copy).then_inc(hi_ready, 1)
            for s in range(2):
                act.wait_ge(h_stored[s], 16 * (KC // 2))

        @block.gpsimd
        def _(pool):
            def lo(n, s):
                pool.wait_ge(rounded, n + 1)
                pool.tensor_tensor(w[LO][:, s], raw[:, s], w[HI][:, s].bitcast(F32), ALU.subtract).then_inc(split, 1)

            def step(n, s, more):
                if more:
                    lo(n + 1, 1 - s)
                pool.wait_ge(squared, n + 1)
                pool.wait_ge(tallied, n + 2)
                pool.sem_inc(c.held, 1)
                pool.tensor_tensor(squares[:, :], squares[:, :], square[:, s, :], ALU.add).then_inc(tallied, 1)

            pool.sem_inc(tallied, 2)
            pool.wait_ge(cleared, 2)
            lo(0, 0)
            in_pairs(pool, KC, step)
            pool.wait_ge(first_rounded, 1)
            pool.tensor_tensor(first_lo[:, :, :], first_raw[:, :, :], first_hi[:, :, :].bitcast(F32), ALU.subtract).then_inc(first_split, 1)
            pool.wait_ge(hi_ready, 2)
            pool.tensor_tensor(c.act[LO][part(1)], normed[1], c.act[HI][part(1)].bitcast(F32), ALU.subtract).then_inc(lo_too, 1)

        @block.vector
        def _(dve):
            def step(n, s, more):
                dve.wait_ge(here[s], n * 16 + 16 * (2 - s))
                for half in range(2):
                    dve.wait_ge(summed, n * 2 + (4 + half + 1))
                    dve.sem_inc(c.held, 1)
                    columns = h_t[:, bass.ds(n, 1), half * HALF:(half + 1) * HALF]
                    dve.tensor_tensor(columns, c.bank[:, 2 * s + half, 0:HALF].unsqueeze(1), columns, ALU.add).then_inc(moved, 1)

            dve.memset(squares[:, :], 0.0).then_inc(cleared, 1)
            dve.memset(ones[:, :], 1.0).then_inc(cleared, 1)
            dve.sem_inc(split, 2)
            dve.sem_inc(moved, 4)
            in_pairs(dve, KC, step)
            for half in range(2):
                dve.wait_ge(whole, half + 1)
                dve.tensor_scalar(scale[:, half * HALF:(half + 1) * HALF], c.bank[:, 4 + half, 0:HALF], 1.0 / D, EPS,
                                  ALU.mult, ALU.add).then_inc(meaned, 1)
            dve.wait_ge(rooted, 1)
            dve.reciprocal(scale[:, :], scale[:, :]).then_inc(inverted, 1)
            dve.wait_ge(inverted, 1)
            def lo(k):
                dve.wait_ge(hi_ready, k + 1)
                dve.tensor_tensor(c.act[LO][part(k)], normed[k], c.act[HI][part(k)].bitcast(F32), ALU.subtract).then_inc(lo_ready, 1)

            for k in range(parts):
                if k == 3:
                    dve.wait_ge(lo_ready, 1)
                for j in range(4):
                    n = 4 * k + j
                    last = dve.scalar_tensor_tensor(out=normed[k][:, j, :], in0=h_t[:, n, :], scalar=c.g_ffn[:, n:n + 1], in1=scale[:, :],
                                                    op0=ALU.mult, op1=ALU.mult)
                last.then_inc(scaled, 1)
                if k % 2:
                    lo(k - 1)
            lo(parts - 1)

        @block.tensor
        def _(pe):
            def step(n, s, more):
                pe.wait_ge(split, n + 3)
                for half in range(2):
                    pe.wait_ge(moved, n * 2 + (half + 1))
                    product(pe, c.bank[:, 2 * s + half, 0:HALF], lambda part, k: w[part][:, s, k, :],
                            lambda part, k: c.act[part][:, k, half * HALF:(half + 1) * HALF]).then_inc(summed, 1)

            pe.sem_inc(summed, 4)
            in_pairs(pe, KC, step)
            pe.wait_ge(cleared, 2)
            pe.wait_ge(tallied, KC + 2)
            for half in range(2):
                pe.matmul(c.bank[:, 4 + half, 0:HALF], ones[:, :], squares[:, half * HALF:(half + 1) * HALF],
                          start=True, stop=True).then_inc(whole, 1)


def attend(nc, c, kind):
    prompt = kind == "prompt"
    turns = PROMPT_TILES if prompt else 1
    T = P if prompt else SAMPLES
    CL = GLA_CHUNK if prompt else DEC_SEQ
    NC = T // CL
    NB = SWA_HEADS if prompt else DEC_BATCH
    KW = 2 * WINDOW if prompt else DEC_SEQ + WINDOW
    ctx, sb_, sem_ = stage(nc)
    per = {}

    def sb(name, shape, dt=F32):
        return sb_(kind + "_" + name, shape, dt)

    def sem(name, n=1):
        s = sem_(kind + "_" + name)
        per[id(s)] = n
        return s

    with ctx:
        cur = sb("cur", [P, PROJ])
        tri = sb("tri", [T, T])
        suf = sb("suf", [T, T])
        ind = sb("ind", [T, NC])
        inside = sb("inside", [T, T])
        gate_w = sb("gate_w", [GATE_RANK + 1, GLA_HEADS * DK])
        ga_t = sb("ga_t", [GATE_RANK + 1, T])
        low = sb("low", [T, 512])
        mag = sb("mag", [T, 512])
        log_a = sb("log_a", [T, 512])
        eb = sb("eb", [T, 512])
        enb = sb("enb", [T, 512])
        ebd = sb("ebd", [T, 512])
        qg, kg, ke = eb, enb, ebd
        decay = sb("decay", [P, GLA_HEADS, NC])
        qg_t = sb("qg_t", [P, GLA_HEADS, T])
        kg_t = sb("kg_t", [P, GLA_HEADS, T])
        q_spread = sb("q_spread", [P, GLA_HEADS, NC * (T + CL)])
        inner = sb("inner", [T, GLA_HEADS, T])
        o_stat = sb("o_stat", [T, 4, GLA_HEADS])
        o_norm = sb("o_norm", [T, GLA_HEADS * DV])
        g_out = sb("g_out", [P, DV])
        er = sb("er", [T, GLA_HEADS * DV])
        silu, log1, o_junk = er, mag, low[:, 0:DV]
        state = sb("state", [P, 2 if prompt else NC, GLA_HEADS, DV])
        if not prompt:
            own = sb("own", [T, NC])
            spare = sb("spare", [P, 2 * NC * DK])
            k_own = spare[0:T, :].rearrange("t (a n d) -> t a n d", a=2, n=NC)
            probs_t = spare[:, 0:NB * P].rearrange("p (b q) -> p b q", b=NB)
            probs_old_t = spare[0:DEC_SEQ, NB * P:2 * NB * P].rearrange("p (b q) -> p b q", b=NB)
        trig = sb("trig", [P, HD])
        roped = sb("roped", [P, SWA_HEADS + KV, HD])
        rt = [sb(f"rt{n}", [P, SWA_HEADS + KV, HD // 2]) for n in range(2)]
        k_twice = sb("k_twice", [P, KV, 2, HD])
        q_t = sb("q_t", [P, PAIRS, T])
        sinks = sb("sinks", [P, NB if prompt else 1])
        mask = sb("mask", [P, KW])
        scores = sb("scores", [P, NB, KW])
        st = sb("st", [P, 6, NB])
        if prompt:
            mask_all = sb("mask_all", [P, KW])
            k_t = sb("k_t", [P, KV, KW])
            v_before = sb("v_before", [P, KV * HD])
            probs_t = sb("probs_t", [P, NB, 2, P])
        else:
            k_t = q_spread[:, :, :].rearrange("p h x -> p (h x)")[:, 0:NB * KV * KW].rearrange("p (b g k) -> p b g k", b=NB, g=KV)
            k_new = sb("k_new", [P, NB, KV * HD])
            v_new = sb("v_new", [P, NB, KV * HD])
            k_old = sb("k_old", [DEC_SEQ, NB, KV * HD])
            v_old = sb("v_old", [DEC_SEQ, NB, KV * HD])
            k2 = sb("k2", [P, 2, KV, 2, HD])
            k2_old = sb("k2_old", [DEC_SEQ, 2, KV, 2, HD])

        const_here = sem("const_here")
        qk_here, vr_here, s_here, sv_here = sem("qk_here", 16), sem("vr_here", 16), sem("s_here", 32), sem("sv_here", 16)
        ga_turned, ga_ready = sem("ga_turned"), sem("ga_ready")
        gate_ready, low_ready, mag_ready = sem("gate_ready"), sem("low_ready"), sem("mag_ready")
        exp1_ready, log1_ready, log_a_ready = sem("exp1_ready"), sem("log1_ready"), sem("log_a_ready")
        sums_ready, exps_ready, gated = sem("sums_ready"), sem("exps_ready", 4), sem("gated", 3)
        gated_turned, qk_ready = sem("gated_turned", 2), sem("qk_ready", 3)
        inner_ready, inner_masked = sem("inner_ready"), sem("inner_masked")
        grown, state_ready = sem("grown", 2 if prompt else 2 * GLA_HEADS), sem("state_ready", 2 if prompt else 2 * GLA_HEADS)
        k_own_ready = sem("k_own_ready", GLA_HEADS)
        o_ready, o_summed, o_meaned, o_rooted = sem("o_ready"), sem("o_summed", GLA_HEADS), sem("o_meaned"), sem("o_rooted")
        o_inverted, o_normed = sem("o_inverted"), sem("o_normed", GLA_HEADS)
        er_ready, er_one, er_inverted, silu_ready = sem("er_ready"), sem("er_one"), sem("er_inverted"), sem("silu_ready")
        o_gated, o_turned, gla_heads_ready = sem("o_gated"), sem("o_turned", 2), sem("gla_heads_ready", 2)
        gla_rounded, swa_rounded = sem("gla_rounded", 2), sem("swa_rounded", 2 if prompt else 1)
        rope_step, k_twice_ready = sem("rope_step", 6), sem("k_twice_ready")
        q_turned, q_t_ready = sem("q_turned"), sem("q_t_ready", 2 if prompt else 1)
        k_turned, k_t_ready = sem("k_turned", 1 if prompt else NB), sem("k_t_ready", 1 if prompt else NB)
        SB = 4 if prompt else 2
        scored, score_moved = sem("scored", NB // SB), sem("score_moved", NB)
        topped, negated, sunk = sem("topped"), sem("negated"), sem("sunk")
        exped, sink_exped, totalled, inverted = sem("exped", NB), sem("sink_exped"), sem("totalled"), sem("inverted")
        weighted, p_turned = sem("weighted", 2), sem("p_turned", NB // 2)
        p_ready = [sem("p_ready_even", NB // 4), sem("p_ready_odd", NB // 4)]
        mixed, swa_heads_ready = sem("mixed"), sem("swa_heads_ready", 2 if prompt else 1)
        kept, stored = sem("kept", 3), sem("stored")

        new_here = sem("new_here", 32 * NB)
        old_here = sem("old_here", 16 * 5)
        first_ready = sem("first_ready")

        k2_ready = sem("k2_ready", NB)

        block = ctx.enter_context(nc.Block())
        b0, b2, b3, b7 = (c.bank[:, n, :] for n in (0, 2, 3, 7))

        def wait(eng, s, i, n=None):
            eng.wait_ge(s, i * per[id(s)] + (per[id(s)] if n is None else n))

        def end_turn(eng, i):
            for s in (gla_heads_ready, swa_heads_ready, kept, state_ready):
                wait(eng, s, i)
                eng.sem_inc(c.held, 1)

        def loop(eng, body):
            if prompt:
                with eng.Fori(0, turns) as i:
                    body(i)
                    end_turn(eng, i)
            else:
                body(0)

        def tokens(i):
            return bass.ds(i * P, P) if prompt else slice(SEQ, TOKENS)

        consts = [(tri, c.d.tri[kind]), (suf, c.d.suf[kind]), (ind, c.d.ind[kind]), (inside, c.d.inside[kind]),
                  (gate_w, c.d.gate_w), (g_out, c.d.g_out), (sinks, c.d.sinks[kind]), (mask, c.d.mask[kind])]
        if prompt:
            consts += [(mask_all, c.d.mask["later"])]
        else:
            consts += [(own, c.d.own)]
            ck, cv = c.d.cache_k, c.d.cache_v

        all_consts = 16 * len(consts)

        if prompt:
            swa_out = [(slice(PAIRS + 4 * n, PAIRS + 4 * n + 4), c.bank[:, n, :].rearrange("p (k t) -> p k t", k=4)) for n in range(2)]
        else:
            swa_out = [(slice(PAIRS, 2 * PAIRS), c.bank[:, 0, :].rearrange("p (k t) -> p k t", k=PAIRS))]

        P_BANK = 4 if prompt else 3
        O_BANK = 2 if prompt else 6

        def score_bank(n):
            if prompt:
                return c.bank[:, 3 + n // 4 % 2 * 2 + n % 2, n // 2 % 2 * KW:(n // 2 % 2 + 1) * KW]
            return c.bank[:, 3 + n // 2 % 4, n % 2 * 256:n % 2 * 256 + KW]

        def move_probs(eng, i, n):
            wait(eng, p_turned, i, n + 1)
            src = c.bank[:, P_BANK + n % 4, :].rearrange("p (a b q) -> p a b q", a=2, b=2)
            if not prompt:
                nc.scalar.activation(probs_t[:, 2 * n:2 * n + 2, :], src[:, :, 0, :], ACT.Copy)
                nc.scalar.activation(probs_old_t[:, 2 * n:2 * n + 2, :], src[0:DEC_SEQ, :, 1, :], ACT.Copy).then_inc(p_ready[n % 2], 1)
            elif n % 2:
                nc.vector.tensor_copy(probs_t[:, 2 * n:2 * n + 2, :, :], src).then_inc(p_ready[1], 1)
            else:
                nc.scalar.activation(probs_t[:, 2 * n:2 * n + 2, :, :], src, ACT.Copy).then_inc(p_ready[0], 1)

        def new_state(dve, i, h):
            wait(dve, o_ready, i)
            for b in range(NC):
                if b % (NC // 2) == 0:
                    wait(dve, grown, i, 2 * h + (1 if b == 0 else 2))
                ins = dve.scalar_tensor_tensor(out=state[:, b, h, :], in0=state[:, b, h, :], scalar=decay[:, h, b:b + 1],
                                               in1=c.bank[:, 4 + b // 2, (b % 2) * DV:(b % 2 + 1) * DV],
                                               op0=ALU.mult, op1=ALU.add)
                if b % (NC // 2) == NC // 2 - 1:
                    ins.then_inc(state_ready, 1)

        def move_keys(dve, i, b):
            wait(dve, k_turned, i, b + 1)
            bank = c.bank[:, 1 + b % 2, :]
            dve.tensor_copy(k_t[:, b, :, DEC_SEQ:KW], bank[:, 0:KV * P].rearrange("p (g t) -> p g t", g=KV))
            dve.tensor_copy(k_t[:, b, :, 0:DEC_SEQ],
                            bank[:, KV * P:KV * P + KV * DEC_SEQ].rearrange("p (g t) -> p g t", g=KV)).then_inc(k_t_ready, 1)

        @block.sync
        def _(sp):
            def load(t, dst, src, here, first, end):
                at = bass.ds(t * P, P) if prompt else slice(SEQ, TOKENS)
                sp.sem_inc(c.held, 1)
                sp.dma_start(dst[0:T, first:end], src[at, first:end]).then_inc(here, 16)

            def load_swa(t):
                load(t, cur, c.d.proj, s_here, SQ0, SV0)
                load(t, trig, c.d.trig, s_here, 0, HD)

            load(0, cur, c.d.proj, qk_here, GA0, V0)
            load_swa(0)
            load(0, cur, c.d.proj, vr_here, V0, SQ0)
            load(0, cur, c.d.proj, sv_here, SV0, PROJ)
            if prompt:
                with sp.Fori(0, turns - 1) as i:
                    wait(sp, rope_step, i)
                    load_swa(i + 1)
                    wait(sp, gated, i)
                    wait(sp, er_ready, i)
                    load(i + 1, cur, c.d.proj, qk_here, GA0, V0)
                    wait(sp, o_ready, i)
                    wait(sp, silu_ready, i)
                    load(i + 1, cur, c.d.proj, vr_here, V0, SQ0)
                    wait(sp, kept, i)
                    load(i + 1, cur, c.d.proj, sv_here, SV0, PROJ)
                for s in (gla_heads_ready, swa_heads_ready, kept, state_ready):
                    wait(sp, s, turns - 1)
            else:
                sp.wait_ge(const_here, all_consts)
                sp.wait_ge(vr_here, 16)
                sp.sem_inc(c.held, 1)
                sp.dma_start(state[:], c.d.state_in.rearrange("b h d v -> d b h v")).then_inc(old_here, 16)
                for dst, src in ((k_old, ck), (v_old, cv)):
                    sp.dma_start(dst[:], src[:, 0:DEC_SEQ, :].rearrange("b t f -> t b f")).then_inc(old_here, 16)
                for dst, src in ((k_new, ck), (v_new, cv)):
                    sp.dma_start(dst[0:WINDOW - DEC_SEQ, :, :],
                                 src[:, DEC_SEQ:WINDOW, :].rearrange("b t f -> t b f")).then_inc(old_here, 16)
            if prompt:
                sp.dma_start(c.d.k_out_prompt, roped[:, SWA_HEADS:SWA_HEADS + KV, :].rearrange("t g d -> t (g d)")).then_inc(stored, 16)
                sp.dma_start(c.d.v_out_prompt, cur[:, SV0:SV0 + KV * HD]).then_inc(stored, 16)
                sp.dma_start(c.d.state_out_prompt.rearrange("h d v -> d h v"), state[:, 0, :, :]).then_inc(stored, 16)
                sp.wait_ge(stored, 48)
            else:
                wait(sp, rope_step, 0)
                wait(sp, sv_here, 0)
                sp.sem_inc(c.held, 1)
                for b in range(NB):
                    rows = slice(b * DEC_SEQ, (b + 1) * DEC_SEQ)
                    sp.dma_start(k_new[WINDOW - DEC_SEQ:WINDOW, b, :],
                                 roped[rows, SWA_HEADS:SWA_HEADS + KV, :].rearrange("t g d -> t (g d)")).then_inc(new_here, 16)
                    sp.dma_start(v_new[WINDOW - DEC_SEQ:WINDOW, b, :], cur[rows, SV0:SV0 + KV * HD]).then_inc(new_here, 16)
                sp.wait_ge(new_here, 32 * NB)
                sp.wait_ge(old_here, 16 * 5)
                sp.dma_start(c.d.k_out_sample.rearrange("b t f -> t b f"), k_new[:, :, :]).then_inc(stored, 16)
                sp.dma_start(c.d.v_out_sample.rearrange("b t f -> t b f"), v_new[:, :, :]).then_inc(stored, 16)
                wait(sp, state_ready, 0)
                sp.dma_start(c.d.state_out_sample.rearrange("b h d v -> d b h v"), state[:, :, :, :]).then_inc(stored, 16)
                sp.wait_ge(stored, 48)

        @block.gpsimd
        def _(pool):
            if prompt:
                pool.memset(v_before[:, :], 0.0).then_inc(first_ready, 1)
            half = HD // 2
            heads = SWA_HEADS + KV

            def rope(i):
                wait(pool, s_here, i)
                pool.sem_inc(c.held, 1)
                x = cur[0:T, SQ0:SQ0 + heads * HD].rearrange("t (h d) -> t h d", d=HD)
                x1, x2 = x[:, :, 0:half], x[:, :, half:HD]
                cos = trig[0:T, 0:half].unsqueeze(1).broadcast_to([T, heads, half])
                sin = trig[0:T, half:HD].unsqueeze(1).broadcast_to([T, heads, half])
                t0, t1 = rt[0][0:T], rt[1][0:T]
                out1, out2 = roped[0:T, :, 0:half], roped[0:T, :, half:HD]
                steps = [(t0, x1, cos, ALU.mult), (t1, x2, sin, ALU.mult), (out1, t0, t1, ALU.subtract),
                         (t0, x2, cos, ALU.mult), (t1, x1, sin, ALU.mult), (out2, t0, t1, ALU.add)]
                for n, (o, a, b, op) in enumerate(steps):
                    if n:
                        wait(pool, rope_step, i, n)
                        pool.sem_inc(c.held, 1)
                    pool.tensor_tensor(o, a, b, op).then_inc(rope_step, 1)
                wait(pool, rope_step, i)
                pool.sem_inc(c.held, 1)
                if prompt:
                    keys = roped[:, SWA_HEADS:heads, :]
                    pool.tensor_copy(k_twice[:, :, 0, :], keys)
                    pool.tensor_copy(k_twice[:, :, 1, :], keys).then_inc(k_twice_ready, 1)

            def weigh_gla(i):
                wait(pool, er_inverted, i)
                wait(pool, vr_here, i)
                pool.sem_inc(c.held, 1)
                pool.tensor_tensor(silu[:, :], cur[0:T, R0:R0 + GLA_HEADS * DV], er[:, :], ALU.mult).then_inc(silu_ready, 1)

            def weigh_swa(i):
                wait(pool, inverted, i)
                wait(pool, exped, i)
                pool.sem_inc(c.held, 1)
                for n in range(2):
                    blocks = slice(n * NB // 2, (n + 1) * NB // 2)
                    pool.tensor_tensor(scores[:, blocks, :], scores[:, blocks, :],
                                       st[:, 5, blocks].unsqueeze(2).broadcast_to([P, NB // 2, KW]), ALU.mult).then_inc(weighted, 1)

            def turn(i, more):
                if more:
                    wait(pool, q_turned, i)
                    wait(pool, k_turned, i)
                    pool.sem_inc(c.held, 1)
                    rope(i + 1)
                weigh_swa(i)
                weigh_gla(i)
                wait(pool, mixed, i)
                wait(pool, sv_here, i)
                pool.sem_inc(c.held, 1)
                pool.tensor_copy(v_before[:, :], cur[:, SV0:SV0 + KV * HD]).then_inc(kept, 1)
                pool.tensor_copy(k_t[:, :, 0:WINDOW], k_t[:, :, WINDOW:KW]).then_inc(kept, 1)
                pool.tensor_copy(mask[:, :], mask_all[:, :]).then_inc(kept, 1)
                end_turn(pool, i)

            rope(0)
            if prompt:
                with pool.Fori(0, turns - 1) as i:
                    turn(i, True)
                turn(turns - 1, False)
            else:
                weigh_gla(0)
                weigh_swa(0)

        @block.scalar
        def _(act):
            for dst, src in consts:
                act.dma_start(dst[:], src).then_inc(const_here, 16)
            act.wait_ge(const_here, all_consts)
            act.sem_inc(c.held, 1)

            def gates(i):
                wait(act, mag_ready, i)
                act.activation(log1[:, :], mag[:, :], ACT.Exp).then_inc(exp1_ready, 1)
                wait(act, vr_here, i)
                act.activation(er[:, :], cur[0:T, R0:R0 + GLA_HEADS * DV], ACT.Exp, scale=-1.0).then_inc(er_ready, 1)
                wait(act, exp1_ready, i)
                act.activation(log1[:, :], log1[:, :], ACT.Ln, bias=1.0).then_inc(log1_ready, 1)
                wait(act, sums_ready, i)
                act.activation(eb[:, :], b2[0:T, :], ACT.Exp).then_inc(exps_ready, 1)
                act.activation(enb[:, :], b2[0:T, :], ACT.Exp, scale=-1.0).then_inc(exps_ready, 1)
                act.activation(ebd[:, :], b3[0:T, :], ACT.Exp).then_inc(exps_ready, 1)
                act.activation(decay[:, :, :], b0[:, 0:GLA_HEADS * NC].rearrange("p (h n) -> p h n", h=GLA_HEADS), ACT.Exp).then_inc(exps_ready, 1)
                wait(act, gated_turned, i)
                act.activation(kg_t[:, :, :], c.bank[:, 5, 0:GLA_HEADS * T].rearrange("p (h t) -> p h t", h=GLA_HEADS), ACT.Copy).then_inc(qk_ready, 1)

            def norms(i):
                wait(act, o_ready, i)
                for h in range(GLA_HEADS):
                    if h:
                        wait(act, o_summed, i, h)
                    act.activation(o_junk, c.bank[0:T, 2 + h // 2, (h % 2) * DV:(h % 2 + 1) * DV], ACT.Square,
                                   accum_out=o_stat[:, 0, h:h + 1]).then_inc(o_summed, 1)
                wait(act, o_meaned, i)
                act.activation(o_stat[:, 2, :], o_stat[:, 1, :], ACT.Sqrt).then_inc(o_rooted, 1)

            def gla_hi(i):
                wait(act, o_turned, i)
                act.sem_inc(c.held, 1)
                for n in range(2):
                    act.activation(c.act[HI][:, 4 * n:4 * n + 4, tokens(i)],
                                   c.bank[:, O_BANK + n, 0:4 * T].rearrange("p (k t) -> p k t", k=4), ACT.Copy).then_inc(gla_rounded, 1)

            def queries(i):
                wait(act, q_turned, i)
                if prompt:
                    for n in range(2):
                        act.activation(q_t[:, 4 * n:4 * n + 4, :], c.bank[:, n, :].rearrange("p (k t) -> p k t", k=4), ACT.Copy,
                                       scale=HD ** -0.5).then_inc(q_t_ready, 1)
                else:
                    act.activation(q_t[:, :, :].rearrange("p k t -> p (k t)").rearrange("p (b k t) -> p k b t", b=NB, k=PAIRS),
                                   b0.rearrange("p (k b t) -> p k b t", b=NB, k=PAIRS), ACT.Copy,
                                   scale=HD ** -0.5).then_inc(q_t_ready, 1)

            def score_exps(i):
                wait(act, negated, i)
                for n in range(NB):
                    act.activation(scores[:, n, :], scores[:, n, :], ACT.Exp, bias=st[:, 2, n:n + 1],
                                   accum_out=st[:, 3, n:n + 1]).then_inc(exped, 1)
                wait(act, sunk, i)
                act.activation(st[:, 4, :], st[:, 4, :], ACT.Exp).then_inc(sink_exped, 1)

            def probs(i):
                for n in range(NB // 2):
                    if n % 2 == 0 or not prompt:
                        move_probs(act, i, n)

            def swa_hi(i):
                wait(act, mixed, i)
                act.sem_inc(c.held, 1)
                for at, src in swa_out:
                    act.activation(c.act[HI][:, at, tokens(i)], src, ACT.Copy).then_inc(swa_rounded, 1)

            def body(i):
                order = (queries, gates, score_exps, norms, probs, gla_hi, swa_hi) if prompt else (
                    gates, norms, gla_hi, queries, score_exps, probs, swa_hi)
                for part in order:
                    part(i)

            loop(act, body)

        @block.vector
        def _(dve):
            dve.memset(ga_t[:, :], 1.0).then_inc(first_ready, 1)
            dve.memset(q_spread[:, :, :], 0.0).then_inc(first_ready, 1)
            if prompt:
                dve.memset(state[:, 0, :, :], 0.0).then_inc(first_ready, 1)
                dve.memset(k_t[:, :, 0:WINDOW], 0.0).then_inc(first_ready, 1)
            dve.wait_ge(const_here, all_consts)
            dve.wait_ge(first_ready, 5 if prompt else 2)
            dve.sem_inc(c.held, 1)

            sink_row = sinks[:, :] if prompt else sinks[:, :].broadcast_to([P, NB])

            def gate_logs_in(i):
                wait(dve, ga_turned, i)
                dve.tensor_copy(ga_t[0:GATE_RANK, :], b7[0:GATE_RANK, 0:T]).then_inc(ga_ready, 1)
                wait(dve, gate_ready, i)
                dve.tensor_scalar(low[:, :], b7[0:T, :], 0.0, None, ALU.min).then_inc(low_ready, 1)
                wait(dve, low_ready, i)
                dve.scalar_tensor_tensor(out=mag[:, :], in0=low[:, :], scalar=2.0, in1=b7[0:T, :],
                                         op0=ALU.mult, op1=ALU.subtract).then_inc(mag_ready, 1)

            def gate_logs(i):
                wait(dve, log1_ready, i)
                dve.tensor_tensor(log_a[:, :], low[:, :], log1[:, :], ALU.subtract).then_inc(log_a_ready, 1)

            def output_gates(i):
                wait(dve, er_ready, i)
                dve.tensor_scalar(er[:, :], er[:, :], 1.0, None, ALU.add).then_inc(er_one, 1)
                wait(dve, er_one, i)
                dve.reciprocal(er[:, :], er[:, :]).then_inc(er_inverted, 1)

            def linear_attention(i):
                wait(dve, exps_ready, i)
                dve.scalar_tensor_tensor(out=qg[:, :], in0=cur[0:T, Q0:Q0 + 512], scalar=DK ** -0.5, in1=eb[:, :],
                                         op0=ALU.mult, op1=ALU.mult).then_inc(gated, 1)
                dve.tensor_tensor(kg[:, :], cur[0:T, K0:K0 + 512], enb[:, :], ALU.mult).then_inc(gated, 1)
                dve.tensor_tensor(ke[:, :], cur[0:T, K0:K0 + 512], ebd[:, :], ALU.mult).then_inc(gated, 1)
                wait(dve, gated_turned, i, 1)
                q_bank = c.bank[:, 4, 0:GLA_HEADS * T].rearrange("p (h t) -> p h t", h=GLA_HEADS)
                dve.tensor_copy(qg_t[:, :, :], q_bank).then_inc(qk_ready, 1)
                for h in range(GLA_HEADS):
                    ins = dve.tensor_copy(q_spread[:, h, :].rearrange("p (n x) -> p n x", n=NC)[:, :, 0:CL],
                                          q_bank[:, h, :].rearrange("p (n x) -> p n x", n=NC))
                ins.then_inc(qk_ready, 1)
                wait(dve, inner_ready, i)
                dve.tensor_tensor(inner[:, :, :], c.bank[0:T, 6, 0:GLA_HEADS * T].rearrange("p (h t) -> p h t", h=GLA_HEADS),
                                  inside[:, :].unsqueeze(1).broadcast_to([T, GLA_HEADS, T]), ALU.mult).then_inc(inner_masked, 1)
                if prompt:
                    wait(dve, grown, i, 1)
                    for h in range(GLA_HEADS):
                        ins = dve.scalar_tensor_tensor(out=state[:, 1, h, :], in0=state[:, 0, h, :], scalar=decay[:, h, 0:1],
                                                       in1=c.bank[:, 4 + h // 2, (h % 2) * DV:(h % 2 + 1) * DV],
                                                       op0=ALU.mult, op1=ALU.add)
                    ins.then_inc(state_ready, 1)
                else:
                    for h in range(GLA_HEADS):
                        if h >= 2:
                            wait(dve, grown, i, 2 * (h - 1))
                        dve.tensor_tensor(k_own[:, h % 2, :, :],
                                          ke[:, h * DK:(h + 1) * DK].unsqueeze(1).broadcast_to([T, NC, DK]),
                                          own[:, :].unsqueeze(2).broadcast_to([T, NC, DK]), ALU.mult).then_inc(k_own_ready, 1)
                        if h >= 1:
                            new_state(dve, i, h - 1)
                    new_state(dve, i, GLA_HEADS - 1)

            def norms(i):
                wait(dve, o_summed, i)
                dve.tensor_scalar(o_stat[:, 1, :], o_stat[:, 0, :], 1.0 / DV, EPS, ALU.mult, ALU.add).then_inc(o_meaned, 1)
                if prompt:
                    wait(dve, grown, i, 2)
                    wait(dve, o_ready, i)
                    for h in range(GLA_HEADS):
                        ins = dve.scalar_tensor_tensor(out=state[:, 0, h, :], in0=state[:, 1, h, :], scalar=decay[:, h, 1:2],
                                                       in1=c.bank[:, h // 2, (h % 2) * DV:(h % 2 + 1) * DV],
                                                       op0=ALU.mult, op1=ALU.add)
                    ins.then_inc(state_ready, 1)
                wait(dve, o_rooted, i)
                dve.reciprocal(o_stat[:, 3, :], o_stat[:, 2, :]).then_inc(o_inverted, 1)
                wait(dve, o_inverted, i)
                for h in range(GLA_HEADS):
                    dve.scalar_tensor_tensor(out=o_norm[:, h * DV:(h + 1) * DV],
                                             in0=c.bank[0:T, 2 + h // 2, (h % 2) * DV:(h % 2 + 1) * DV],
                                             scalar=o_stat[:, 3, h:h + 1], in1=g_out[0:T, :],
                                             op0=ALU.mult, op1=ALU.mult).then_inc(o_normed, 1)
                wait(dve, silu_ready, i)
                wait(dve, o_normed, i)
                dve.tensor_tensor(o_norm[:, :], o_norm[:, :], silu[:, :], ALU.mult).then_inc(o_gated, 1)

            def gla_lo(i):
                wait(dve, gla_rounded, i)
                dve.sem_inc(c.held, 1)
                for n in range(2):
                    at = (slice(None), slice(4 * n, 4 * n + 4), tokens(i))
                    dve.tensor_tensor(c.act[LO][at], c.bank[:, O_BANK + n, 0:4 * T].rearrange("p (k t) -> p k t", k=4),
                                      c.act[HI][at].bitcast(F32), ALU.subtract).then_inc(gla_heads_ready, 1)

            def keys(i):
                if prompt:
                    wait(dve, k_turned, i)
                    dve.tensor_copy(k_t[:, :, WINDOW:KW], c.bank[:, 2, 0:KV * P].rearrange("p (g t) -> p g t", g=KV)).then_inc(k_t_ready, 1)
                else:
                    dve.wait_ge(new_here, 32 * NB)
                    wait(dve, old_here, i)
                    dve.sem_inc(c.held, 1)
                    for b in range(NB):
                        if b >= 2:
                            wait(dve, k_turned, i, b - 1)
                        fresh = k_new[:, b, :].rearrange("t (g d) -> t g d", g=KV)
                        old = k_old[:, b, :].rearrange("t (g d) -> t g d", g=KV)
                        for twice in range(2):
                            dve.tensor_copy(k2[:, b % 2, :, twice, :], fresh)
                            ins = dve.tensor_copy(k2_old[:, b % 2, :, twice, :], old)
                        ins.then_inc(k2_ready, 1)
                        if b:
                            move_keys(dve, i, b - 1)
                    move_keys(dve, i, NB - 1)

            def move_scores(i, blocks):
                for n in blocks:
                    wait(dve, scored, i, n // SB + 1)
                    dve.sem_inc(c.held, 1)
                    dve.tensor_tensor_reduce(out=scores[:, n, :], in0=score_bank(n),
                                             in1=mask[:, :], scale=1.0, scalar=NEG, op0=ALU.add, op1=ALU.max,
                                             accum_out=st[:, 0, n:n + 1]).then_inc(score_moved, 1)

            def tops(i):
                wait(dve, score_moved, i)

                dve.tensor_tensor(st[:, 1, :], st[:, 0, :], sink_row, ALU.max).then_inc(topped, 1)
                wait(dve, topped, i)
                dve.tensor_scalar(st[:, 2, :], st[:, 1, :], -1.0, None, ALU.mult).then_inc(negated, 1)
                dve.tensor_tensor(st[:, 4, :], sink_row, st[:, 1, :], ALU.subtract).then_inc(sunk, 1)

            def totals(i):
                wait(dve, exped, i)
                wait(dve, sink_exped, i)
                dve.tensor_tensor(st[:, 3, :], st[:, 3, :], st[:, 4, :], ALU.add).then_inc(totalled, 1)
                wait(dve, totalled, i)
                dve.reciprocal(st[:, 5, :], st[:, 3, :]).then_inc(inverted, 1)

            def swa_lo(i):
                wait(dve, swa_rounded, i)
                dve.sem_inc(c.held, 1)
                for at, src in swa_out:
                    dve.tensor_tensor(c.act[LO][:, at, tokens(i)], src, c.act[HI][:, at, tokens(i)].bitcast(F32),
                                      ALU.subtract).then_inc(swa_heads_ready, 1)

            def body(i):
                if prompt:
                    gate_logs_in(i)
                    keys(i)
                    move_scores(i, range(NB // 2))
                    gate_logs(i)
                    move_scores(i, range(NB // 2, NB))
                    tops(i)
                    linear_attention(i)
                    totals(i)
                    output_gates(i)
                    norms(i)
                    for n in range(1, NB // 2, 2):
                        move_probs(dve, i, n)
                    gla_lo(i)
                else:
                    gate_logs_in(i)
                    gate_logs(i)
                    output_gates(i)
                    linear_attention(i)
                    norms(i)
                    gla_lo(i)
                    keys(i)
                    move_scores(i, range(NB))
                    tops(i)
                    totals(i)
                swa_lo(i)

            loop(dve, body)

        @block.tensor
        def _(pe):
            pe.wait_ge(const_here, all_consts)
            pe.wait_ge(first_ready, 5 if prompt else 2)
            pe.sem_inc(c.held, 1)
            ident = c.ident

            def gate_logits(i):
                wait(pe, qk_here, i)
                pe.transpose(b7[0:GATE_RANK, 0:T], cur[0:T, GA0:GA0 + GATE_RANK], ident[0:T, 0:T]).then_inc(ga_turned, 1)
                wait(pe, ga_ready, i)
                pe.matmul(b7[0:T, :], ga_t[:, :], gate_w[:, :], start=True, stop=True).then_inc(gate_ready, 1)

            def linear_attention(i):
                wait(pe, log_a_ready, i)
                pe.matmul(b2[0:T, :], tri[:, :], log_a[:, :], start=True, stop=True)
                pe.matmul(b3[0:T, :], suf[:, :], log_a[:, :], start=True, stop=True)
                for h in range(GLA_HEADS):
                    last = pe.matmul(b0[:, h * NC:(h + 1) * NC], log_a[:, h * DK:(h + 1) * DK], ind[:, :], start=True, stop=True)
                last.then_inc(sums_ready, 1)
                for bank, x, n in ((4, qg, 1), (5, kg, 2)):
                    wait(pe, gated, i, n)
                    for h in range(GLA_HEADS):
                        last = pe.transpose(c.bank[:, bank, h * T:(h + 1) * T], x[:, h * DK:(h + 1) * DK], ident[0:T, 0:T])
                    last.then_inc(gated_turned, 1)
                wait(pe, qk_ready, i)
                for h in range(GLA_HEADS):
                    last = pe.matmul(c.bank[0:T, 6, h * T:(h + 1) * T], kg_t[:, h, :], qg_t[:, h, :], start=True, stop=True)
                last.then_inc(inner_ready, 1)
                wait(pe, gated, i)
                wait(pe, vr_here, i)
                if prompt:
                    for n, bank in ((0, 4), (1, 0)):
                        rows = slice(n * CL, (n + 1) * CL)
                        for h in range(GLA_HEADS):
                            last = pe.matmul(c.bank[:, bank + h // 2, (h % 2) * DV:(h % 2 + 1) * DV],
                                             ke[rows, h * DK:(h + 1) * DK], cur[rows, V0 + h * DV:V0 + (h + 1) * DV],
                                             start=True, stop=True)
                        last.then_inc(grown, 1)
                    wait(pe, state_ready, i, 1)
                wait(pe, inner_masked, i)
                if not prompt:
                    wait(pe, old_here, i)
                    pe.sem_inc(c.held, 1)
                for h in range(GLA_HEADS):
                    out = c.bank[0:T, 2 + h // 2, (h % 2) * DV:(h % 2 + 1) * DV]
                    pe.matmul(out, inner[:, h, :], cur[0:T, V0 + h * DV:V0 + (h + 1) * DV], start=True, stop=False)
                    for n in range(NC):
                        last = pe.matmul(out, q_spread[:, h, n * T:(n + 1) * T], state[:, n, h, :], start=False, stop=(n == NC - 1))
                last.then_inc(o_ready, 1)
                if not prompt:
                    for h in range(GLA_HEADS):
                        wait(pe, k_own_ready, i, h + 1)
                        for b in range(NC):
                            if h and b % (NC // 2) == 0:
                                wait(pe, state_ready, i, 2 * h - (1 if b == 0 else 0))
                            last = pe.matmul(c.bank[:, 4 + b // 2, (b % 2) * DV:(b % 2 + 1) * DV], k_own[:, h % 2, b, :],
                                             cur[0:T, V0 + h * DV:V0 + (h + 1) * DV], start=True, stop=True)
                            if b % (NC // 2) == NC // 2 - 1:
                                last.then_inc(grown, 1)
                    wait(pe, state_ready, i)

            def turn_linear(i):
                wait(pe, o_gated, i)
                for n in range(2):
                    for j in range(4):
                        k = 4 * n + j
                        last = pe.transpose(c.bank[:, O_BANK + n, j * T:(j + 1) * T], o_norm[:, k * P:(k + 1) * P], ident[0:T, 0:T])
                    last.then_inc(o_turned, 1)

            def scores_of_keys(i):
                wait(pe, rope_step, i)
                if not prompt:
                    wait(pe, state_ready, i)
                per_bank = 4 if prompt else PAIRS
                for k in range(PAIRS):
                    last = pe.transpose(c.bank[:, k // per_bank, k % per_bank * T:(k % per_bank + 1) * T],
                                        roped[0:T, 2 * k:2 * k + 2, :].rearrange("t h d -> t (h d)"), ident[0:T, 0:T])
                last.then_inc(q_turned, 1)
                if prompt:
                    wait(pe, k_twice_ready, i)
                    for g in range(KV):
                        last = pe.transpose(c.bank[:, 2, g * P:(g + 1) * P], k_twice[:, g, :, :].rearrange("t a d -> t (a d)"), ident[:, :])
                    last.then_inc(k_turned, 1)
                    wait(pe, q_t_ready, i)
                    wait(pe, k_t_ready, i)
                    for h in range(SWA_HEADS):
                        n, par, g = h // 2, h % 2, h // (SWA_HEADS // KV)
                        if h % SB == 0 and h >= 2 * SB:
                            wait(pe, score_moved, i, h - SB)
                        rows = slice(par * HD, (par + 1) * HD)
                        last = pe.matmul(score_bank(h), q_t[rows, h // 2, :], k_t[rows, g, :],
                                         start=True, stop=True)
                        if h % SB == SB - 1:
                            last.then_inc(scored, 1)
                else:
                    wait(pe, o_normed, i)
                    for b in range(NB):
                        wait(pe, k2_ready, i, b + 1)
                        if b >= 2:
                            wait(pe, k_t_ready, i, b - 1)
                        bank = c.bank[:, 1 + b % 2, :]
                        for g in range(KV):
                            pe.transpose(bank[:, g * P:(g + 1) * P], k2[:, b % 2, g, :, :].rearrange("t a d -> t (a d)"), ident[:, :])
                            at = KV * P + g * DEC_SEQ
                            last = pe.transpose(bank[:, at:at + DEC_SEQ], k2_old[:, b % 2, g, :, :].rearrange("t a d -> t (a d)"),
                                                ident[0:DEC_SEQ, 0:DEC_SEQ])
                        last.then_inc(k_turned, 1)
                    wait(pe, q_t_ready, i)
                    wait(pe, gla_heads_ready, i)
                    for b in range(NB):
                        n = b // 2
                        wait(pe, k_t_ready, i, b + 1)
                        for g in range(KV):
                            for par in range(2):
                                rows = slice(par * HD, (par + 1) * HD)
                                at = g * HD + par * 32
                                last = pe.matmul(c.bank[at:at + 32, 3 + n % 4, (b % 2) * 256:(b % 2) * 256 + KW],
                                                 q_t[rows, b, 32 * g:32 * g + 32],
                                                 k_t[rows, b, g, :], start=True, stop=True)
                        if b % 2:
                            last.then_inc(scored, 1)

            def turn_probs(i):
                for n in range(NB // 2):
                    wait(pe, weighted, i, 1 if n < NB // 4 else 2)
                    if n == 0:
                        wait(pe, score_moved, i)
                    if n >= 4:
                        wait(pe, p_ready[n % 2], i, (n - 4) // 2 + 1)
                    for a in range(2):
                        for half in range(2):
                            dst = c.bank[:, P_BANK + n % 4, (2 * a + half) * P:(2 * a + half + 1) * P]
                            if prompt:
                                last = pe.transpose(dst, scores[:, 2 * n + a, half * P:(half + 1) * P], ident[:, :])
                            elif half == 0:
                                last = pe.transpose(dst, scores[:, 2 * n + a, DEC_SEQ:KW], ident[:, :])
                            else:
                                last = pe.transpose(dst[0:DEC_SEQ, :], scores[:, 2 * n + a, 0:DEC_SEQ], ident[:, :])
                    last.then_inc(p_turned, 1)

            def mix(i):
                wait(pe, p_ready[0], i)
                wait(pe, p_ready[1], i)
                wait(pe, sv_here, i)
                pe.sem_inc(c.held, 1)
                if prompt:
                    wait(pe, state_ready, i)
                    for h in range(SWA_HEADS):
                        par, g = h % 2, h // (SWA_HEADS // KV)
                        out = c.bank[par * HD:(par + 1) * HD, h // 8, h // 2 % 4 * P:(h // 2 % 4 + 1) * P]
                        pe.matmul(out, v_before[:, g * HD:(g + 1) * HD], probs_t[:, h, 0, :], start=True, stop=False)
                        last = pe.matmul(out, cur[:, SV0 + g * HD:SV0 + (g + 1) * HD], probs_t[:, h, 1, :], start=False, stop=True)
                else:
                    for b in range(NB):
                        for g in range(KV):
                            for par in range(2):
                                at = g * HD + par * 32
                                out = c.bank[par * HD:(par + 1) * HD, 0, :].rearrange("p (k t) -> p k t", k=PAIRS)[
                                    :, 4 * g:4 * g + 4, b * DEC_SEQ:(b + 1) * DEC_SEQ]
                                pe.matmul(out, v_new[:, b, g * HD:(g + 1) * HD],
                                          probs_t[:, b, at:at + 32].rearrange("p (k t) -> p k t", k=4), start=True, stop=False)
                                last = pe.matmul(out, v_old[:, b, g * HD:(g + 1) * HD],
                                                 probs_old_t[:, b, at:at + 32].rearrange("p (k t) -> p k t", k=4),
                                                 start=False, stop=True)
                last.then_inc(mixed, 1)

            def body(i):
                gate_logits(i)
                if prompt:
                    scores_of_keys(i)
                    wait(pe, score_moved, i)
                    linear_attention(i)
                    turn_probs(i)
                    turn_linear(i)
                else:
                    linear_attention(i)
                    turn_linear(i)
                    scores_of_keys(i)
                    turn_probs(i)
                mix(i)

            loop(pe, body)


def expert_queries(nc, c, first):
    ctx, sb, sem = stage(nc)
    with ctx:
        raw = [first[0], sb("pq_raw", [P, KC, P])]
        w = [[first[1 + part], sb("pq" + tag, [P, KC, P], F32R)] for part, tag in ((HI, "_hi"), (LO, "_lo"))]
        raw_here = [sem(f"pq_raw_here{s}") for s in range(2)]
        rounded, split, summed, moved = sem("pq_rounded"), sem("pq_split"), sem("pq_summed"), sem("pq_moved")
        block = ctx.enter_context(nc.Block())

        @block.sync
        def _(sp):
            def load(h, s, more):
                if more:
                    sp.wait_ge(split, h + 1)
                    sp.sem_inc(c.held, 1)
                    sp.dma_start(raw[1 - s][:, :, :], c.d.w_peer_q[bass.ds(h + 1, 1)].rearrange("a p k n -> (a p) k n")).then_inc(raw_here[1 - s], 16)

            in_pairs(sp, PHEADS, load)

        @block.scalar
        def _(act):
            def hi(h, s, more):
                if more:
                    act.wait_ge(raw_here[1 - s], h * 8 + (16 - 8 * s))
                    act.wait_ge(summed, h * 2 + 4)
                    act.activation(w[HI][1 - s][:, :, :], raw[1 - s][:, :, :], ACT.Copy).then_inc(rounded, 1)

            in_pairs(act, PHEADS, hi)

        @block.gpsimd
        def _(pool):
            def lo(h, s, more):
                if more:
                    pool.wait_ge(rounded, h + 1)
                    pool.tensor_tensor(w[LO][1 - s][:, :, :], raw[1 - s][:, :, :], w[HI][1 - s][:, :, :].bitcast(F32),
                                       ALU.subtract).then_inc(split, 1)

            in_pairs(pool, PHEADS, lo)

        @block.vector
        def _(dve):
            def move(h, s, more):
                for n in range(2):
                    dve.wait_ge(summed, h * 2 + (4 + n + 1))
                    dve.sem_inc(c.held, 1)
                    dve.tensor_copy(c.query_t[:, bass.ds(h, 1), n * HALF:(n + 1) * HALF],
                                    c.bank[:, 2 * s + n, 0:HALF].unsqueeze(1)).then_inc(moved, 1)

            dve.sem_inc(moved, 4)
            dve.sem_inc(split, 2)
            in_pairs(dve, PHEADS, move)

        @block.tensor
        def _(pe):
            def products(h, s, more):
                pe.wait_ge(split, h + 2)
                for n in range(2):
                    pe.wait_ge(moved, h * 2 + (n + 1))
                    product(pe, c.bank[:, 2 * s + n, 0:HALF], lambda part, k: w[part][s][:, k, :],
                            lambda part, k: c.act[part][:, k, n * HALF:(n + 1) * HALF]).then_inc(summed, 1)

            pe.sem_inc(summed, 4)
            in_pairs(pe, PHEADS, products)


AHEAD_PER_TILE = 4
AHEAD = AHEAD_PER_TILE * TILES


def route(nc, c, slot0):
    ctx, sb, sem = stage(nc)
    HP = 2 * PHEADS
    with ctx:
        query = sb("rt_query", [P, PHEADS, P])
        keys = sb("rt_keys", [P, PHEADS, N_KEYS])
        score = sb("rt_score", [P, 2, HP, N_KEYS])
        top = sb("rt_top", [P, HP, TOPK])
        top_at = sb("rt_top_at", [P, HP, TOPK], U32)
        top_atf = sb("rt_top_atf", [P, 2, HP, TOPK])
        pair = sb("rt_pair", [P, PHEADS, TOPK * TOPK])
        best = sb("rt_best", [P, PHEADS, TOPK])
        best_at = sb("rt_best_at", [P, PHEADS, TOPK], U32)
        weight = sb("rt_weight", [P, 2, PHEADS, TOPK])
        rank = sb("rt_rank", [P, 2, SEL], U32)
        rankf = sb("rt_rankf", [P, 2, SEL])
        rank16 = sb("rt_rank16", [P, TOPK])
        hit = sb("rt_hit", [P, 2, PHEADS, TOPK, TOPK])
        picks = sb("rt_picks", [P, 3, SEL])
        total = sb("rt_total", [P, 2, PHEADS])
        raw = [slot0[0], sb("rt_raw", [P, KC, P])]
        u = [[slot0[1 + part], sb("rt_u" + tag, [P, KC, P], F32R)] for part, tag in ((HI, "_hi"), (LO, "_lo"))]
        hot = sb("rt_hot", [P, 2, TOKENS])
        const_here, query_ready, scored, score_ready = sem("rt_const"), sem("rt_query_ready"), sem("rt_scored"), sem("rt_score_ready")
        found, shifted, exped = sem("rt_found"), sem("rt_shifted"), sem("rt_exped")
        compared, looked_up, summed, gated, tallied = (
            sem("rt_" + x) for x in ("compared", "looked_up", "summed", "gated", "tallied"))
        turned, moved = sem("rt_turned"), sem("rt_moved")
        raw_here, hot_stored = [[sem(f"rt_{x}{s}") for s in range(2)] for x in ("raw_here", "hot_stored")]
        u_rounded, u_split, dotted, hot_ready, hot_free = (
            sem("rt_" + x) for x in ("u_rounded", "u_split", "dotted", "hot_ready", "hot_free"))
        block = ctx.enter_context(nc.Block())
        four = [P, PHEADS, TOPK, TOPK]

        @block.sync
        def _(sp):
            def load(r, s):
                sp.wait_ge(u_split, r + 1)
                sp.sem_inc(c.held, 1)
                sp.dma_start(raw[s][:, :, :], c.d.u_t[bass.ds(r, 1)].rearrange("a p k e -> (a p) k e")).then_inc(raw_here[s], 16)

            def turn(i, slot, more):
                for m in range(AHEAD_PER_TILE):
                    r = i * AHEAD_PER_TILE + m
                    if more or m < AHEAD_PER_TILE - 2:
                        load(r + 2, m % 2)
                        sp.wait_ge(hot_stored[m % 2], r * 8 + 8 * (2 - m % 2))
                        sp.sem_inc(hot_free, 1)

            sp.dma_start(keys[:, :, :], c.d.sub_keys).then_inc(const_here, 16)
            sp.dma_start(rank16[:, :], c.d.rank16).then_inc(const_here, 16)
            load(0, 0)
            load(1, 1)
            each_tile(sp, turn)
            for s in range(2):
                sp.wait_ge(hot_stored[s], 16 * (AHEAD // 2))

        @block.scalar
        def _(act):
            def queries(i):
                act.wait_ge(scored, i + 1)
                act.sem_inc(c.held, 1)
                act.activation(query[:, :, :], c.query_t[:, :, bass.ds(i * STRIDE, P)], ACT.Copy).then_inc(query_ready, 1)

            def scores(i, s):
                act.wait_ge(scored, i + 2)
                act.wait_ge(shifted, i + 1)
                act.sem_inc(c.held, 1)
                act.activation(score[:, s, :, :], c.bank[:, 0:4, :].rearrange("p b (s n) -> p (b s) n", n=N_KEYS), ACT.Copy).then_inc(score_ready, 1)

            def u_hi(r, s):
                act.wait_ge(raw_here[s], r * 8 + 8 * (2 - s))
                act.wait_ge(dotted, r * 2 + 2)
                act.activation(u[HI][s][:, :, :], raw[s][:, :, :], ACT.Copy).then_inc(u_rounded, 1)

            def gelu(r, s):
                act.wait_ge(hot_free, r + 1)
                for n in range(2):
                    act.wait_ge(dotted, r * 2 + (n + 5))
                    act.activation(hot[:, s, n * HALF:(n + 1) * HALF], c.bank[:, 5 + n, 0:HALF], ACT.Gelu).then_inc(hot_ready, 1)
                act.wait_ge(hot_ready, r * 2 + 4)
                act.sem_inc(c.held, 1)
                act.dma_start(c.d.hot[bass.ds(r, 1)].rearrange("a e t -> (a e) t"), hot[:, s, :]).then_inc(hot_stored[s], 16)

            def turn(i, slot, more):
                if more:
                    queries(i + 1)
                for m in range(AHEAD_PER_TILE):
                    r = i * AHEAD_PER_TILE + m
                    gelu(r, m % 2)
                    if m == 0 and more:
                        scores(i + 1, 1 - slot)
                    if more or m < AHEAD_PER_TILE - 2:
                        u_hi(r + 2, m % 2)
                    if m == 0:
                        act.wait_ge(shifted, i + 3)
                        act.activation(weight[:, slot, :, :], weight[:, slot, :, :], ACT.Exp).then_inc(exped, 1)

            act.sem_inc(score_ready, 1)
            queries(0)
            u_hi(0, 0)
            scores(0, 0)
            u_hi(1, 1)
            each_tile(act, turn)

        @block.gpsimd
        def _(pool):
            def look_up(i, s):
                for half in range(2):
                    pool.wait_ge(compared, i * 2 + (half + 1))
                    number = top_atf[:, s, half * PHEADS:(half + 1) * PHEADS, :]
                    pool.tensor_tensor(hit[:, half], hit[:, half], number.unsqueeze(2).broadcast_to(four), ALU.mult).then_inc(looked_up, 1)

            def u_lo(r, s):
                pool.wait_ge(u_rounded, r + 1)
                pool.tensor_tensor(u[LO][s][:, :, :], raw[s][:, :, :], u[HI][s][:, :, :].bitcast(F32), ALU.subtract).then_inc(u_split, 1)

            def turn(i, slot, more):
                for m in range(AHEAD_PER_TILE):
                    if more or m < AHEAD_PER_TILE - 2:
                        u_lo(i * AHEAD_PER_TILE + (m + 2), m % 2)
                    if m == 0:
                        look_up(i, slot)

            u_lo(0, 0)
            u_lo(1, 1)
            each_tile(pool, turn)

        @block.vector
        def _(dve):
            n_steps = [0]

            def steps(i, instructions):
                for make in instructions:
                    if n_steps[0]:
                        dve.wait_ge(found, i * STEPS + n_steps[0])
                        dve.sem_inc(c.held, 1)
                    make().then_inc(found, 1)
                    n_steps[0] += 1

            def top16(values, out, at, n):
                def each(make):
                    def run():
                        for r in range(n):
                            last = make(r)
                        return last
                    return run
                return [each(lambda r: dve.max(out[:, r, 0:8], values[:, r, :])),
                        each(lambda r: dve.max_index(at[:, r, 0:8], out[:, r, 0:8], values[:, r, :])),
                        each(lambda r: dve.match_replace(values[:, r, :], out[:, r, 0:8], values[:, r, :], NEG)),
                        each(lambda r: dve.max(out[:, r, 8:16], values[:, r, :])),
                        each(lambda r: dve.max_index(at[:, r, 8:16], out[:, r, 8:16], values[:, r, :]))]

            top4 = top[:, :, :].rearrange("p (s h) k -> p s h k", s=2)
            gate = picks[:, 2, :].rearrange("p (h k) -> p h k", h=PHEADS)

            def key_steps(s):
                return top16(score[:, s], top, top_at, HP) + [lambda: dve.tensor_copy(top_atf[:, s, :, :], top_at[:, :, :])]

            def sum_steps():
                flat = best_at[:, :, :].rearrange("p h k -> p (h k)")
                return ([lambda: dve.tensor_tensor(pair[:, :, :].rearrange("p h (a b) -> p h a b", b=TOPK),
                                                   top4[:, 0, :, :].unsqueeze(3).broadcast_to(four),
                                                   top4[:, 1, :, :].unsqueeze(2).broadcast_to(four), ALU.add)]
                        + top16(pair, best, best_at, PHEADS)
                        + [lambda: dve.tensor_scalar(rank[:, 0, :], flat, 4, None, ALU.logical_shift_right),
                           lambda: dve.tensor_scalar(rank[:, 1, :], flat, TOPK - 1, None, ALU.bitwise_and),
                           lambda: dve.tensor_copy(rankf[:, :, :], rank[:, :, :])])

            STEPS = len(key_steps(0)) + len(sum_steps())

            def pick_keys(i, s):
                n_steps[0] = 0
                dve.wait_ge(score_ready, i + 2)
                dve.wait_ge(gated, i + 1)
                dve.wait_ge(shifted, i + 2)
                dve.sem_inc(c.held, 1)
                steps(i, key_steps(s))

            def pick_sums(i, s):
                n_steps[0] = len(key_steps(0))
                steps(i, sum_steps())
                dve.wait_ge(found, i * STEPS + STEPS)
                dve.tensor_tensor(weight[:, s, :, :], best[:, :, :], best[:, :, 0:1].broadcast_to([P, PHEADS, TOPK]),
                                  ALU.subtract).then_inc(shifted, 1)
                for half in range(2):
                    dve.wait_ge(tallied, i * 2 + (half + 1))
                    mine = rankf[:, half, :].rearrange("p (h k) -> p h k", h=PHEADS).unsqueeze(3).broadcast_to(four)
                    dve.tensor_tensor(hit[:, half], mine, rank16[:, :].unsqueeze(1).unsqueeze(1).broadcast_to(four),
                                      ALU.is_equal).then_inc(compared, 1)

            def gather(i, s):
                dve.wait_ge(exped, i + 1)
                dve.tensor_reduce(total[:, 0, :], weight[:, s, :, :], AX_X, ALU.add).then_inc(summed, 1)
                dve.wait_ge(summed, i * 2 + 1)
                dve.reciprocal(total[:, 1, :], total[:, 0, :]).then_inc(summed, 1)
                dve.wait_ge(moved, i + 1)
                dve.wait_ge(summed, i * 2 + 2)
                dve.tensor_tensor(gate, weight[:, s, :, :], total[:, 1, :].unsqueeze(2).broadcast_to([P, PHEADS, TOPK]),
                                  ALU.mult).then_inc(gated, 1)
                for half in range(2):
                    dve.wait_ge(looked_up, i * 2 + (half + 1))
                    dve.tensor_reduce(picks[:, half, :].rearrange("p (h k) -> p h k", h=PHEADS), hit[:, half], AX_X, ALU.add).then_inc(tallied, 1)

            def keep(i):
                dve.wait_ge(turned, i + 1)
                dve.sem_inc(c.held, 1)
                dve.tensor_copy(c.picks_t[:, :, bass.ds(i * STRIDE, P)],
                                c.bank[:, 4, 0:3 * P].rearrange("p (a t) -> p a t", a=3)).then_inc(moved, 1)

            dve.sem_inc(moved, 1)
            dve.sem_inc(gated, 2)
            dve.sem_inc(shifted, 2)
            dve.sem_inc(tallied, 2)
            dve.sem_inc(u_split, 2)
            dve.sem_inc(hot_free, 2)
            dve.wait_ge(const_here, 32)

            def turn(i, s, more):
                if more:
                    pick_keys(i + 1, 1 - s)
                gather(i, s)
                if more:
                    pick_sums(i + 1, 1 - s)
                keep(i)

            pick_keys(0, 0)
            pick_sums(0, 0)
            each_tile(dve, turn)

        @block.tensor
        def _(pe):
            def scores(i):
                pe.wait_ge(query_ready, i + 1)
                pe.wait_ge(score_ready, i + 1)
                for h in range(PHEADS):
                    for half in range(2):
                        rows = slice(64 * half, 64 * half + 64)
                        n = PHEADS * half + h
                        last = pe.matmul(c.bank[:, n // 4, n % 4 * P:(n % 4 + 1) * P], query[rows, h, :], keys[rows, h, :],
                                         start=True, stop=True)
                last.then_inc(scored, 1)

            def turn_picks(i):
                pe.wait_ge(gated, i + 3)
                pe.wait_ge(tallied, i * 2 + 4)
                pe.wait_ge(moved, i + 1)
                for n in range(3):
                    last = pe.transpose(c.bank[:, 4, n * P:(n + 1) * P], picks[:, n, :], c.ident[:, :])
                last.then_inc(turned, 1)

            def dots(r, s):
                pe.wait_ge(u_split, r + 3)
                for n in range(2):
                    pe.wait_ge(hot_ready, r * 2 + (n + 1))
                    product(pe, c.bank[:, 5 + n, 0:HALF], lambda part, k: u[part][s][:, k, :],
                            lambda part, k: c.act[part][:, k, n * HALF:(n + 1) * HALF]).then_inc(dotted, 1)

            def turn(i, slot, more):
                for m in range(AHEAD_PER_TILE):
                    dots(i * AHEAD_PER_TILE + m, m % 2)
                    if m == 0 and more:
                        scores(i + 1)
                turn_picks(i)

            pe.wait_ge(const_here, 32)
            pe.sem_inc(scored, 1)
            pe.sem_inc(dotted, 4)
            pe.sem_inc(hot_ready, 2)
            scores(0)
            each_tile(pe, turn)


GROUP = 64
GROUPS = TOKENS // GROUP
STEP = 8
ROW_SLOTS = 4


def gate_arrays(nc, c):
    ctx, sb, sem = stage(nc)
    GROUP_STEPS = GROUP // STEP
    with ctx:
        number = sb("ga_number", [P, N_KEYS])
        second = c.query_t[:, :, :].rearrange("p h t -> p (h t)")[:, 0:ROW_SLOTS * STEP * N_KEYS].rearrange(
            "p (s t n) -> p s t n", s=ROW_SLOTS, t=STEP)
        first = sb("ga_first", [P, ROW_SLOTS, STEP, N_KEYS])
        out = sb("ga_out", [P, 2, N_KEYS, GROUP])
        number_here, summed, moved = sem("ga_number_here"), sem("ga_summed"), sem("ga_moved")
        first_there, second_ready, first_ready = sem("ga_first_there"), sem("ga_second_ready"), sem("ga_first_ready")
        stored, slot_free = [sem(f"ga_stored{s}") for s in range(2)], sem("ga_slot_free")
        block = ctx.enter_context(nc.Block())
        wide = [P, STEP, N_KEYS]

        def each_step(eng, step):
            with eng.Fori(0, TOKENS // (ROW_SLOTS * STEP)) as i:
                for s in range(ROW_SLOTS):
                    step(i * ROW_SLOTS + s, s)

        def of_tokens(which, n):
            return c.picks_t[:, which, bass.ds(n * STEP, STEP)].unsqueeze(2).broadcast_to(wide)

        @block.sync
        def _(sp):
            sp.dma_start(number[:, :], c.d.number).then_inc(number_here, 16)

            def store(g, s):
                sp.wait_ge(moved, g * GROUP_STEPS + (GROUP_STEPS + 2))
                sp.sem_inc(c.held, 1)
                sp.dma_start(c.d.gates[bass.ds(g, 1)].rearrange("a j i t -> (a j) i t"), out[:, s, :, :]).then_inc(stored[s], 16)
                sp.wait_ge(stored[s], g * 8 + 8 * (2 - s))
                sp.sem_inc(slot_free, 1)

            with sp.Fori(0, GROUPS // 2) as i:
                for s in range(2):
                    store(i * 2 + s, s)
            if GROUPS % 2:
                store(GROUPS - 1, 0)

        @block.vector
        def _(dve):
            def rows(n, s):
                dve.wait_ge(summed, n + 1)
                dve.sem_inc(c.held, 1)
                every = number[:, :].unsqueeze(1).broadcast_to(wide)
                dve.tensor_tensor(first[:, s], every, of_tokens(0, n), ALU.is_equal).then_inc(first_there, 1)
                dve.tensor_tensor(second[:, s], every, of_tokens(1, n), ALU.is_equal).then_inc(second_ready, 1)

            dve.wait_ge(number_here, 16)
            each_step(dve, rows)

        @block.gpsimd
        def _(pool):
            def gate(n, s):
                pool.wait_ge(first_there, n + 1)
                pool.sem_inc(c.held, 1)
                pool.tensor_tensor(first[:, s], first[:, s], of_tokens(2, n), ALU.mult).then_inc(first_ready, 1)

            each_step(pool, gate)

        @block.tensor
        def _(pe):
            def arrays(n, s):
                pe.wait_ge(second_ready, n + 1)
                pe.wait_ge(first_ready, n + 1)
                pe.wait_ge(moved, n + 1)
                for t in range(STEP):
                    last = pe.matmul(c.bank[:, s % 2 * 2 + t // 4, t % 4 * P:(t % 4 + 1) * P], second[:, s, t, :], first[:, s, t, :],
                                     start=True, stop=True)
                last.then_inc(summed, 1)

            pe.sem_inc(summed, ROW_SLOTS)
            each_step(pe, arrays)

        @block.scalar
        def _(act):
            act.sem_inc(moved, 2)
            act.sem_inc(slot_free, 2)

            def group(g, s):
                act.wait_ge(slot_free, g + 1)
                for q in range(GROUP_STEPS):
                    act.wait_ge(summed, g * GROUP_STEPS + (q + 1 + ROW_SLOTS))
                    b = 2 * (q % 2)
                    act.activation(out[:, s, :, q * STEP:(q + 1) * STEP],
                                   c.bank[:, b:b + 2, :].rearrange("p b (t i) -> p i (b t)", i=N_KEYS), ACT.Copy).then_inc(moved, 1)

            with act.Fori(0, GROUPS // 2) as i:
                for s in range(2):
                    group(i * 2 + s, s)
            if GROUPS % 2:
                group(GROUPS - 1, 0)


ROW_PAIR = 2
BLOCKS = (N_KEYS - AHEAD) // ROW_PAIR
OUTS = 2 * KC


def output(pe, c, m, v, coef):
    k, n = m % KC, m // KC
    for r in range(ROW_PAIR):
        for q, (a, z) in enumerate(PASSES):
            last = pe.matmul(c.bank[:, 4 + m % 4, 0:HALF], v(a, r)[:, k * P:(k + 1) * P], coef[z][:, r, n * HALF:(n + 1) * HALF],
                             start=(r == 0 and q == 0), stop=(r == ROW_PAIR - 1 and q == len(PASSES) - 1))
    return last


def add_output(dve, c, m):
    y = c.y_t[:, m % KC, m // KC * HALF:(m // KC + 1) * HALF]
    return dve.tensor_tensor(y, y, c.bank[:, 4 + m % 4, 0:HALF], ALU.add)


def outputs_ahead(nc, c):
    ctx, sb, sem = stage(nc)
    with ctx:
        raw = sb("oa_raw", [P, 2, D])
        v = [sb("oa_v" + part, [P, 2, 2, D], F32R) for part in ("_hi", "_lo")]
        gates = sb("oa_gates", [P, GROUPS, 2, GROUP])
        hot = sb("oa_hot", [P, 2, TOKENS])
        coef = [sb("oa_coef" + part, [P, 2, TOKENS], F32R) for part in ("_hi", "_lo")]
        raw_here = [sem(f"oa_raw_here{r}") for r in range(2)]
        g_here, hot_here = sem("oa_g_here"), sem("oa_hot_here")
        v_rounded, v_split, weighed, coef_rounded, coef_split = (
            sem("oa_" + x) for x in ("v_rounded", "v_split", "weighed", "coef_rounded", "coef_split"))
        mixed, added, cleared = sem("oa_mixed"), sem("oa_added"), sem("oa_cleared")
        block = ctx.enter_context(nc.Block())
        blocks = AHEAD // ROW_PAIR

        @block.sync
        def _(sp):
            def load_hot(b):
                sp.wait_ge(coef_split, b * 2 + 2)
                sp.sem_inc(c.held, 1)
                sp.dma_start(hot[:, :, :], c.d.hot[bass.ds(b * 2, 2)].rearrange("r e t -> e r t")).then_inc(hot_here, 16)
                sp.sem_inc(c.held, 1)
                sp.dma_start(gates[:, :, :, :].rearrange("j g i t -> j g (i t)"),
                             c.d.gates[:, :, bass.ds(b * 2, 2), :].rearrange("g j i t -> j g (i t)")).then_inc(g_here, 16)

            def load_v(b):
                for r in range(2):
                    sp.wait_ge(v_split, b * 2 + (r + 1))
                    sp.sem_inc(c.held, 1)
                    sp.dma_start(raw[:, r, :], c.d.v[bass.ds(b * (2 * P) + r * P, P), :]).then_inc(raw_here[r], 16)

            def turn(b, s, more):
                if more:
                    load_v(b + 1)
                    load_hot(b + 1)

            load_v(0)
            load_hot(0)
            in_pairs(sp, blocks, turn)

        @block.scalar
        def _(act):
            def v_hi(b, s):
                act.wait_ge(mixed, b * OUTS + 2)
                for r in range(2):
                    act.wait_ge(raw_here[r], b * 16 + 16)
                    act.activation(v[HI][:, s, r, :], raw[:, r, :], ACT.Copy).then_inc(v_rounded, 1)

            def coef_hi(b, n):
                act.wait_ge(mixed, b * OUTS + (n + 1) * KC + 2)
                act.wait_ge(weighed, b + 1)
                at = slice(n * HALF, (n + 1) * HALF)
                act.activation(coef[HI][:, :, at], hot[:, :, at], ACT.Copy).then_inc(coef_rounded, 1)

            def turn(b, s, more):
                coef_hi(b, 1)
                if more:
                    v_hi(b + 1, 1 - s)
                    coef_hi(b + 1, 0)

            v_hi(0, 0)
            coef_hi(0, 0)
            in_pairs(act, blocks, turn)

        @block.gpsimd
        def _(pool):
            def v_lo(b, s, more):
                for r in range(2):
                    pool.wait_ge(v_rounded, b * 2 + (r + 1))
                    pool.tensor_tensor(v[LO][:, s, r, :], raw[:, r, :], v[HI][:, s, r, :].bitcast(F32), ALU.subtract).then_inc(v_split, 1)

            in_pairs(pool, blocks, v_lo)

        @block.vector
        def _(dve):
            def weigh(b):
                dve.wait_ge(hot_here, b * 16 + 16)
                dve.wait_ge(g_here, b * 16 + 16)
                for r in range(2):
                    x = hot[:, r, :].rearrange("p (g t) -> p g t", t=GROUP)
                    last = dve.tensor_tensor(x, x, gates[:, :, r, :], ALU.mult)
                last.then_inc(weighed, 1)

            def coef_lo(b, n):
                dve.wait_ge(coef_rounded, b * 2 + (n + 1))
                at = slice(n * HALF, (n + 1) * HALF)
                dve.tensor_tensor(coef[LO][:, :, at], hot[:, :, at], coef[HI][:, :, at].bitcast(F32), ALU.subtract).then_inc(coef_split, 1)

            def turn(b, s, more):
                coef_lo(b, 1)
                for m in range(OUTS):
                    if m == KC - 2 and more:
                        weigh(b + 1)
                    if m == KC + 4 and more:
                        coef_lo(b + 1, 0)
                    dve.wait_ge(mixed, b * OUTS + (OUTS + 2 + m + 1))
                    add_output(dve, c, m).then_inc(added, 1)

            dve.sem_inc(mixed, OUTS + 2)
            dve.sem_inc(added, 4)
            dve.sem_inc(coef_split, 2)
            dve.sem_inc(v_split, 2)
            dve.memset(c.y_t[:, :, :], 0.0).then_inc(cleared, 1)
            dve.wait_ge(cleared, 1)
            weigh(0)
            coef_lo(0, 0)
            in_pairs(dve, blocks, turn)

        @block.tensor
        def _(pe):
            def turn(b, s, more):
                pe.wait_ge(v_split, b * 2 + 4)
                for m in range(OUTS):
                    if m % KC == 0:
                        pe.wait_ge(coef_split, b * 2 + (m // KC + 3))
                    pe.wait_ge(added, b * OUTS + (m + 1))
                    output(pe, c, m, lambda part, r: v[part][:, s, r, :], coef).then_inc(mixed, 1)

            in_pairs(pe, blocks, turn)


def experts(nc, c):
    ctx, sb, sem = stage(nc)
    with ctx:
        raw = sb("raw", [P, 2, D])
        u = [sb("u" + part, [P, 2, KC, P], F32R) for part in ("_hi", "_lo")]
        v = [sb("v" + part, [P, 2, D], F32R) for part in ("_hi", "_lo")]
        gates = sb("gates", [P, GROUPS, 2, GROUP])
        hot = sb("hot", [P, 2, TOKENS])
        coef = [sb("coef" + part, [P, 2, TOKENS], F32R) for part in ("_hi", "_lo")]
        raw_here = [sem(f"raw_here{s}") for s in range(2)]
        g_here = sem("g_here")
        u_rounded, u_split, v_rounded, v_split = sem("u_rounded"), sem("u_split"), sem("v_rounded"), sem("v_split")
        dotted, hot_ready, weighed = sem("dotted"), sem("hot_ready"), sem("weighed")
        coef_rounded, coef_split = sem("coef_rounded"), sem("coef_split")
        mixed, added = sem("mixed"), sem("added")
        block = ctx.enter_context(nc.Block())


        def turns(eng, turn):
            with eng.Fori(0, BLOCKS - 2) as b:
                turn(b, True, True)
            turn(BLOCKS - 2, True, False)
            turn(BLOCKS - 1, False, False)

        @block.sync
        def _(sp):
            def load_u(i, s):
                src = c.d.u_t[bass.ds(i + AHEAD, 1)].rearrange("a p k e -> (a p) (k e)")
                sp.dma_start(raw[:, s, :], src).then_inc(raw_here[s], 16)

            load_u(0, 1)
            load_u(1, 0)
            sp.dma_start(gates[:, :, 1, :], c.d.gates[:, :, AHEAD, :].rearrange("g j t -> j g t")).then_inc(g_here, 16)
            sp.wait_ge(u_split, 1)
            load_u(2, 1)

            def turn(b, more1, more0):
                sp.wait_ge(weighed, b * 2 + 1)
                sp.sem_inc(c.held, 1)
                if more1:
                    sp.dma_start(gates[:, :, :, :].rearrange("j g i t -> j g (i t)"),
                                 c.d.gates[:, :, bass.ds(b * 2 + (AHEAD + 1), 2), :].rearrange("g j i t -> j g (i t)")).then_inc(g_here, 16)
                else:
                    sp.dma_start(gates[:, :, 0, :], c.d.gates[:, :, N_KEYS - 1, :].rearrange("g j t -> j g t")).then_inc(g_here, 16)
                for r in range(2):
                    if r == 0 or more1:
                        sp.wait_ge(u_split, b * 2 + (2 + r))
                    else:
                        sp.wait_ge(v_split, b * 2)
                    sp.sem_inc(c.held, 1)
                    sp.dma_start(raw[:, r, :], c.d.v[bass.ds(b * (2 * P) + (AHEAD + r) * P, P), :]).then_inc(raw_here[r], 16)
                for r, more in ((0, more1), (1, more0)):
                    if more:
                        sp.wait_ge(v_split, b * 2 + (1 + r))
                        sp.sem_inc(c.held, 1)
                        load_u(b * 2 + (3 + r), r)

            turns(sp, turn)

        @block.scalar
        def _(act):
            def u_hi(slot, row, uses, dots):
                act.wait_ge(raw_here[slot], uses)
                act.wait_ge(dotted, dots)
                act.activation(u[HI][:, row].rearrange("p k e -> p (k e)"), raw[:, slot, :], ACT.Copy).then_inc(u_rounded, 1)

            def gelu(row, first):
                for n in range(2):
                    act.wait_ge(dotted, first + n + 4)
                    act.activation(hot[:, row, n * HALF:(n + 1) * HALF], c.bank[:, 2 * row + n, 0:HALF], ACT.Gelu).then_inc(hot_ready, 1)

            def coef_hi(row, number):
                act.wait_ge(weighed, number)
                act.activation(coef[HI][:, row, :], hot[:, row, :], ACT.Copy).then_inc(coef_rounded, 1)

            u_hi(1, 0, 16, 1)
            u_hi(0, 1, 16, 1)
            gelu(0, 1)
            u_hi(1, 0, 32, 6)

            def turn(b, more1, more0):
                act.wait_ge(mixed, b * OUTS + 1)
                coef_hi(0, b * 2 + 1)
                for r in range(2):
                    act.wait_ge(raw_here[r], b * 32 + 16 * (2 + r - (r == 1 and not more1)))
                    act.activation(v[HI][:, r, :], raw[:, r, :], ACT.Copy).then_inc(v_rounded, 1)
                act.wait_ge(coef_split, b * 2 + 1)
                gelu(1, b * 4 + 3)
                if more1:
                    u_hi(0, 1, b * 32 + 48, b * 4 + 8)
                coef_hi(1, b * 2 + 2)
                if more1:
                    gelu(0, b * 4 + 5)
                if more0:
                    u_hi(1, 0, b * 32 + 64, b * 4 + 10)

            turns(act, turn)

        @block.gpsimd
        def _(pool):
            def u_lo(slot, row, number):
                pool.wait_ge(u_rounded, number)
                pool.tensor_tensor(u[LO][:, row].rearrange("p k e -> p (k e)"), raw[:, slot, :],
                                   u[HI][:, row].rearrange("p k e -> p (k e)").bitcast(F32), ALU.subtract).then_inc(u_split, 1)

            u_lo(1, 0, 1)
            u_lo(0, 1, 2)
            u_lo(1, 0, 3)

            def turn(b, more1, more0):
                if more1:
                    u_lo(0, 1, b * 2 + 4)
                if more0:
                    u_lo(1, 0, b * 2 + 5)

            turns(pool, turn)

        @block.vector
        def _(dve):
            def weigh(row, at, gelus, loads):
                dve.wait_ge(hot_ready, gelus)
                dve.wait_ge(g_here, loads)
                x = hot[:, row, :].rearrange("p (g t) -> p g t", t=GROUP)
                dve.tensor_tensor(x, x, gates[:, :, at, :], ALU.mult).then_inc(weighed, 1)

            def coef_lo(row, number):
                dve.wait_ge(coef_rounded, number)
                dve.tensor_tensor(coef[LO][:, row, :], hot[:, row, :], coef[HI][:, row, :].bitcast(F32), ALU.subtract).then_inc(coef_split, 1)

            dve.sem_inc(added, 4)
            weigh(0, 1, 6, 16)

            def turn(b, more1, more0):
                coef_lo(0, b * 2 + 1)
                for r in range(2):
                    dve.wait_ge(v_rounded, b * 2 + (r + 1))
                    dve.tensor_tensor(v[LO][:, r, :], raw[:, r, :], v[HI][:, r, :].bitcast(F32), ALU.subtract).then_inc(v_split, 1)
                weigh(1, 0, b * 4 + 8, b * 16 + 32)
                coef_lo(1, b * 2 + 2)
                if more1:
                    weigh(0, 1, b * 4 + 10, b * 16 + 32)
                for m in range(OUTS):
                    dve.wait_ge(mixed, b * OUTS + (m + 2))
                    add_output(dve, c, m).then_inc(added, 1)

            turns(dve, turn)

        @block.tensor
        def _(pe):
            pe.sem_inc(dotted, 4)
            pe.sem_inc(mixed, 1)
            pe.sem_inc(hot_ready, 4)

            def dots(row, number, gelus):
                pe.wait_ge(u_split, number)
                for n in range(2):
                    pe.wait_ge(hot_ready, gelus + n)
                    product(pe, c.bank[:, 2 * row + n, 0:HALF], lambda part, k: u[part][:, row, k, :],
                            lambda part, k: c.act[part][:, k, n * HALF:(n + 1) * HALF]).then_inc(dotted, 1)

            dots(0, 1, 1)

            def turn(b, more1, more0):
                dots(1, b * 2 + 2, b * 4 + 3)
                if more1:
                    dots(0, b * 2 + 3, b * 4 + 5)
                pe.wait_ge(v_split, b * 2 + 2)
                pe.wait_ge(coef_split, b * 2 + 2)
                for m in range(OUTS):
                    pe.wait_ge(added, b * OUTS + (m + 1))
                    output(pe, c, m, lambda part, r: v[part][:, r, :], coef).then_inc(mixed, 1)

            turns(pe, turn)


def finish(nc, c):
    ctx, sb, sem = stage(nc)
    with ctx:
        h = sb("fi_h", [P, 2, KC, P])
        square = sb("fi_square", [P, D])
        out = sb("fi_out", [P, 2, D])
        gain = sb("fi_gain", [P, D])
        stat = sb("fi_stat", [P, 2, 4])
        gain_here, added, turned = (sem("fi_" + s) for s in ("gain_here", "added", "turned"))
        summed, meaned, rooted, inverted, scaled = (sem("fi_" + s) for s in ("summed", "meaned", "rooted", "inverted", "scaled"))
        h_here, stored = [[sem(f"fi_{x}{s}") for s in range(2)] for x in ("h_here", "stored")]
        out_free = sem("fi_out_free")
        block = ctx.enter_context(nc.Block())

        def sums(s):
            return c.bank[:, 4 * s:4 * s + 4, :]

        @block.sync
        def _(sp):
            def load(i, s, more):
                sp.wait_ge(turned, i + 1)
                sp.sem_inc(c.held, 1)
                sp.dma_start(h[:, s], c.d.h_t[:, :, bass.ds(i * STRIDE, P)]).then_inc(h_here[s], 16)

            each_tile(sp, load)

        @block.gpsimd
        def _(pool):
            def store(i, s, more):
                pool.wait_ge(scaled, i + 3)
                pool.sem_inc(c.held, 1)
                pool.dma_start(c.d.y[bass.ds(i * STRIDE, P), :], out[:, s, :]).then_inc(stored[s], 16)
                pool.wait_ge(stored[s], i * 8 + 8 * (2 - s))
                pool.sem_inc(out_free, 1)

            each_tile(pool, store)

        @block.scalar
        def _(act):
            def turn(i, s, more):
                act.wait_ge(turned, i + 3)
                act.activation(square[:, :].rearrange("p (b n) -> p b n", b=4), sums(s), ACT.Square,
                               accum_out=stat[:, s, 0:1]).then_inc(summed, 1)
                act.wait_ge(meaned, i + 1)
                act.activation(stat[:, s, 2:3], stat[:, s, 1:2], ACT.Sqrt).then_inc(rooted, 1)

            act.dma_start(gain[:, :], c.d.g_final).then_inc(gain_here, 16)
            each_tile(act, turn)

        @block.vector
        def _(dve):
            def add(i, s):
                dve.wait_ge(h_here[s], i * 8 + 8 * (2 - s))
                dve.sem_inc(c.held, 1)
                dve.tensor_tensor(h[:, s], h[:, s], c.y_t[:, :, bass.ds(i * STRIDE, P)], ALU.add).then_inc(added, 1)

            def turn(i, s, more):
                if more:
                    add(i + 1, 1 - s)
                dve.wait_ge(summed, i + 1)
                dve.tensor_scalar(stat[:, s, 1:2], stat[:, s, 0:1], 1.0 / D, EPS, ALU.mult, ALU.add).then_inc(meaned, 1)
                dve.wait_ge(rooted, i + 1)
                dve.reciprocal(stat[:, s, 3:4], stat[:, s, 2:3]).then_inc(inverted, 1)
                dve.wait_ge(inverted, i + 1)
                dve.wait_ge(out_free, i + 1)
                dve.scalar_tensor_tensor(out=out[:, s, :].rearrange("p (b n) -> p b n", b=4), in0=sums(s), scalar=stat[:, s, 3:4],
                                         in1=gain[:, :].rearrange("p (b n) -> p b n", b=4),
                                         op0=ALU.mult, op1=ALU.mult).then_inc(scaled, 1)

            dve.sem_inc(scaled, 2)
            dve.sem_inc(turned, 2)
            dve.sem_inc(out_free, 2)
            add(0, 0)
            dve.wait_ge(gain_here, 16)
            dve.sem_inc(c.held, 1)
            each_tile(dve, turn)

        @block.tensor
        def _(pe):
            def turn(i, s, more):
                pe.wait_ge(added, i + 1)
                pe.wait_ge(scaled, i + 1)
                for n in range(KC):
                    last = pe.transpose(c.bank[:, 4 * s + n // 4, n % 4 * P:(n % 4 + 1) * P], h[:, s, n, :], c.ident[:, :])
                last.then_inc(turned, 1)

            each_tile(pe, turn)


def build(nc, d):
    c = Chip()
    c.d = d
    with ExitStack() as ctx:
        c.bank = ctx.enter_context(nc.psum_tensor("bank", [P, 8, 512], F32))
        c.act = [ctx.enter_context(nc.sbuf_tensor(name, [P, KC, TOKENS], F32R)) for name in ("act_hi", "act_lo")]
        c.ident = ctx.enter_context(nc.sbuf_tensor("ident", [P, P], F32))
        c.g_attn = ctx.enter_context(nc.sbuf_tensor("g_attn", [P, KC], F32))
        c.g_ffn = ctx.enter_context(nc.sbuf_tensor("g_ffn", [P, KC], F32))
        c.held = ctx.enter_context(nc.semaphore("held"))
        with ExitStack() as projection:
            first = [projection.enter_context(nc.sbuf_tensor("slice_" + name, [P, KC, PROJ // W_IN_SLICES], dt))
                     for name, dt in (("raw", F32), ("hi", F32R), ("lo", F32R))]
            norm_transpose(nc, c, "norm1", d.x, c.g_attn, d.w_in, first)
            project(nc, c, "proj", d.w_in, first, d.proj)
        attend(nc, c, "prompt")
        attend(nc, c, "sample")
        with ExitStack() as routing:
            first = [routing.enter_context(nc.sbuf_tensor("first_" + name, [P, KC, P], dt))
                     for name, dt in (("raw", F32), ("hi", F32R), ("lo", F32R))]
            merge_heads(nc, c, d.w_peer_q, first)
            c.query_t = routing.enter_context(nc.sbuf_tensor("query_t", [P, PHEADS, TOKENS], F32))
            expert_queries(nc, c, first)
            c.picks_t = routing.enter_context(nc.sbuf_tensor("picks_t", [P, 3, TOKENS], F32))
            route(nc, c, first)
            gate_arrays(nc, c)
        c.y_t = ctx.enter_context(nc.sbuf_tensor("y_t", [P, KC, TOKENS], F32))
        outputs_ahead(nc, c)
        experts(nc, c)
        finish(nc, c)



def _chunk_arrays(T, CL):
    import numpy as np
    s, t = np.arange(T)[:, None], np.arange(T)[None, :]
    same = s // CL == t // CL
    one = lambda m: np.ascontiguousarray(m.astype(np.float32))
    inside = one(same & (s <= t))
    own = one(s // CL == np.arange(T // CL)[None, :])
    return inside / np.float32(TAU), one(same & (s > t)) / np.float32(TAU), own / np.float32(TAU), inside, own


def _trig():
    import math
    import numpy as np
    half = HD // 2
    inv = np.exp(np.float32(-math.log(10000.0)) * np.arange(half, dtype=np.float32) * np.float32(2.0 / HD)).astype(np.float32)
    pos = np.concatenate([np.arange(SEQ), 1024 + np.arange(SAMPLES) % DEC_SEQ]).astype(np.float32)
    ang = (pos[:, None] * inv[None, :]).astype(np.float32)
    return np.concatenate([np.cos(ang), np.sin(ang)], axis=1)


def _masks():
    import numpy as np
    masked = np.float32(-1e30)
    q, s = np.arange(P)[:, None], np.arange(2 * WINDOW)[None, :]
    later = np.where((s > q) & (s <= q + WINDOW), np.float32(0), masked)
    first = np.where(s >= WINDOW, later, masked)
    t, j = np.arange(P)[:, None] % DEC_SEQ, np.arange(DEC_SEQ + WINDOW)[None, :]
    sample = np.where((j > t) & (j <= t + WINDOW), np.float32(0), masked)
    return first.astype(np.float32), later.astype(np.float32), sample.astype(np.float32)


def kernel(**inputs):
    import types
    import numpy as np
    import concourse.bacc as bacc
    from concourse.bass_utils import run_bass_kernel_spmd

    a = {k: np.asarray(x) for k, x in inputs.items()}
    put = np.ascontiguousarray
    x = np.concatenate([a["x_prompt"].reshape(SEQ, D), a["x_sample"].reshape(SAMPLES, D)])
    w = a["w_in"][0]
    ga = 2 * GLA_HEADS * DK + 2 * GLA_HEADS * DV
    w = np.concatenate([w[:, ga:ga + GATE_RANK], w[:, :ga], w[:, ga + GATE_RANK:]], axis=1)

    def slices(m, n):
        return put(m.reshape(KC, P, m.shape[1] // n, n).transpose(2, 1, 0, 3))

    def rows(v):
        return put(np.broadcast_to(v.reshape(1, -1), (P, v.size)))

    tri_p, suf_p, ind_p, inside_p, _ = _chunk_arrays(P, GLA_CHUNK)
    tri_s, suf_s, ind_s, inside_s, own = _chunk_arrays(SAMPLES, DEC_SEQ)
    first, later, sample = _masks()
    sinks = a["attn_sinks"][0]
    by_row = sinks.reshape(KV, PAIRS // KV, 2).transpose(0, 2, 1).reshape(-1)
    arrays = {
        "x": x, "x_t": x.T.reshape(KC, P, TOKENS).transpose(1, 0, 2),
        "w_in": slices(w, PROJ // W_IN_SLICES),
        "w_out": slices(a["w_out"][0], P),
        "w_peer_q": slices(a["w_peer_q"][0], P),
        "g_attn": put(a["g_attn"][0].reshape(KC, P).T), "g_ffn": put(a["g_ffn"][0].reshape(KC, P).T),
        "g_out": rows(a["g_gla_out"][0]), "g_final": rows(a["g_final"]),
        "gate_w": np.concatenate([a["w_gate_up"][0], a["b_gate"]], axis=0),
        "sinks_prompt": rows(sinks), "sinks_sample": put(np.repeat(by_row, DEC_SEQ).reshape(P, 1)),
        "cache_k": a["cache_win_k"][0].reshape(DEC_BATCH, WINDOW, KV * HD),
        "cache_v": a["cache_win_v"][0].reshape(DEC_BATCH, WINDOW, KV * HD),
        "state_in": a["state_gla"][0],
        "sub_keys": put(a["peer_sub_keys"][0].transpose(1, 3, 0, 2).reshape(P, PHEADS, N_KEYS)),
        "u_t": put(a["peer_u"][0].reshape(N_KEYS, P, KC, P).transpose(0, 3, 2, 1)),
        "v": a["peer_v"][0],
        "ident": np.eye(P, dtype=np.float32), "trig": _trig(),
        "tri_prompt": tri_p, "suf_prompt": suf_p, "ind_prompt": ind_p, "inside_prompt": inside_p,
        "tri_sample": tri_s, "suf_sample": suf_s, "ind_sample": ind_s, "inside_sample": inside_s, "own": own,
        "mask_prompt": first, "mask_later": later, "mask_sample": sample,
        "rank16": rows(np.arange(TOPK, dtype=np.float32)), "number": rows(np.arange(N_KEYS, dtype=np.float32)),
    }
    arrays = {k: put(v) for k, v in arrays.items()}
    outs = {
        "y": (TOKENS, D),
        "state_out_prompt": (GLA_HEADS, DK, DV), "k_out_prompt": (WINDOW, KV * HD), "v_out_prompt": (WINDOW, KV * HD),
        "state_out_sample": (DEC_BATCH, GLA_HEADS, DK, DV),
        "k_out_sample": (DEC_BATCH, WINDOW, KV * HD), "v_out_sample": (DEC_BATCH, WINDOW, KV * HD),
    }
    scratch = {"proj": (TOKENS, PROJ), "h_t": (P, KC, TOKENS), "gates": (GROUPS, N_KEYS, N_KEYS, GROUP), "hot": (AHEAD, P, TOKENS)}

    nc = bacc.Bacc("TRN2", target_bir_lowering=False, num_devices=1)
    d = types.SimpleNamespace()
    for k, v in arrays.items():
        vars(d)[k] = nc.dram_tensor("in_" + k, v.shape, mybir.dt.from_np(v.dtype), kind="ExternalInput").ap()
    for k, shape in outs.items():
        vars(d)[k] = nc.dram_tensor("out_" + k, shape, F32, kind="ExternalOutput").ap()
    for k, shape in scratch.items():
        vars(d)[k] = nc.dram_tensor(k + "_scratch", shape, F32, kind="Internal").ap()
    d.tri = {"prompt": d.tri_prompt, "sample": d.tri_sample}
    d.suf = {"prompt": d.suf_prompt, "sample": d.suf_sample}
    d.ind = {"prompt": d.ind_prompt, "sample": d.ind_sample}
    d.inside = {"prompt": d.inside_prompt, "sample": d.inside_sample}
    d.sinks = {"prompt": d.sinks_prompt, "sample": d.sinks_sample}
    d.mask = {"prompt": d.mask_prompt, "later": d.mask_later, "sample": d.mask_sample}
    build(nc, d)
    r = run_bass_kernel_spmd(nc, [{"in_" + k: v for k, v in arrays.items()}], core_ids=[0]).results[0]
    y = r["out_y"]
    return (y[:SEQ].reshape(1, SEQ, D), y[SEQ:TOKENS].reshape(DEC_BATCH, DEC_SEQ, D),
            r["out_state_out_prompt"].reshape(1, 1, GLA_HEADS, DK, DV),
            r["out_k_out_prompt"].reshape(1, 1, WINDOW, KV, HD), r["out_v_out_prompt"].reshape(1, 1, WINDOW, KV, HD),
            r["out_state_out_sample"].reshape(1, DEC_BATCH, GLA_HEADS, DK, DV),
            r["out_k_out_sample"].reshape(1, DEC_BATCH, WINDOW, KV, HD),
            r["out_v_out_sample"].reshape(1, DEC_BATCH, WINDOW, KV, HD))
```
